# Optimizing a Trainium2 kernel written in Bass

```python
import math
import jax
import jax.numpy as jnp
from jax import lax
import numpy as np

D_MODEL = 1024
BATCH = 1
SEQ = 256
DEPTH = 2
DEC_BATCH = 8
DEC_SEQ = 4
PAST_LEN = 2048
PAGE_SIZE = 128

RET_HEADS = 4
RET_DK = 64
RET_DV = 128
ML_HEADS = 4
ML_DH = 128
CONV_W = 4
RW_HEADS = 8
RW_DH = 64
RW_LORA_W = 64
RW_LORA_A = 64
RW_LORA_G = 128
RET_W = RET_HEADS * RET_DV
ML_W = ML_HEADS * ML_DH
RW_W = RW_HEADS * RW_DH
BRANCH_W = RET_W
N_BRANCH = 3
RW_COLS = 3 * RW_W + RW_LORA_W + RW_LORA_A + RW_LORA_G
IN_SPLITS = (RET_HEADS * RET_DK, RET_HEADS * RET_DK, RET_W, RET_W,
             ML_W, ML_W, ML_HEADS, ML_HEADS, ML_W,
             RW_COLS, N_BRANCH * D_MODEL)
RW_SPLITS = (RW_W, RW_W, RW_W, RW_LORA_W, RW_LORA_A, RW_LORA_G)
N_IN = sum(IN_SPLITS)
D_FF = 2816
N_EXPERTS = 8
TOP_K = 2
D_FF_EXPERT = 1408
N_DENSE = (DEPTH + 1) // 2
N_MOE = DEPTH // 2
CHUNK = 128
NORM_EPS = 1e-6
GN_EPS = 1e-5
RW_GN_EPS = 64e-5
ROPE_BASE = 10000.0
RW_DECAY_SCALE = 0.606531

kernel_name = 'hybrid_retention_mlstm_rwkv7_moe_step'

def _split(z, sizes):
    out, off = [], 0
    for s in sizes:
        out.append(z[..., off:off + s])
        off += s
    return out

def _rmsnorm(x, g):
    xf = x.astype(jnp.float32)
    y = xf * lax.rsqrt(jnp.mean(xf * xf, axis=-1, keepdims=True) + NORM_EPS)
    return (y * g.astype(jnp.float32)).astype(x.dtype)

def _head_norm(x, gain, bias, eps):
    xf = x.astype(jnp.float32)
    xc = xf - jnp.mean(xf, axis=-1, keepdims=True)
    y = xc * lax.rsqrt(jnp.mean(xc * xc, axis=-1, keepdims=True) + eps)
    y = y.reshape(x.shape[:-2] + (-1,)) * gain.astype(jnp.float32)
    if bias is not None:
        y = y + bias.astype(jnp.float32)
    return y

def _rotary(x, pos):
    half = x.shape[-1] // 2
    inv = ROPE_BASE ** (-jnp.arange(half, dtype=jnp.float32) / half)
    ang = pos.astype(jnp.float32)[:, None] * inv[None, :]
    cos = jnp.cos(ang)[None, :, None, :]
    sin = jnp.sin(ang)[None, :, None, :]
    xf = x.astype(jnp.float32)
    x1, x2 = xf[..., :half], xf[..., half:]
    return jnp.concatenate([x1 * cos - x2 * sin, x1 * sin + x2 * cos], axis=-1)

def _to_chunks(x, L):
    B, T = x.shape[0], x.shape[1]
    return jnp.moveaxis(x.reshape((B, T // L, L) + x.shape[2:]), 1, 0)

def _from_chunks(x):
    x = jnp.moveaxis(x, 0, 1)
    return x.reshape((x.shape[0], -1) + x.shape[3:])

def _retention(q, k, v, S0):
    L = math.gcd(q.shape[1], CHUNK)
    log_gamma = jnp.log1p(-(2.0 ** (-5.0 - jnp.arange(RET_HEADS, dtype=jnp.float32))))
    idx = jnp.arange(L, dtype=jnp.float32)
    diff = idx[:, None] - idx[None, :]
    causal = diff >= 0
    decay_intra = jnp.where(causal[None], jnp.exp(jnp.where(causal, diff, 0.0)[None] * log_gamma[:, None, None]), 0.0)
    decay_q = jnp.exp((idx[:, None] + 1.0) * log_gamma[None, :])
    decay_k = jnp.exp((L - 1.0 - idx)[:, None] * log_gamma[None, :])
    decay_chunk = jnp.exp(L * log_gamma)

    def step(S, blk):
        qc, kc, vc = blk
        s = jnp.einsum('blhd,bshd->bhls', qc, kc) * decay_intra[None]
        inner = jnp.einsum('bhls,bshv->blhv', s, vc)
        cross = jnp.einsum('blhd,bhdv->blhv', qc, S) * decay_q[None, :, :, None]
        S_new = S * decay_chunk[None, :, None, None] + jnp.einsum('blhd,blhv->bhdv', kc * decay_k[None, :, :, None], vc)
        return S_new, inner + cross

    S, o = lax.scan(step, S0.astype(jnp.float32),
                    (_to_chunks(q, L), _to_chunks(k, L), _to_chunks(v.astype(jnp.float32), L)))
    return _from_chunks(o), S

def _mlstm(q, k, v, ig, lf, C0, n0, m0):
    L = math.gcd(q.shape[1], CHUNK)
    tri = jnp.tril(jnp.ones((L, L), dtype=bool))

    def step(carry, blk):
        C, n, m = carry
        qc, kc, vc, ic, fc = blk
        F = jnp.cumsum(fc, axis=1)
        Dlog = F[:, :, None, :] - F[:, None, :, :] + ic[:, None, :, :]
        Dlog = jnp.where(tri[None, :, :, None], Dlog, -jnp.inf)
        inter = F + m[:, None, :]
        m_t = jnp.maximum(jnp.max(Dlog, axis=2), inter)
        W = jnp.exp(Dlog - m_t[:, :, None, :])
        s = jnp.einsum('blhd,bshd->blsh', qc, kc) * W
        a_inter = jnp.exp(inter - m_t)
        num = jnp.einsum('blsh,bshv->blhv', s, vc) + a_inter[..., None] * jnp.einsum('blhd,bhdv->blhv', qc, C)
        den = jnp.sum(s, axis=2) + a_inter * jnp.einsum('blhd,bhd->blh', qc, n)
        h = num / jnp.maximum(jnp.abs(den), jnp.exp(-m_t))[..., None]
        FL = F[:, -1]
        log_end = FL[:, None, :] - F + ic
        m_new = jnp.maximum(FL + m, jnp.max(log_end, axis=1))
        w_end = jnp.exp(log_end - m_new[:, None, :])
        a_old = jnp.exp(FL + m - m_new)
        C_new = a_old[..., None, None] * C + jnp.einsum('blh,blhd,blhv->bhdv', w_end, kc, vc)
        n_new = a_old[..., None] * n + jnp.einsum('blh,blhd->bhd', w_end, kc)
        return (C_new, n_new, m_new), h

    f32 = jnp.float32
    (C, n, m), h = lax.scan(step, (C0.astype(f32), n0.astype(f32), m0.astype(f32)),
                            (_to_chunks(q.astype(f32), L), _to_chunks(k.astype(f32), L), _to_chunks(v.astype(f32), L),
                             _to_chunks(ig, L), _to_chunks(lf, L)))
    return _from_chunks(h), C, n, m

def _rwkv_scan(r, w, k, v, kk, a, S0):
    def step(S, inp):
        rt, wt, kt, vt, kkt, at = inp
        Skk = jnp.einsum('bhvk,bhk->bhv', S, kkt)
        S = S * wt[:, :, None, :] - Skk[..., None] * (kkt * at)[:, :, None, :] + vt[..., None] * kt[:, :, None, :]
        return S, jnp.einsum('bhvk,bhk->bhv', S, rt)

    xs = tuple(jnp.moveaxis(t, 1, 0) for t in (r, w, k, v, kk, a))
    S, o = lax.scan(step, S0.astype(jnp.float32), xs)
    return jnp.moveaxis(o, 0, 1), S

def _causal_conv(x, buf, w, b):
    T = x.shape[1]
    xp = jnp.concatenate([buf.astype(x.dtype), x], axis=1)
    y = b + sum(xp[:, j:j + T] * w[j] for j in range(CONV_W))
    return y, xp[:, xp.shape[1] - (CONV_W - 1):]

def _token_shift(z, prev, mu):
    zp = jnp.concatenate([prev.astype(z.dtype)[:, None], z[:, :-1]], axis=1)
    return z + (zp - z) * mu, z[:, -1]

def _swiglu(h, wg, wu, wd):
    return (jax.nn.silu(h @ wg) * (h @ wu)) @ wd

def _moe(h, router, wg, wu, wd):
    logits = jnp.einsum('btd,de->bte', h, router).astype(jnp.float32)
    top_v, top_i = lax.top_k(logits, TOP_K)
    probs = jax.nn.softmax(top_v, axis=-1)
    combine = jnp.sum(jax.nn.one_hot(top_i, N_EXPERTS, dtype=jnp.float32) * probs[..., None], axis=-2)
    y = jnp.zeros(h.shape[:-1] + (wd.shape[-1],), h.dtype)
    for e in range(N_EXPERTS):
        y = y + combine[..., e:e + 1].astype(h.dtype) * _swiglu(h, wg[e], wu[e], wd[e])
    return y

def _mixer(x, pos, states, p):
    ret_S, ml_C, ml_n, ml_m, ml_buf, rw_S, rw_prev = states
    B, T = x.shape[0], x.shape[1]
    dt = x.dtype
    f32 = jnp.float32
    h = _rmsnorm(x, p['norm_mix'])
    z = h @ p['w_in']
    rq, rk, rv, rg, mx, mv, mi, mf, mo, zrw, zgate = _split(z, IN_SPLITS)

    q = _rotary(rq.reshape(B, T, RET_HEADS, RET_DK), pos)
    k = _rotary(rk.reshape(B, T, RET_HEADS, RET_DK), pos) * (RET_DK ** -0.5)
    v = rv.reshape(B, T, RET_HEADS, RET_DV)
    o_ret, ret_S_new = _retention(q, k, v, ret_S)
    y_ret = jax.nn.silu(rg.astype(f32)) * _head_norm(o_ret, p['ret_gn'], None, GN_EPS)

    xc, buf_new = _causal_conv(mx, ml_buf, p['ml_conv_w'], p['ml_conv_b'])
    xc = jax.nn.silu(xc)
    xch = xc.reshape(B, T, ML_HEADS, ML_DH)
    mq = jnp.einsum('bthd,hde->bthe', xch, p['ml_wq'])
    mk = jnp.einsum('bthd,hde->bthe', xch, p['ml_wk']) * (ML_DH ** -0.5)
    mvh = mv.reshape(B, T, ML_HEADS, ML_DH)
    ig = (mi + p['ml_bi']).astype(f32)
    lf = jax.nn.log_sigmoid((mf + p['ml_bf']).astype(f32))
    o_ml, C_new, n_new, m_new = _mlstm(mq, mk, mvh, ig, lf, ml_C, ml_n, ml_m)
    y_ml = jax.nn.sigmoid(mo.astype(f32)) * (_head_norm(o_ml, p['ml_gn'], None, GN_EPS)
                                              + p['ml_skip'].astype(f32) * xc.astype(f32))

    zs, prev_new = _token_shift(zrw, rw_prev, p['rw_mu'])
    r, kr, vr, wl, al, gl = _split(zs.astype(f32), RW_SPLITS)
    w = jnp.exp(-RW_DECAY_SCALE * jax.nn.sigmoid(p['rw_w0'] + jnp.tanh(wl) @ p['rw_w2']))
    a = jax.nn.sigmoid(p['rw_a0'] + al @ p['rw_a2'])
    g = jax.nn.sigmoid(gl) @ p['rw_g2']
    hd = lambda t: t.reshape(B, T, RW_HEADS, RW_DH)
    kk = hd(kr * p['rw_kk'])
    kk = kk / jnp.maximum(jnp.sqrt(jnp.sum(kk * kk, axis=-1, keepdims=True)), 1e-12)
    kr = kr * (1.0 + (a - 1.0) * p['rw_ka'])
    o_rw, rw_S_new = _rwkv_scan(hd(r), hd(w), hd(kr), hd(vr), kk, hd(a), rw_S)
    bonus = jnp.sum(hd(r * kr * p['rw_rk']), axis=-1, keepdims=True) * hd(vr)
    y_rw = (_head_norm(o_rw, p['rw_gn_w'], p['rw_gn_b'], RW_GN_EPS) + bonus.reshape(B, T, RW_W)) * g

    branches = jnp.stack([y_ret, y_ml, y_rw], axis=2).astype(dt)
    proj = jnp.einsum('btnc,ncd->btnd', branches, p['w_branch'])
    gates = jax.nn.sigmoid(zgate.reshape(B, T, N_BRANCH, D_MODEL))
    out = jnp.sum(gates * proj, axis=2) @ p['w_out']
    new = (ret_S_new, C_new, n_new, m_new, buf_new, rw_S_new, prev_new)
    return x + out.astype(dt), tuple(ns.astype(s.dtype) for ns, s in zip(new, states))

def setup_inputs(seed: int = 0) -> dict:
    key = jax.random.key(seed)
    ks = iter(jax.random.split(key, 64))
    f32 = jnp.float32

    def nrm(shape, s):
        return s * jax.random.normal(next(ks), shape, f32)

    def gain(shape):
        return 1.0 + nrm(shape, 0.02)

    inp = {}
    inp['x_prompt'] = nrm((BATCH, SEQ, D_MODEL), 1.0)
    inp['x_sample'] = nrm((DEC_BATCH, DEC_SEQ, D_MODEL), 1.0)
    inp['state_ret'] = nrm((DEPTH, DEC_BATCH, RET_HEADS, RET_DK, RET_DV), 0.3)
    inp['state_mlstm_C'] = nrm((DEPTH, DEC_BATCH, ML_HEADS, ML_DH, ML_DH), 0.1)
    inp['state_mlstm_n'] = jnp.abs(nrm((DEPTH, DEC_BATCH, ML_HEADS, ML_DH), 0.3))
    inp['state_mlstm_m'] = nrm((DEPTH, DEC_BATCH, ML_HEADS), 1.0)
    inp['state_mlstm_conv'] = nrm((DEPTH, DEC_BATCH, CONV_W - 1, ML_W), 1.0)
    inp['state_rwkv'] = nrm((DEPTH, DEC_BATCH, RW_HEADS, RW_DH, RW_DH), 0.1)
    inp['state_rwkv_shift'] = nrm((DEPTH, DEC_BATCH, RW_COLS), 1.0)
    inp['norm_mix'] = gain((DEPTH, D_MODEL))
    inp['w_in'] = nrm((DEPTH, D_MODEL, N_IN), D_MODEL ** -0.5)
    inp['ret_gn'] = gain((DEPTH, RET_W))
    inp['ml_conv_w'] = nrm((DEPTH, CONV_W, ML_W), CONV_W ** -0.5)
    inp['ml_conv_b'] = nrm((DEPTH, ML_W), 0.01)
    inp['ml_wq'] = nrm((DEPTH, ML_HEADS, ML_DH, ML_DH), ML_DH ** -0.5)
    inp['ml_wk'] = nrm((DEPTH, ML_HEADS, ML_DH, ML_DH), ML_DH ** -0.5)
    inp['ml_bi'] = nrm((DEPTH, ML_HEADS), 0.1)
    inp['ml_bf'] = jnp.linspace(3.0, 6.0, ML_HEADS, dtype=f32)[None, :] + nrm((DEPTH, ML_HEADS), 0.1)
    inp['ml_gn'] = gain((DEPTH, ML_W))
    inp['ml_skip'] = gain((DEPTH, ML_W))
    inp['rw_mu'] = jax.random.uniform(next(ks), (DEPTH, RW_COLS), f32)
    inp['rw_w0'] = nrm((DEPTH, RW_W), 1.0)
    inp['rw_w2'] = nrm((DEPTH, RW_LORA_W, RW_W), RW_LORA_W ** -0.5)
    inp['rw_a0'] = nrm((DEPTH, RW_W), 0.5)
    inp['rw_a2'] = nrm((DEPTH, RW_LORA_A, RW_W), RW_LORA_A ** -0.5)
    inp['rw_g2'] = nrm((DEPTH, RW_LORA_G, RW_W), RW_LORA_G ** -0.5)
    inp['rw_kk'] = 0.85 + nrm((DEPTH, RW_W), 0.02)
    inp['rw_ka'] = gain((DEPTH, RW_W))
    inp['rw_rk'] = nrm((DEPTH, RW_W), 0.1)
    inp['rw_gn_w'] = gain((DEPTH, RW_W))
    inp['rw_gn_b'] = nrm((DEPTH, RW_W), 0.01)
    inp['w_branch'] = nrm((DEPTH, N_BRANCH, BRANCH_W, D_MODEL), BRANCH_W ** -0.5)
    inp['w_out'] = nrm((DEPTH, D_MODEL, D_MODEL), D_MODEL ** -0.5)
    inp['norm_ffn'] = gain((DEPTH, D_MODEL))
    inp['ffn_w_gate'] = nrm((N_DENSE, D_MODEL, D_FF), D_MODEL ** -0.5)
    inp['ffn_w_up'] = nrm((N_DENSE, D_MODEL, D_FF), D_MODEL ** -0.5)
    inp['ffn_w_down'] = nrm((N_DENSE, D_FF, D_MODEL), D_FF ** -0.5)
    inp['moe_router'] = nrm((N_MOE, D_MODEL, N_EXPERTS), D_MODEL ** -0.5)
    inp['moe_w_gate'] = nrm((N_MOE, N_EXPERTS, D_MODEL, D_FF_EXPERT), D_MODEL ** -0.5)
    inp['moe_w_up'] = nrm((N_MOE, N_EXPERTS, D_MODEL, D_FF_EXPERT), D_MODEL ** -0.5)
    inp['moe_w_down'] = nrm((N_MOE, N_EXPERTS, D_FF_EXPERT, D_MODEL), D_FF_EXPERT ** -0.5)
    inp['final_norm'] = gain((D_MODEL,))
    return inp

def reference(x_prompt, x_sample, state_ret, state_mlstm_C, state_mlstm_n, state_mlstm_m, state_mlstm_conv,
              state_rwkv, state_rwkv_shift, norm_mix, w_in, ret_gn, ml_conv_w, ml_conv_b, ml_wq, ml_wk, ml_bi,
              ml_bf, ml_gn, ml_skip, rw_mu, rw_w0, rw_w2, rw_a0, rw_a2, rw_g2, rw_kk, rw_ka, rw_rk, rw_gn_w,
              rw_gn_b, w_branch, w_out, norm_ffn, ffn_w_gate, ffn_w_up, ffn_w_down, moe_router, moe_w_gate,
              moe_w_up, moe_w_down, final_norm):
    Bp = x_prompt.shape[0]
    pos_p = jnp.arange(x_prompt.shape[1], dtype=jnp.int32)
    pos_s = PAST_LEN + jnp.arange(x_sample.shape[1], dtype=jnp.int32)
    sample_states = (state_ret, state_mlstm_C, state_mlstm_n, state_mlstm_m, state_mlstm_conv,
                     state_rwkv, state_rwkv_shift)
    yp, ys = x_prompt, x_sample
    new_p, new_s = [], []
    for l in range(DEPTH):
        p = {'norm_mix': norm_mix[l], 'w_in': w_in[l], 'ret_gn': ret_gn[l],
             'ml_conv_w': ml_conv_w[l], 'ml_conv_b': ml_conv_b[l], 'ml_wq': ml_wq[l], 'ml_wk': ml_wk[l],
             'ml_bi': ml_bi[l], 'ml_bf': ml_bf[l], 'ml_gn': ml_gn[l], 'ml_skip': ml_skip[l],
             'rw_mu': rw_mu[l], 'rw_w0': rw_w0[l], 'rw_w2': rw_w2[l], 'rw_a0': rw_a0[l], 'rw_a2': rw_a2[l],
             'rw_g2': rw_g2[l], 'rw_kk': rw_kk[l], 'rw_ka': rw_ka[l], 'rw_rk': rw_rk[l],
             'rw_gn_w': rw_gn_w[l], 'rw_gn_b': rw_gn_b[l], 'w_branch': w_branch[l], 'w_out': w_out[l]}
        zero_states = tuple(jnp.zeros((Bp,) + s.shape[2:], s.dtype) for s in sample_states)
        yp, st_p = _mixer(yp, pos_p, zero_states, p)
        ys, st_s = _mixer(ys, pos_s, tuple(s[l] for s in sample_states), p)
        i = l // 2
        if l % 2 == 0:
            yp = yp + _swiglu(_rmsnorm(yp, norm_ffn[l]), ffn_w_gate[i], ffn_w_up[i], ffn_w_down[i])
            ys = ys + _swiglu(_rmsnorm(ys, norm_ffn[l]), ffn_w_gate[i], ffn_w_up[i], ffn_w_down[i])
        else:
            yp = yp + _moe(_rmsnorm(yp, norm_ffn[l]), moe_router[i], moe_w_gate[i], moe_w_up[i], moe_w_down[i])
            ys = ys + _moe(_rmsnorm(ys, norm_ffn[l]), moe_router[i], moe_w_gate[i], moe_w_up[i], moe_w_down[i])
        new_p.append(st_p)
        new_s.append(st_s)
    y_prompt = _rmsnorm(yp, final_norm)
    y_sample = _rmsnorm(ys, final_norm)
    ret_p, mlstm_C_p, mlstm_n_p, mlstm_m_p, mlstm_conv_p, rwkv_p, rwkv_shift_p = (
        jnp.stack([st[j] for st in new_p]) for j in range(7))
    ret_s, mlstm_C_s, mlstm_n_s, mlstm_m_s, mlstm_conv_s, rwkv_s, rwkv_shift_s = (
        jnp.stack([st[j] for st in new_s]) for j in range(7))
    return (y_prompt, y_sample, ret_p, mlstm_C_p, mlstm_n_p, mlstm_m_p, mlstm_conv_p, rwkv_p, rwkv_shift_p,
            ret_s, mlstm_C_s, mlstm_n_s, mlstm_m_s, mlstm_conv_s, rwkv_s, rwkv_shift_s)


_drawn_inputs = setup_inputs


def setup_inputs(seed=0):
    import zlib

    import numpy as np

    out = dict(_drawn_inputs(seed))
    spreads = {}
    factors = {'ml_gn': 11.698,
     'ml_skip': 24.072,
     'rw_kk': 133.746,
     'rw_gn_b': 26.538,
     'final_norm': 24.071,
     'ret_gn': 6.403,
     'rw_ka': 2.81,
     'rw_gn_w': 11.946,
     'norm_ffn': 3.284}
    for name, (base, spread) in spreads.items():
        noise = np.random.default_rng([zlib.crc32(name.encode()), seed]).standard_normal(out[name].shape)
        drawn = base * np.exp(spread * noise) if base else spread * noise
        out[name] = jnp.asarray(drawn.astype(out[name].dtype))
    for name, factor in factors.items():
        out[name] = (out[name] * factor).astype(out[name].dtype)
    return out
```

```python
from contextlib import ExitStack

import concourse.bass as bass
import numpy as np
from concourse import mybir

F32 = mybir.dt.float32
ACT = mybir.ActivationFunctionType
ALU = mybir.AluOpType
AX_X = mybir.AxisListType.X

P = 128
DEPTH = 2
D = 1024
KT = D // P
TP, SB, ST = 256, 8, 4
TS = SB * ST
T = TP + TS
PAST = 2048
NH = 4
DK = 64
CONV = 4
ZT = 14
ZP = 1 + TP + SB * (1 + ST)
XPAD = CONV - 1
XW = XPAD + TP + SB * (XPAD + ST)
FT = 11
NE = 8
NDENSE = 2
CH = 64
NC = TP // CH + 1
NP4 = 4
NU = NC * NP4
PW = 2 * P + P + TS
RING = 5
SLOT = 2048
NORM_EPS, GN_EPS, RW_GN_EPS = 1e-6, 1e-5, 64e-5
RW_DECAY = 0.606531
NEG = -1.0e30
LEVELS = (2, 4, 8, 16, 32)

VEC = {}
_at = 0
for _n, _w in (("norm_mix", 8), ("norm_ffn", 8), ("ret_gn", 4), ("conv_w", 16), ("conv_b", 4), ("ml_gn", 4),
               ("ml_skip", 4), ("mu", 14), ("w0", 4), ("a0", 4), ("kk", 4), ("ka", 4), ("rk", 4), ("gn_w", 4),
               ("gn_b", 4), ("final", 8)):
    VEC[_n] = _at
    _at += _w
NVEC = _at

LW = {}
_at = 0
for _n, _w in (("if", KT * 8), ("wq", 512), ("wk", 512), ("lora", 512), ("g2", 512), ("router", KT * NE)):
    LW[_n] = _at
    _at += _w
NLW = _at

CON = {}
_at = 0
for _n, _w in (("ident", 128), ("ones", 128), ("swap", 128), ("cent128", 128), ("cent64", 128), ("ones64", 128),
               ("cos", T), ("sin", T), ("causal_neg", 128), ("sample_neg", TS), ("reset64", T), ("reset_mul", T),
               ("reset_add", T), ("gram_p", 128), ("gram_s", 128), ("a_p", 64), ("a_s", 64), ("ident64", 64),
               ("join0", 64), ("join0t", 64), ("joins", 5 * 64), ("kdec", 12), ("qdec", 2 * TS), ("g4", 2),
               ("bmask", 8), ("bmask2", 8), ("sel", 1024)):
    CON[_n] = _at
    _at += _w
NCON = _at


def shape_constants():
    c = np.zeros((P, NCON), np.float32)
    r = np.arange(P)

    def put(name, a):
        a = np.asarray(a, np.float32)
        c[:a.shape[0], CON[name]:CON[name] + a.shape[1]] = a

    put("ident", np.eye(P))
    put("ones", np.ones((P, P)))
    half = DK // 2
    other = r // DK * DK + (r % DK + half) % DK
    put("swap", (other[:, None] == r[None, :]))
    put("cent128", np.eye(P) - 1.0 / P)
    same = (r[:, None] // DK == r[None, :] // DK)
    put("cent64", np.eye(P) - same / DK)
    put("ones64", same)
    pos = np.concatenate([np.arange(TP), np.tile(PAST + np.arange(ST), SB)]).astype(np.float32)
    inv = (10000.0 ** (-np.arange(half, dtype=np.float64) / half)).astype(np.float32)
    ang = (pos[None, :] * inv[r % half][:, None]).astype(np.float32).astype(np.float64)
    put("cos", np.cos(ang))
    put("sin", np.sin(ang) * np.where(r % DK < half, -1.0, 1.0)[:, None])
    put("causal_neg", np.where(r[:, None] <= r[None, :], 0.0, NEG))
    s = np.arange(TS)
    seq = s[:, None] // ST == s[None, :] // ST
    put("sample_neg", np.where(seq & (s[:, None] <= s[None, :]), 0.0, NEG))
    col = np.arange(T)
    starts = (col >= TP) & ((col - TP) % ST == 0)
    put("reset64", np.tile(~(starts | ((col < TP) & (col % CH == 0))), (P, 1)))
    put("reset_mul", np.tile(~(starts | (col == 0)), (P, 1)))
    put("reset_add", np.tile(np.where(starts | (col == 0), NEG, 0.0), (P, 1)))
    t = np.arange(CH)
    blk = (t[:, None] // ST == t[None, :] // ST) & (t[:, None] < TS) & (t[None, :] < TS)
    for name, ok in (("p", np.ones((CH, CH), bool)), ("s", blk)):
        strict, incl = (t[:, None] < t[None, :]) & ok, (t[:, None] <= t[None, :]) & ok
        put("gram_" + name, np.tile(np.concatenate([strict, incl], 1), (2, 1)))
        put("a_" + name, np.tile((t[None, :] < t[:, None]) & ok, (2, 1)))
    put("ident64", np.tile(np.eye(CH), (2, 1)))

    def join(m):
        return np.where((t[:, None] // m + 1 == t[None, :] // m) & (t[:, None] // (2 * m) == t[None, :] // (2 * m)), -1.0, 0.0)

    put("join0", np.tile(join(1), (2, 1)))
    put("join0t", np.tile(join(1).T, (2, 1)))
    put("joins", np.tile(np.concatenate([join(m) for m in LEVELS], 1), (2, 1)))
    lg = np.log1p(-(2.0 ** (-5.0 - np.arange(NH))))
    tok = np.arange(P)[:, None]
    kd = [np.exp((TP - 1 - tok) * lg), np.exp((TP - 1 - tok - P) * lg), np.exp((ST - 1 - tok % ST) * lg)]
    put("kdec", np.concatenate(kd, 1))
    head = r // DK
    put("qdec", np.concatenate([np.exp((s % ST + 1)[None, :] * lg[2 * i + head][:, None]) for i in range(2)], 1))
    put("g4", np.stack([np.exp(ST * lg[2 * i + head]) for i in range(2)], 1))
    put("bmask", r[:, None] // ST == np.arange(SB)[None, :])
    put("bmask2", (r % CH)[:, None] // ST == np.arange(SB)[None, :])
    put("sel", np.repeat(np.eye(8), P, 1))
    dec = np.zeros((P, NH, PW), np.float32)
    for h in range(NH):
        d0 = np.arange(TP)[None, :] - r[:, None]
        d1 = d0[:, :P]
        ds = s[None, :] - s[:, None]
        dec[:, h, 0:TP] = np.where(d0 >= 0, np.exp(np.maximum(d0, 0) * lg[h]), 0)
        dec[:, h, TP:TP + P] = np.where(d1 >= 0, np.exp(np.maximum(d1, 0) * lg[h]), 0)
        dec[:TS, h, TP + P:] = np.where(seq & (ds >= 0), np.exp(np.maximum(ds, 0) * lg[h]), 0)
    return c, dec.reshape(P, NH * PW)


def mixer_slabs():
    early = [("mx", 0), ("mx", 1), ("mv", 0), ("mv", 1)] + [("zrw", i) for i in range(7)]
    early += [("rq", 0), ("rk", 0), ("rv", 0), ("rv", 1), ("mo", 0), ("mo", 1), ("rg", 0), ("rg", 1)]
    late = []
    for j in range(KT // 2):
        late += [("gate", 3 * j + n) for n in range(3)] + [("branch", 2 * j), ("branch", 2 * j + 1)]
    return early, late, [("out", j) for j in range(4)]


EARLY, LATE, OUTS = mixer_slabs()
NSLAB = len(EARLY) + len(LATE) + len(OUTS)


class Signal:

    def __init__(self, sem, per_layer=1):
        self.sem, self.per = sem, per_layer

    def __call__(self, layer, k=1):
        return self.sem, layer * self.per + k


class Turns:

    def __init__(self):
        self.turn, self.used = 0, [0] * RING

    def take(self):
        s = self.turn % RING
        n = self.used[s]
        self.turn, self.used[s] = self.turn + 1, n + 1
        return s, n

    def pass_over(self, n):
        for _ in range(n):
            self.take()

    def loop(self, i, turns, padded=0):
        inner = Turns()
        inner.turn = self.turn
        per = [0] * RING
        for k in range(turns):
            per[(self.turn + k) % RING] += 1
        inner.used = [self.used[s] + i * per[s] for s in range(RING)]
        return inner

    def after(self, passes, turns, padded=0):
        for k in range(turns):
            self.used[(self.turn + k) % RING] += passes
        self.turn += passes * (turns + padded)


GROUPS = ([("mx", j) for j in range(4)] + [("mi", 0), ("mf", 0)] + [("mv", j) for j in range(6)] +
          [("zrw", j) for j in range(ZT)] + [("rq", j) for j in range(2)] + [("rk", j) for j in range(2)] +
          [("rv", j) for j in range(6)] + [("mo", j) for j in range(4)] + [("rg", j) for j in range(4)])
NG = len(GROUPS)


def piece_of(kind, j):
    if kind in ("mi", "mf"):
        return None, 0, False
    if kind in ("mv", "rv"):
        return j // 3, j % 3, j % 3 == 2
    return j // 2, j % 2, j % 2 == 1


NPROJ = sum(not piece_of(*g)[2] for g in GROUPS)


def seq4(ap):
    return ap.rearrange("p (b t) -> p b t", t=ST)


def build(nc, a, o):
    with ExitStack() as ctx:
        def sb(name, shape):
            return ctx.enter_context(nc.sbuf_tensor(name, shape, F32))

        def sig(name, per_layer=1):
            return Signal(ctx.enter_context(nc.semaphore(name)), per_layer)

        ps = ctx.enter_context(nc.psum_tensor("ps", [P, 8, 512], F32))
        X = sb("X", [P, KT, T])
        xn = sb("xn", [P, KT, T])
        ring = sb("ring", [P, RING, SLOT])
        lw = sb("lw", [P, NLW])
        vec = sb("vec", [P, DEPTH, NVEC])
        con = sb("con", [P, NCON])
        y_ret, y_ml, y_rw = sb("y_ret", [P, 4, T]), sb("y_ml", [P, 4, T]), sb("y_rw", [P, 4, T])
        rstd = sb("rstd", [P, T])
        gate_bias = sb("gate_bias", [NH, DEPTH, 2])
        m0 = sb("m0", [NH, DEPTH, SB])
        hist = sb("hist", [P, 4 * SB * XPAD])
        prev = sb("prev", [P, ZT * SB])
        conv_out = sb("conv_out", [P, 4, (1 + SB) * XPAD])
        shift_out = sb("shift_out", [P, ZT, 1 + SB])
        m_out = sb("m_out", [NH, 1 + SB])
        n_out = sb("n_out", [P, NH + SB * NH])
        gate_rows = sb("gate_rows", [NH, 1, T])
        ARENA = 26900
        arena = sb("arena", [P, ARENA])

        def at(start, *dims):
            n = int(np.prod(dims))
            assert start + n <= ARENA, (start, dims)
            v = arena[:, start:start + n]
            if len(dims) == 2:
                v = v.rearrange("p (a b) -> p a b", a=dims[0])
            if len(dims) == 3:
                v = v.rearrange("p (a b c) -> p a b c", a=dims[0], b=dims[1])
            if len(dims) == 4:
                v = v.rearrange("p (a b c d) -> p a b c d", a=dims[0], b=dims[1], c=dims[2])
            return v

        def C(name, w, rows=P, off=0):
            return con[0:rows, CON[name] + off:CON[name] + off + w]

        def V(l, name, j=0):
            return vec[:, l, VEC[name] + j:VEC[name] + j + 1]

        norm_sq = at(4158, KT, T)
        z = at(0, ZT, ZP)
        mxp = at(4158, 4, XW)
        ml_o = at(4158, 4, T)
        xc = at(5418, 4, T)
        mq = at(6570, 4, T)
        mk = at(7722, 4, T)
        mkt = at(8874, 3, 512)
        mvt = at(10410, 3, 512)
        C0 = at(11946, SB, NH, P)
        kb = at(16042, 2, 512)
        rows = at(17066, 4, T)
        ml_W = at(18218, PW)
        ml_PW = at(18634, PW)
        ml_sq = at(19050, 4, T)
        ml_den = at(20202, T)
        gwc = at(20490, 24)
        qa = at(20514, TS)
        nq = at(20546, TS)
        aL = at(20578, SB, NH)
        n0 = at(20610, SB * NH)
        Cp = at(20642, 512)
        arow = at(21154, TS)
        rqk = at(21186, 4, T)
        rvt = at(22338, 3, 512)
        qr = at(4158, 4, T)
        rt = at(5310, 4, T)
        ktd = at(6462, 3, 256)
        qd = at(7230, 2, TS)
        rpw = at(7294, 2, PW)
        rkb = at(8126, 2, 256)
        Sp_ret = at(8638, 256)
        ret_o = at(8894, 4, T)
        ret_sq = at(10046, 4, T)
        dec = at(16042, NH, PW)
        S0_ret = at(17706, SB, 2, P)
        zs = at(4158, ZT, T)
        rw_lw = at(8190, 4, T)
        rw_a = at(9342, 4, T)
        rw_kk = at(10494, 4, T)
        rw_kp = at(11646, 4, T)
        rw_e1 = at(12798, 4, T)
        rw_e2 = at(13950, 4, T)
        lora_in = at(15102, T)
        lora_g = at(15390, T)
        rw_g = at(15678, 4, T)
        rw_bv = at(16830, 4, T)
        BK = at(17982, NP4, NC, 2 * CH)
        KR = at(20542, NP4, NC, 2 * CH)
        UV = at(23102, NC, 512)
        PL = at(25662, NP4, 4 + SB)
        rw_o = at(25710, 4, T)
        G = at(0, NC, 2, NP4 * P)
        XT = at(5120, NU, 2 * CH)
        Abd = at(7680, NU, P)
        Xbd = at(10240, NU, P)
        Xc = at(12800, NU, CH)
        Yc = at(14080, NU, CH)
        BKt = at(7680, NC, 512)
        S0bd = at(10240, SB, NP4, P)
        Sbd = at(14336, NP4, P)
        Rn = at(14848, 512)
        CX = at(15360, NP4, 2, TS)
        KBm = [at(14848, 512), at(5120, 512)]
        rw_sq = at(0, 4, T)
        gates = at(0, 6, T)
        gtmp = at(1728, 3, T)
        mixed = at(2592, KT, T)
        hid = at(7000, FT, T)
        sil = at(10200, 3, T)
        comb = at(11100, NE, T)
        ytmp = at(13500, 2, T)
        lg, top, gt, eq, cum, ex = (at(14100 + 24 * k, 3, NE) for k in range(6))
        cnt, cnt2 = at(14300, 3), at(14304, 3)
        crow = at(14310, T)

        slot_ld = [sig(f"slot_loaded{s}") for s in range(RING)]
        slot_fr = [sig(f"slab_used{s}") for s in range(RING)]
        ld_con, ld_x, ld_lw, ld_hist = sig("ld_con"), sig("ld_x"), sig("ld_lw"), sig("ld_hist")
        ld_c0, ld_n0, ld_ret, ld_rw = sig("ld_c0"), sig("ld_n0"), sig("ld_ret"), sig("ld_rw")
        st_ml, st_small, st_ret, st_rw, st_y = sig("st_ml"), sig("st_small"), sig("st_ret"), sig("st_rw"), sig("st_y")
        dch, ach, gch = sig("vector_chain"), sig("scalar_chain"), sig("pool_chain")
        nm_sq, nm_ms, nm_rec, nm_rstd, nm_xn = (sig(n) for n in ("nm_sq", "nm_ms", "nm_rec", "nm_rstd", "nm_xn"))
        proj, evac = sig("proj", NPROJ), sig("evac", NG)
        pads = sig("pads")
        conv_acc, xc_ok = sig("conv_acc"), sig("xc_ok")
        u_abs, u_exp, lf_ok, gr_ok, er_ok = sig("u_min"), sig("u_softplus"), sig("lf_ok"), sig("gr_ok"), sig("er_ok")
        ml_col, ml_colv = sig("ml_col"), sig("ml_colv")
        mqk_p, mqk_e, kdec_ok = sig("mqk_p", 11), sig("mqk_e", 11), sig("kdec_ok")
        ml_bc, ml_wl, ml_ex, ml_pw = sig("ml_bc", 4), sig("ml_wl", 4), sig("ml_ex", 4), sig("ml_pw", 4)
        ml_s = sig("ml_scores", 4)
        ml_nd, ml_ad, ml_h = sig("ml_nd", 4), sig("ml_ad", 4), sig("ml_h", 4)
        ml_cp, ml_cpe, ml_kb, ml_sc, ml_sca = sig("ml_cp"), sig("ml_cpe"), sig("ml_kb", 8), sig("ml_sc", 8), sig("ml_sca", 8)
        ml_out, co_ok, so_ok = sig("ml_out"), sig("conv_out_ok"), sig("shift_out_ok")
        hn_c, hn_s, hn_x, hn_v = sig("hn_c", 12), sig("hn_s", 12), sig("hn_x", 12), sig("hn_v", 12)
        hn_r, hn_q, hn_y = sig("hn_r", 3), sig("hn_q", 3), sig("hn_y", 3)
        r_sw, r_qr, r_kt, r_ktd = sig("r_sw", 4), sig("r_qr"), sig("r_kt", 3), sig("r_ktd", 3)
        r_sc, r_pw, r_o, r_oe = sig("r_sc", 4), sig("r_pw", 4), sig("r_o", 4), sig("r_oe", 4)
        r_sp, r_spe, r_kb, r_ss, r_ssa = sig("r_sp"), sig("r_spe"), sig("r_kb", 8), sig("r_ss", 8), sig("r_ssa", 8)
        w_zs, w_thl, w_lora, w_lorae = sig("w_zs"), sig("w_thl"), sig("w_lora", 12), sig("w_lorae", 12)
        w_sq, w_ss, w_rk, w_bo = sig("w_sq"), sig("w_ss", 4), sig("w_rk"), sig("w_bo", 4)
        w_ssr, w_ssq, w_F, w_E, w_vt, w_vte = sig("w_ssr"), sig("w_ssq"), sig("w_F"), sig("w_E"), sig("w_vt", 5), sig("w_vte", 5)
        w_pre, w_sz, w_zuv, w_zab, rw_y, w_ob = (sig("w_pre"), sig("w_sz"), sig("w_zuv", 4), sig("w_zab", 2), sig("rw_y"),
                                                sig("w_ob", 5))
        w_g1, w_g1e, w_g2, w_g2e = sig("w_g1", 10), sig("w_g1e", 10), sig("w_g2", 6), sig("w_g2e", 6)
        w_x0 = sig("w_x0")
        w_y, w_ye, w_p, w_pe, w_t, w_te = (sig("w_y", 15), sig("w_ye", 15), sig("w_p", 15), sig("w_pe", 15),
                                           sig("w_t", 20), sig("w_te", 12))
        w_to = sig("w_to", 8)
        w_xt, w_bt, w_bte = sig("w_xt", 2), sig("w_bt", 5), sig("w_bte", 5)
        w_r, w_rn, w_u, w_ue, w_s, w_su, w_oc = (sig("w_r", 5), sig("w_rn", 5), sig("w_u", 5), sig("w_ue", 5),
                                                 sig("w_s", 4), sig("w_su", 4), sig("w_oc", 5))
        w_oe = sig("w_oe", 5)
        w_cx, w_cxe, w_ct = sig("w_cx"), sig("w_cxe"), sig("w_ct")
        w_kb, w_st, w_sta = sig("w_kb", 8), sig("w_st", 8), sig("w_sta", 8)
        f_zg, f_zs, f_br = sig("f_zg", 12), sig("f_zs", 24), sig("f_br", 16)
        f_gm, f_out, x_mix = sig("f_gm", 24), sig("f_out", 4), sig("x_mix", 8)
        f_mul = sig("f_mul", 24)
        g_done, s_done, h_done = sig("g_done"), sig("s_done"), sig("h_done")
        y_mul, y_done = sig("y_mul"), sig("y_done")
        rt_lg, rt_e, rt_ex, rt_cb, rt_ct, rt_cr, rt_bc, rt_bce = (sig(n) for n in (
            "rt_lg", "rt_e", "rt_ex", "rt_cb", "rt_ct", "rt_cr", "rt_bc", "rt_bce"))
        PASSES = (NDENSE, NE)
        CREDIT_H, CREDIT_Y = 3, 2

        def h_base(l):
            return FT * NDENSE * l

        def y_base(l):
            return KT * NDENSE * l

        TOK = ((0, P), (P, P), (TP, TS))

        block = ctx.enter_context(nc.Block())

        @block.sync
        def _(sp):
            turns = Turns()

            def load(turns, src, width):
                s, n = turns.take()
                if not isinstance(n, int) or n > 0:
                    sp.wait_ge(slot_fr[s].sem, n)
                sp.dma_start(ring[:, s, 0:width], src).then_inc(slot_ld[s].sem, 16)

            sp.dma_start(X[:, :, :], a["x"]).then_inc(ld_x.sem, 16)
            sp.dma_start(con[:, :], a["con"]).then_inc(ld_con.sem, 16)
            sp.dma_start(vec[:, :, :], a["vec"]).then_inc(ld_con.sem, 16)
            sp.dma_start(gate_bias[:, :, :], a["bias"]).then_inc(ld_con.sem, 16)
            sp.dma_start(m0[:, :, :], a["m0"]).then_inc(ld_con.sem, 16)
            for l in range(DEPTH):
                if l > 0:
                    sp.wait_ge(*x_mix(l - 1, 8))
                    sp.wait_ge(*nm_xn(2 * l - 1))
                sp.dma_start(lw[:, :], a["lw"][l]).then_inc(ld_lw.sem, 16)
                for k in range(len(EARLY)):
                    load(turns, a["mix"][l, k], SLOT)
                with sp.Fori(0, KT // 2) as j:
                    inner = turns.loop(j, 5)
                    for k in range(5):
                        slab = a["mix"][l, bass.ds(j * 5 + (len(EARLY) + k), 1)].rearrange("a p n -> p (a n)")
                        load(inner, slab, SLOT)
                turns.after(KT // 2, 5)
                for k in range(4):
                    load(turns, a["mix"][l, len(EARLY) + len(LATE) + k], SLOT)
                with sp.Fori(0, PASSES[l]) as e:
                    inner = turns.loop(e, FT + KT, 1)
                    first = e + l * NDENSE
                    for f in range(FT):
                        load(inner, a["gu"][bass.ds(first * FT + f, 1)].rearrange("a p n -> p (a n)"), SLOT)
                    for d in range(KT):
                        load(inner, a["down"][bass.ds(first * KT + d, 1)].rearrange("a p n -> p (a n)"), FT * P)
                turns.after(PASSES[l], FT + KT, 1)
            sp.wait_ge(*nm_xn(2 * DEPTH))
            sp.dma_start(o["y"], xn[:, :, :]).then_inc(st_y.sem, 16)
            sp.wait_ge(st_y.sem, 16)

        @block.tensor
        def _(pe):
            turns = Turns()
            mm = pe.matmul

            def slab(turns):
                s, n = turns.take()
                pe.wait_ge(slot_ld[s].sem, (n + 1) * 16)
                return s

            def norm(n):
                pe.wait_ge(*nm_sq(n))
                for k in range(KT):
                    last = mm(ps[:, 4, 0:T], C("ones", P), norm_sq[:, k, :], start=(k == 0), stop=(k == KT - 1))
                last.then_inc(nm_ms.sem, 1)
                pe.wait_ge(*nm_xn(n))

            current = [None, None]

            def groups(l, first, end):
                for n in range(first, end):
                    kind, j = GROUPS[n]
                    if n >= 4:
                        pe.wait_ge(*evac(l, n - 3))
                    bank = ps[:, n % 4, :]
                    if kind in ("mi", "mf"):
                        if kind == "mi":
                            pe.wait_ge(ld_lw.sem, 16 * (l + 1))
                        off = LW["if"] + (4 if kind == "mf" else 0)
                        for k in range(KT):
                            last = mm(bank[0:NH, 0:T], lw[:, off + 8 * k:off + 8 * k + 4], xn[:, k, :],
                                      start=(k == 0), stop=(k == KT - 1))
                        last.then_inc(proj.sem, 1)
                        continue
                    tokens = kind in ("mv", "rv")
                    piece, part, is_last = piece_of(kind, j)
                    if current[0] != (l, kind, piece):
                        current[0], current[1] = (l, kind, piece), slab(turns)
                    s = current[1]
                    for k in range(KT):
                        if tokens:
                            c0, m = TOK[part]
                            last = mm(bank[0:m, 0:256], xn[:, k, c0:c0 + m], ring[:, s, 256 * k:256 * k + 256],
                                      start=(k == 0), stop=(k == KT - 1))
                        else:
                            w0 = 256 * k + P * part
                            last = mm(bank[:, 0:T], ring[:, s, w0:w0 + P], xn[:, k, :],
                                      start=(k == 0), stop=(k == KT - 1))
                    if is_last:
                        last.then_inc(slot_fr[s].sem, 1)
                    else:
                        last.then_inc(proj.sem, 1)

            def head_norm(q, src, sq, centre, ones):
                for j in range(4):
                    last = mm(ps[:, 4 + j, 0:T], centre, src[:, j, :], start=True, stop=True)
                    last.then_inc(hn_c.sem, 1)
                for j in range(4):
                    pe.wait_ge(hn_s.sem, 4 * q + j + 1)
                    pe.wait_ge(hn_x.sem, 4 * q + j + 1)
                    mm(ps[:, 4 + j, 0:T], ones, sq[:, j, :], start=True, stop=True).then_inc(hn_v.sem, 1)

            def mlstm_columns(l):
                pe.wait_ge(*gr_ok(l))
                for i, (c0, m) in enumerate(TOK):
                    for r in range(2):
                        last = pe.transpose(ps[0:m, 4, 8 * i + 4 * r:8 * i + 4 * r + 4],
                                            (rows[0:NH, 0, c0:c0 + m], rows[0:NH, 3, c0:c0 + m])[r],
                                            C("ident", NH, NH))
                last.then_inc(ml_col.sem, 1)

            def mlstm_qk(l):
                pe.wait_ge(*xc_ok(l))
                for n in range(8):
                    h, which = n // 2, ("wq", "wk")[n % 2]
                    if n >= 2:
                        pe.wait_ge(*mqk_e(l, n - 1))
                    mm(ps[:, 5 + n % 2, 0:T], lw[:, LW[which] + P * h:LW[which] + P * h + P], xc[:, h, :],
                       start=True, stop=True).then_inc(mqk_p.sem, 1)
                for i, (c0, m) in enumerate(TOK):
                    pe.wait_ge(*mqk_e(l, 8 + i - 1))
                    for h in range(NH):
                        last = mm(ps[0:m, 5 + i % 2, P * h:P * h + P], xc[:, h, c0:c0 + m],
                                  lw[:, LW["wk"] + P * h:LW["wk"] + P * h + P], start=True, stop=True)
                    last.then_inc(mqk_p.sem, 1)

            def mlstm_head(l, h):
                if h == 0:
                    pe.wait_ge(*ml_colv(l))
                    pe.wait_ge(*mqk_e(l, 11))
                    pe.wait_ge(*er_ok(l))
                    pe.wait_ge(*evac(l, 12))
                    pe.wait_ge(ld_c0.sem, 16 * (l + 1))
                else:
                    pe.wait_ge(*ml_h(l, h))
                pick = con[0:NH, CON["sel"] + P * h:CON["sel"] + P * h + P]
                mm(ps[:, 4, 0:T], pick, rows[0:NH, 1, :], start=True, stop=True)
                mm(ps[:, 4, T:T + TS], pick, arow[0:NH, :], start=True, stop=True)
                mm(ps[:, 5, 0:T], pick, rows[0:NH, 2, :], start=True, stop=True).then_inc(ml_bc.sem, 1)
                mm(ps[:, 6, 0:TP], mk[:, h, 0:P], mq[:, h, 0:TP], start=True, stop=True)
                mm(ps[:, 6, TP:TP + P], mk[:, h, P:TP], mq[:, h, P:TP], start=True, stop=True)
                mm(ps[0:TS, 6, TP + P:PW], mk[:, h, TP:T], mq[:, h, TP:T], start=True, stop=True).then_inc(ml_s.sem, 1)
                pe.wait_ge(*ml_pw(l, h + 1))
                for bank, part in ((7, "num"), (4, "den")):
                    def left(i):
                        rows_ = TOK[i][1]
                        return mvt[0:rows_, i, P * h:P * h + P] if part == "num" else C("ones", P, rows_)
                    mm(ps[:, bank, 0:TP], left(0), ml_PW[:, 0:TP], start=True, stop=False, skip_group_check=True)
                    mm(ps[:, bank, P:TP], left(1), ml_PW[:, TP:TP + P], start=False, stop=False,
                       skip_group_check=True)
                    last = mm(ps[:, bank, TP:T], left(2), ml_PW[0:TS, TP + P:PW], start=False, stop=False,
                              skip_group_check=True)
                    if part == "num":
                        for b in range(SB):
                            cs = slice(ST * b, ST * b + ST)
                            mm(ps[:, bank, TP + ST * b:TP + ST * b + ST], C0[:, b, h, :], qa[:, cs],
                               start=False, stop=(b == SB - 1), skip_group_check=True)
                    else:
                        mm(ps[:, bank, TP:T], C("ones", P), nq, start=False, stop=True,
                           skip_group_check=True).then_inc(ml_nd.sem, 1)

            def mlstm_state(l):
                pe.wait_ge(*kdec_ok(l))
                pe.wait_ge(*ml_h(l, 4))
                for h in range(NH):
                    for i in range(2):
                        mm(ps[:, 4, P * h:P * h + P], mkt[:, i, P * h:P * h + P], mvt[:, i, P * h:P * h + P],
                           start=(i == 0), stop=(i == 1))
                for h in range(NH):
                    for i in range(2):
                        last = mm(ps[:, 5, h:h + 1], mkt[:, i, P * h:P * h + P], C("ones", 1),
                                  start=(i == 0), stop=(i == 1))
                last.then_inc(ml_cp.sem, 1)
                for b in range(SB):
                    pe.wait_ge(*ml_kb(l, b + 1))
                    if b >= 2:
                        pe.wait_ge(*ml_sca(l, b - 1))
                    for h in range(NH):
                        mm(ps[:, 6 + b % 2, P * h:P * h + P], kb[0:TS, b % 2, P * h:P * h + P],
                           mvt[0:TS, 2, P * h:P * h + P], start=True, stop=True)
                        last = mm(ps[:, 5, 8 + NH * b + h:9 + NH * b + h], kb[0:TS, b % 2, P * h:P * h + P],
                                  C("ones", 1, TS), start=True, stop=True)
                    last.then_inc(ml_sc.sem, 1)

            def retention_rotate(l):
                pe.wait_ge(*evac(l, 30))
                for j in range(4):
                    mm(ps[:, 4 + j, 0:T], C("swap", P), rqk[:, j, :], start=True, stop=True).then_inc(r_sw.sem, 1)

            def retention_keys(l):
                pe.wait_ge(*r_qr(l))
                for i, (c0, m) in enumerate(TOK):
                    for j in range(2):
                        last = pe.transpose(ps[0:m, 4 + i, P * j:P * j + P], qr[:, 2 + j, c0:c0 + m], C("ident", P))
                    last.then_inc(r_kt.sem, 1)

            def retention_scores(l, h):
                i, p0 = h // 2, DK * (h % 2)
                if h == 0:
                    pe.wait_ge(*r_ktd(l, 3))
                if h >= 2:
                    pe.wait_ge(*r_pw(l, h - 1))
                bank, r = 4 + h % 2, slice(p0, p0 + DK)
                mm(ps[:, bank, 0:TP], qr[r, 2 + i, 0:P], qr[r, i, 0:TP], start=True, stop=True)
                mm(ps[:, bank, TP:TP + P], qr[r, 2 + i, P:TP], qr[r, i, P:TP], start=True, stop=True)
                mm(ps[0:TS, bank, TP + P:PW], qr[r, 2 + i, TP:T], qr[r, i, TP:T], start=True,
                   stop=True).then_inc(r_sc.sem, 1)

            def retention_values(l, h):
                i, p0 = h // 2, DK * (h % 2)
                r = slice(p0, p0 + DK)
                if h == 0:
                    pe.wait_ge(*evac(l, 36))
                    pe.wait_ge(ld_ret.sem, 32 * (l + 1))
                if h >= 2:
                    pe.wait_ge(*r_oe(l, h - 1))
                pe.wait_ge(*r_pw(l, h + 1))
                bank, w = 6 + h % 2, rpw[:, h % 2, :]
                mm(ps[:, bank, 0:TP], rvt[:, 0, P * h:P * h + P], w[:, 0:TP], start=True, stop=False,
                   skip_group_check=True)
                mm(ps[:, bank, P:TP], rvt[:, 1, P * h:P * h + P], w[:, TP:TP + P], start=False, stop=False,
                   skip_group_check=True)
                mm(ps[:, bank, TP:T], rvt[0:TS, 2, P * h:P * h + P], w[0:TS, TP + P:PW], start=False, stop=False,
                   skip_group_check=True)
                for b in range(SB):
                    last = mm(ps[:, bank, TP + ST * b:TP + ST * b + ST], S0_ret[r, b, i, :],
                              qd[r, i, ST * b:ST * b + ST], start=False, stop=(b == SB - 1), skip_group_check=True)
                last.then_inc(r_o.sem, 1)

            def retention_state(l):
                pe.wait_ge(*r_pw(l, 4))
                pe.wait_ge(*r_oe(l, 4))
                for h in range(NH):
                    i, p0 = h // 2, DK * (h % 2)
                    for t in range(2):
                        last = mm(ps[p0:p0 + DK, 4, P * i:P * i + P], ktd[:, t, DK * h:DK * h + DK],
                                  rvt[:, t, P * h:P * h + P], start=(t == 0), stop=(t == 1))
                last.then_inc(r_sp.sem, 1)
                for b in range(SB):
                    pe.wait_ge(*r_kb(l, b + 1))
                    if b >= 2:
                        pe.wait_ge(*r_ssa(l, b - 1))
                    for h in range(NH):
                        i, p0 = h // 2, DK * (h % 2)
                        last = mm(ps[p0:p0 + DK, 5 + b % 2, P * i:P * i + P], rkb[0:TS, b % 2, DK * h:DK * h + DK],
                                  rvt[0:TS, 2, P * h:P * h + P], start=True, stop=True)
                    last.then_inc(r_ss.sem, 1)

            def rwkv_prepare(l):
                pe.wait_ge(*w_thl(l))
                pe.wait_ge(*hn_y(l, 2))
                for n in range(12):
                    which, j = n // 4, n % 4
                    if n >= 2:
                        pe.wait_ge(*w_lorae(l, n - 1))
                    r = (slice(0, DK), slice(DK, P), slice(0, P))[which]
                    off = LW["g2" if which == 2 else "lora"] + P * j
                    mm(ps[:, 4 + n % 2, 0:T], lw[r, off:off + P], (lora_g if which == 2 else lora_in)[r, :],
                       start=True, stop=True).then_inc(w_lora.sem, 1)
                pe.wait_ge(*w_lorae(l, 12))
                pe.wait_ge(*w_sq(l))
                for j in range(4):
                    mm(ps[:, 4 + j, 0:T], C("ones64", P), rw_e1[:, j, :], start=True, stop=True)\
                        .then_inc(w_ss.sem, 1)
                pe.wait_ge(*w_rk(l))
                for j in range(4):
                    mm(ps[:, 4 + j, 0:T], C("ones64", P), rw_e2[:, j, :], start=True, stop=True)\
                        .then_inc(w_bo.sem, 1)
                for c in range(NC):
                    w = CH if c < NC - 1 else TS
                    for j in range(4):
                        last = pe.transpose(ps[0:w, c % 4, P * j:P * j + P], zs[:, 8 + j, CH * c:CH * c + w],
                                            C("ident", P))
                    last.then_inc(w_vt.sem, 1)
                    if c == NC - 2:
                        pe.wait_ge(*w_vte(l, 1))
                pe.wait_ge(*w_vte(l, 5))

            def rwkv_gram(l):
                pe.wait_ge(*w_pre(l))
                for c in range(NC):
                    for p in range(2):
                        n, r = 2 * c + p, slice(CH * p, CH * p + CH)
                        if n >= 4:
                            pe.wait_ge(*w_g1e(l, n - 3))
                        for j in range(NP4):
                            last = mm(ps[:, n % 4, P * j:P * j + P], BK[r, j, c, :], KR[r, j, c, :],
                                      start=True, stop=True)
                        last.then_inc(w_g1.sem, 1)
                for n in range(6):
                    p, c0 = n % 2, 2 * (n // 2)
                    r = slice(CH * p, CH * p + CH)
                    if n >= 4:
                        pe.wait_ge(*w_g2e(l, n - 3))
                    for c in range(c0, min(c0 + 2, NC)):
                        for j in range(NP4):
                            at_ = 256 * (c - c0) + CH * j
                            last = mm(ps[r, 4 + n % 4, at_:at_ + CH], KR[r, j, c, 0:CH], BK[r, j, c, 0:CH],
                                      start=True, stop=True)
                    last.then_inc(w_g2.sem, 1)

            def rwkv_invert(l):
                pe.wait_ge(*w_x0(l))
                pe.wait_ge(*w_g2e(l, 6))
                pe.wait_ge(*w_g1e(l, 10))
                for m in range(len(LEVELS)):
                    for g in range(3):
                        us = range(8 * g, min(8 * g + 8, NU))
                        if m > 0:
                            pe.wait_ge(*w_te(l, 3 * m))
                            pe.wait_ge(*w_to(l, 2 * m))
                        for u in us:
                            last = mm(ps[:, g, CH * (u - 8 * g):CH * (u - 8 * g) + CH], Abd[:, u, :], Xc[:, u, :],
                                      start=True, stop=True)
                        last.then_inc(w_y.sem, 1)
                    for g in range(3):
                        us = range(8 * g, min(8 * g + 8, NU))
                        pe.wait_ge(*w_ye(l, 3 * m + g + 1))
                        for u in us:
                            last = mm(ps[:, 3 + g, CH * (u - 8 * g):CH * (u - 8 * g) + CH], Xbd[:, u, :],
                                      Yc[:, u, :], start=True, stop=True)
                        last.then_inc(w_p.sem, 1)
                    if m < len(LEVELS) - 1:
                        for q in range(5):
                            pe.wait_ge(*w_pe(l, 3 * m + q // 2 + 1))
                            for k in range(4):
                                u = 4 * q + k
                                last = pe.transpose(ps[0:CH, (6, 7, 0, 1, 2)[q], P * k:P * k + P], Xc[:, u, :],
                                                    C("ident", P))
                            last.then_inc(w_t.sem, 1)

            def rwkv_tokens(l):
                pe.wait_ge(*w_pe(l, 15))
                for c in range(NC):
                    for j in range(NP4):
                        last = pe.transpose(ps[:, c, P * j:P * j + P], BK[:, j, c, :], C("ident", P))
                    last.then_inc(w_bt.sem, 1)

            def head_cols(h):
                return slice(CH * h, CH * h + CH)

            def rwkv_chunk(l, c):
                sample = c == NC - 1
                if c == 0:
                    pe.wait_ge(*w_xt(l, 2))
                    pe.wait_ge(*w_bte(l, 5))
                    pe.wait_ge(*w_sz(l))
                if sample:
                    pe.wait_ge(ld_rw.sem, 16 * (l + 1))
                    for j in range(NP4):
                        for b in range(SB):
                            dst = ps[:, 6, :].rearrange("p (j q n) -> p j q n", j=8, q=2)[:, j, :, ST * b:ST * b + ST]
                            src = KR[:, j, c, :].rearrange("p (q n) -> p q n", q=2)[:, :, ST * b:ST * b + ST]
                            last = mm(dst, S0bd[:, b, j, :], src, start=True, stop=True)
                    last.then_inc(w_cx.sem, 1)
                for h in range(2 * NP4):
                    j, p = h // 2, h % 2
                    last = mm(ps[0:CH, 0, head_cols(h)], G[:, c, p, P * j:P * j + CH], UV[:, c, head_cols(h)],
                              start=(h == 0), stop=False, skip_group_check=True)
                if not sample:
                    if c > 0:
                        pe.wait_ge(*w_su(l, c))
                    for j in range(NP4):
                        last = mm(ps[0:CH, 0, P * j:P * j + P], KR[:, j, c, 0:CH], Sbd[:, j, :], start=False,
                                  stop=(j == NP4 - 1), skip_group_check=True)
                last.then_inc(w_r.sem, 1)
                obank = 4 + c % 2
                if c >= 2:
                    pe.wait_ge(*w_oe(l, c - 1))
                if sample:
                    pe.wait_ge(*w_cxe(l))
                    for j in range(NP4):
                        last = pe.transpose(ps[0:TS, 3, P * j:P * j + P], CX[:, j, 0, :], C("ident", P))
                    last.then_inc(w_ct.sem, 1)
                else:
                    for j in range(NP4):
                        last = mm(ps[:, obank, CH * j:CH * j + CH], Sbd[:, j, :], KR[:, j, c, CH:2 * CH],
                                  start=(j == 0), stop=False, skip_group_check=True)
                    last.then_inc(w_oc.sem, 1)
                pe.wait_ge(*w_rn(l, c + 1))
                for h in range(2 * NP4):
                    j, p = h // 2, h % 2
                    last = mm(ps[0:CH, 1, head_cols(h)], XT[0:CH, NP4 * c + j, CH * p:CH * p + CH],
                              Rn[0:CH, head_cols(h)], start=True, stop=True)
                last.then_inc(w_u.sem, 1)
                pe.wait_ge(*w_ue(l, c + 1))
                if not sample:
                    for j in range(NP4):
                        last = mm(ps[:, 2, P * j:P * j + P], BKt[:, c, P * j:P * j + P], UV[:, c, P * j:P * j + P],
                                  start=True, stop=True)
                    last.then_inc(w_s.sem, 1)
                for h in range(2 * NP4):
                    j, p = h // 2, h % 2
                    last = mm(ps[CH * p:CH * p + CH, obank, CH * j:CH * j + CH], UV[:, c, head_cols(h)],
                              G[:, c, p, P * j + CH:P * j + P], start=(sample and h < 2), stop=True,
                              skip_group_check=True)
                last.then_inc(w_ob.sem, 1)

            def rwkv_sample_state(l):
                for b in range(SB):
                    pe.wait_ge(*w_kb(l, b + 1))
                    if b >= 2:
                        pe.wait_ge(*w_sta(l, b - 1))
                    for j in range(NP4):
                        last = mm(ps[:, 1 + b % 2, P * j:P * j + P], KBm[b % 2][:, P * j:P * j + P],
                                  UV[:, NC - 1, P * j:P * j + P], start=True, stop=True)
                    last.then_inc(w_st.sem, 1)

            def closing(l):
                pe.wait_ge(*hn_y(l, 3))
                pe.wait_ge(*rw_y(l))
                pe.wait_ge(*w_sta(l, 8))
                with pe.Fori(0, KT // 2) as i:
                    inner = turns.loop(i, 5)
                    for n in range(3):
                        s = slab(inner)
                        for dd in range(2):
                            q = 2 * n + dd
                            pe.wait_ge(f_zs.sem, i * 6 + (24 * l + q + 1))
                            for k in range(KT):
                                w0 = 256 * k + P * dd
                                last = mm(ps[:, q % 3, 0:T], ring[:, s, w0:w0 + P], xn[:, k, :],
                                          start=(k == 0), stop=(k == KT - 1))
                            last.then_inc((slot_fr[s] if dd else f_zg).sem, 1)
                    for dd in range(2):
                        s = slab(inner)
                        for n, y in enumerate((y_ret, y_ml, y_rw)):
                            q = 3 * dd + n
                            pe.wait_ge(f_gm.sem, i * 6 + (24 * l + q + 1))
                            for k in range(4):
                                w0 = P * (4 * n + k)
                                last = mm(ps[:, 3 + q % 3, 0:T], ring[:, s, w0:w0 + P], y[:, k, :],
                                          start=(k == 0), stop=(k == 3))
                            last.then_inc((slot_fr[s] if n == 2 else f_br).sem, 1)
                turns.after(KT // 2, 5)
                pe.wait_ge(f_gm.sem, 3 + 24 * (l + 1))
                for d in range(KT):
                    if d % 2 == 0:
                        s = slab(turns)
                    if d >= 2:
                        pe.wait_ge(*x_mix(l, d - 1))
                    for k in range(KT):
                        w0 = 256 * k + P * (d % 2)
                        last = mm(ps[:, 6 + d % 2, 0:T], ring[:, s, w0:w0 + P], mixed[:, k, :],
                                  start=(k == 0), stop=(k == KT - 1))
                    last.then_inc((slot_fr[s] if d % 2 else f_out).sem, 1)

            def route(l):
                for i, (c0, m) in enumerate(TOK):
                    for k in range(KT):
                        last = mm(ps[0:m, 6, NE * i:NE * i + NE], xn[:, k, c0:c0 + m],
                                  lw[:, LW["router"] + NE * k:LW["router"] + NE * k + NE],
                                  start=(k == 0), stop=(k == KT - 1))
                last.then_inc(rt_lg.sem, 1)
                pe.wait_ge(rt_cb.sem, 1)
                for i, (c0, m) in enumerate(TOK):
                    last = pe.transpose(ps[0:NE, 7, c0:c0 + m], ex[0:m, i, :], C("ident", m, m))
                last.then_inc(rt_ct.sem, 1)
                pe.wait_ge(rt_cr.sem, 1)
                for e in range(NE):
                    if e >= 2:
                        pe.wait_ge(rt_bce.sem, e - 1)
                    mm(ps[:, 4 + e % 2, 0:T], con[0:NE, CON["sel"] + P * e:CON["sel"] + P * e + P], crow[0:NE, :],
                       start=True, stop=True).then_inc(rt_bc.sem, 1)
                pe.wait_ge(rt_bce.sem, NE)

            def feed_forward(l):
                with pe.Fori(0, PASSES[l]) as e:
                    inner = turns.loop(e, FT + KT, 1)
                    for f in range(FT):
                        s = slab(inner)
                        pe.wait_ge(h_done.sem, e * FT + (h_base(l) + f + (2 if f < 2 else 1)))
                        for w in range(2):
                            for k in range(KT):
                                w0 = P * (KT * w + k)
                                last = mm(ps[:, 2 * (f % 3) + w, 0:T], ring[:, s, w0:w0 + P], xn[:, k, :],
                                          start=(k == 0), stop=(k == KT - 1))
                            last.then_inc((slot_fr[s] if w else g_done).sem, 1)
                    for d in range(KT):
                        s = slab(inner)
                        pe.wait_ge(y_done.sem, e * KT + (y_base(l) + d + 1))
                        for f in range(FT):
                            if d == 0:
                                pe.wait_ge(h_done.sem, e * FT + (h_base(l) + CREDIT_H + f + 1))
                            last = mm(ps[:, 6 + d % 2, 0:T], ring[:, s, P * f:P * f + P], hid[:, f, :],
                                      start=(f == 0), stop=(f == FT - 1))
                        last.then_inc(slot_fr[s].sem, 1)
                turns.after(PASSES[l], FT + KT, 1)

            pe.wait_ge(ld_con.sem, 64)
            for l in range(DEPTH):
                norm(2 * l)
                groups(l, 0, 26)
                mlstm_columns(l)
                mlstm_qk(l)
                for h in range(NH):
                    mlstm_head(l, h)
                    groups(l, 26 + 4 * h, 30 + 4 * h)
                mlstm_state(l)
                groups(l, 42, NG)
                pe.wait_ge(*ml_sca(l, 8))
                pe.wait_ge(*ml_cpe(l))
                pe.wait_ge(*ml_out(l))
                head_norm(3 * l, ml_o, ml_sq, C("cent128", P), C("ones", P))
                pe.wait_ge(*hn_r(l, 1))
                retention_rotate(l)
                retention_keys(l)
                retention_scores(l, 0)
                for h in range(NH):
                    if h < NH - 1:
                        retention_scores(l, h + 1)
                    retention_values(l, h)
                retention_state(l)
                pe.wait_ge(*r_ssa(l, 8))
                pe.wait_ge(*r_spe(l))
                head_norm(3 * l + 1, ret_o, ret_sq, C("cent128", P), C("ones", P))
                rwkv_prepare(l)
                rwkv_gram(l)
                rwkv_invert(l)
                rwkv_tokens(l)
                for c in range(NC):
                    rwkv_chunk(l, c)
                rwkv_sample_state(l)
                pe.wait_ge(*w_oe(l, 5))
                head_norm(3 * l + 2, rw_o, rw_sq, C("cent64", P), C("ones64", P))
                closing(l)
                norm(2 * l + 1)
                if l == 1:
                    route(l)
                feed_forward(l)
            norm(2 * DEPTH)

        @block.scalar
        def _(act):
            turns = Turns()
            A = act.activation
            links = [0]

            def link(ins):
                links[0] += 1
                ins.then_inc(ach.sem, 1)
                act.wait_ge(ach.sem, links[0])

            def norm(n):
                if n == 0:
                    act.wait_ge(ld_x.sem, 16)
                elif n % 2 == 1:
                    act.wait_ge(*x_mix(n // 2, 8))
                    act.wait_ge(st_rw.sem, 32 * (n // 2 + 1))
                else:
                    act.wait_ge(y_done.sem, CREDIT_Y + KT * (NDENSE if n == 2 else NDENSE + NE))
                A(norm_sq, X[:, :, :], ACT.Square).then_inc(nm_sq.sem, 1)
                act.wait_ge(*nm_rec(n))
                A(rstd[:, :], rstd[:, :], ACT.Sqrt).then_inc(nm_rstd.sem, 1)

            current = [None, 0, 0]

            def projections(l, first, end):
                for n in range(first, end):
                    kind, j = GROUPS[n]
                    piece, part, is_last = piece_of(kind, j)
                    if piece is not None and current[0] != (l, kind, piece):
                        current[0] = (l, kind, piece)
                        current[1:] = turns.take()
                    if is_last:
                        act.wait_ge(slot_fr[current[1]].sem, current[2] + 1)
                    else:
                        act.wait_ge(*proj(l, sum(not piece_of(*g)[2] for g in GROUPS[:n + 1])))
                    src = ps[:, n % 4, 0:T]
                    if kind == "mx":
                        A(mxp[:, j, XPAD:XPAD + TP], src[:, 0:TP], ACT.Copy)
                        dst = mxp[:, j, XPAD + TP:].rearrange("p (b t) -> p b t", b=SB)[:, :, XPAD:]
                        last = A(dst, seq4(src[:, TP:T]), ACT.Copy)
                    elif kind == "zrw":
                        A(z[:, j, 1:1 + TP], src[:, 0:TP], ACT.Copy)
                        dst = z[:, j, 1 + TP:].rearrange("p (b t) -> p b t", b=SB)[:, :, 1:]
                        last = A(dst, seq4(src[:, TP:T]), ACT.Copy)
                    elif kind in ("mi", "mf"):
                        w = 0 if kind == "mi" else 1
                        last = A(rows[0:NH, w, :], src[0:NH, :], ACT.Identity, bias=gate_bias[:, l, w:w + 1])
                    elif kind in ("mv", "rv"):
                        m = TOK[part][1]
                        dst = (mvt if kind == "mv" else rvt)[0:m, part, 256 * piece:256 * piece + 256]
                        last = A(dst, ps[0:m, n % 4, 0:256], ACT.Copy)
                    elif kind in ("rq", "rk"):
                        last = A(rqk[:, j + (2 if kind == "rk" else 0), :], src, ACT.Copy,
                                 scale=1.0 if kind == "rq" else DK ** -0.5)
                    elif kind == "mo":
                        last = A(y_ml[:, j, :], src, ACT.Sigmoid)
                    else:
                        last = A(y_ret[:, j, :], src, ACT.Silu)
                    last.then_inc(evac.sem, 1)

            def head_norm(q, src, sq):
                for j in range(4):
                    act.wait_ge(hn_x.sem, 4 * q + j + 1)
                    A(sq[:, j, :], src[:, j, :], ACT.Square).then_inc(hn_s.sem, 1)
                act.wait_ge(*hn_r(0, q + 1))
                A(sq, sq, ACT.Sqrt).then_inc(hn_q.sem, 1)

            def mlstm_gates(l):
                act.wait_ge(*u_abs(l))
                link(A(rows[0:NH, 2, :], rows[0:NH, 2, :], ACT.Exp, scale=-1.0))
                A(rows[0:NH, 2, :], rows[0:NH, 2, :], ACT.Ln, bias=1.0).then_inc(u_exp.sem, 1)
                act.wait_ge(*lf_ok(l))
                A(rows[0:NH, 3, :], rows[0:NH, 3, :], ACT.Exp)
                A(arow[0:NH, :], arow[0:NH, :], ACT.Exp).then_inc(gr_ok.sem, 1)
                A(rows[0:NH, 2, :], rows[0:NH, 2, :], ACT.Exp, scale=-1.0).then_inc(er_ok.sem, 1)

            def mlstm_qk(l):
                for n in range(11):
                    act.wait_ge(*mqk_p(l, n + 1))
                    if n < 8:
                        h = n // 2
                        last = A((mq, mk)[n % 2][:, h, :], ps[:, 5 + n % 2, 0:T], ACT.Copy,
                                 scale=(1.0, P ** -0.5)[n % 2])
                    else:
                        m = TOK[n - 8][1]
                        last = A(mkt[0:m, n - 8, :], ps[0:m, 5 + n % 2, :], ACT.Copy, scale=P ** -0.5)
                    last.then_inc(mqk_e.sem, 1)

            def mlstm_head(l, h):
                act.wait_ge(*ml_wl(l, h + 1))
                A(ml_W[:, 0:TP + P], ml_W[:, 0:TP + P], ACT.Exp)
                A(ml_W[0:TS, TP + P:PW], ml_W[0:TS, TP + P:PW], ACT.Exp).then_inc(ml_ex.sem, 1)
                act.wait_ge(*ml_nd(l, h + 1))
                A(ml_den, ps[:, 4, 0:T], ACT.Abs).then_inc(ml_ad.sem, 1)

            def mlstm_state(l):
                act.wait_ge(*ml_cp(l))
                if l > 0:
                    act.wait_ge(st_ml.sem, 64 * l)
                A(Cp, ps[:, 4, :], ACT.Copy)
                A(n_out[:, 0:NH], ps[:, 5, 0:NH], ACT.Copy).then_inc(ml_cpe.sem, 1)

            def retention(l):
                for h in range(NH):
                    act.wait_ge(*r_o(l, h + 1))
                    A(ret_o[:, h, :], ps[:, 6 + h % 2, 0:T], ACT.Copy).then_inc(r_oe.sem, 1)
                act.wait_ge(*r_sp(l))
                A(Sp_ret, ps[:, 4, 0:256], ACT.Copy).then_inc(r_spe.sem, 1)

            def rwkv_prepare(l):
                act.wait_ge(*w_zs(l))
                A(lora_in[0:DK, :], zs[0:DK, 12, :], ACT.Tanh)
                A(lora_in[DK:P, :], zs[DK:P, 12, :], ACT.Copy)
                A(lora_g, zs[:, 13, :], ACT.Sigmoid).then_inc(w_thl.sem, 1)
                act.wait_ge(st_ret.sem, 32 * (l + 1))
                for n in range(12):
                    which, j = n // 4, n % 4
                    act.wait_ge(*w_lora(l, n + 1))
                    src = ps[:, 4 + n % 2, 0:T]
                    if which == 2:
                        last = A(rw_g[:, j, :], src, ACT.Copy)
                    else:
                        last = A((rw_lw, rw_a)[which][:, j, :], src, ACT.Sigmoid,
                                 bias=V(l, ("w0", "a0")[which], j))
                    last.then_inc(w_lorae.sem, 1)
                act.wait_ge(*w_ssr(l))
                A(rw_e1, rw_e1, ACT.Sqrt).then_inc(w_ssq.sem, 1)
                act.wait_ge(*w_F(l))
                A(rw_e2, rw_e2, ACT.Exp)
                A(rw_lw, rw_e1, ACT.Exp, scale=-1.0)
                A(rw_e1, rw_e1, ACT.Exp).then_inc(w_E.sem, 1)
                for c in range(NC):
                    act.wait_ge(*w_vt(l, c + 1))
                    if c == 0:
                        act.wait_ge(*w_zuv(l, 4))
                    w = CH if c < NC - 1 else TS
                    A(UV[CH:CH + w, c, :], ps[0:w, c % 4, :], ACT.Copy).then_inc(w_vte.sem, 1)

            def rwkv_invert(l):
                for m in range(len(LEVELS)):
                    for g in range(3):
                        n = min(8, NU - 8 * g)
                        act.wait_ge(*w_y(l, 3 * m + g + 1))
                        A(Yc[:, 8 * g:8 * g + n, :], ps[:, g, 0:CH * n].rearrange("p (a b) -> p a b", a=n),
                          ACT.Copy).then_inc(w_ye.sem, 1)
                    if m < len(LEVELS) - 1:
                        for q in (0, 2, 4):
                            act.wait_ge(*w_t(l, 5 * m + q + 1))
                            src = ps[0:CH, (6, 7, 0, 1, 2)[q], :].rearrange("p (a b) -> p a b", a=4)
                            A(Xbd[0:CH, 4 * q:4 * q + 4, 0:CH], src[:, :, 0:CH], ACT.Copy)
                            A(Xbd[CH:P, 4 * q:4 * q + 4, CH:P], src[:, :, CH:P], ACT.Copy).then_inc(w_te.sem, 1)
                act.wait_ge(*w_pe(l, 15))
                A(XT[0:CH, :, 0:CH], Xc[0:CH, :, :], ACT.Copy).then_inc(w_xt.sem, 1)
                for c in range(NC):
                    act.wait_ge(*w_bt(l, c + 1))
                    A(BKt[:, c, :], ps[:, c, :], ACT.Copy).then_inc(w_bte.sem, 1)

            def rwkv_chunks(l):
                for c in range(NC):
                    if c == NC - 1:
                        act.wait_ge(*w_cx(l))
                        A(CX, ps[:, 6, 0:256].rearrange("p (j q n) -> p j q n", j=4, q=2), ACT.Copy)\
                            .then_inc(w_cxe.sem, 1)
                    act.wait_ge(*w_u(l, c + 1))
                    A(UV[0:CH, c, :], ps[0:CH, 1, :], ACT.Copy).then_inc(w_ue.sem, 1)
                    if c < NC - 1:
                        act.wait_ge(*w_ob(l, c + 1))
                        A(rw_o[:, :, CH * c:CH * c + CH],
                          ps[:, 4 + c % 2, 0:256].rearrange("p (a b) -> p a b", a=4), ACT.Copy).then_inc(w_oe.sem, 1)

            def closing(l):
                with act.Fori(0, KT // 2) as i:
                    inner = turns.loop(i, 5)
                    for n in range(3):
                        s, used = inner.take()
                        for dd in range(2):
                            q = 2 * n + dd
                            if dd:
                                act.wait_ge(slot_fr[s].sem, used + 1)
                            else:
                                act.wait_ge(f_zg.sem, i * 3 + (12 * l + n + 1))
                            act.wait_ge(f_mul.sem, i * 6 + (24 * l + 3 * dd + n + 1))
                            A(gates[:, q, :], ps[:, q % 3, 0:T], ACT.Sigmoid).then_inc(f_zs.sem, 1)
                turns.after(KT // 2, 5)
                turns.pass_over(len(OUTS))

            def feed_forward(l):
                with act.Fori(0, PASSES[l]) as e:
                    for f in range(FT):
                        act.wait_ge(g_done.sem, e * FT + (h_base(l) + f + 1))
                        A(sil[:, f % 3, :], ps[:, 2 * (f % 3), 0:T], ACT.Silu).then_inc(s_done.sem, 1)
                turns.after(PASSES[l], FT + KT, 1)

            act.wait_ge(ld_con.sem, 64)
            for _ in range(3):
                act.sem_inc(f_zs.sem, 1)
            for l in range(DEPTH):
                norm(2 * l)
                projections(l, 0, 16)
                act.wait_ge(*conv_acc(l))
                A(xc, xc, ACT.Silu).then_inc(xc_ok.sem, 1)
                projections(l, 16, 20)
                mlstm_gates(l)
                projections(l, 20, 26)
                mlstm_qk(l)
                for h in range(NH):
                    mlstm_head(l, h)
                    projections(l, 26 + 4 * h, 30 + 4 * h)
                mlstm_state(l)
                projections(l, 42, NG)
                head_norm(3 * l, ml_o, ml_sq)
                retention(l)
                head_norm(3 * l + 1, ret_o, ret_sq)
                rwkv_prepare(l)
                rwkv_invert(l)
                rwkv_chunks(l)
                head_norm(3 * l + 2, rw_o, rw_sq)
                closing(l)
                norm(2 * l + 1)
                if l == 1:
                    act.wait_ge(rt_e.sem, 1)
                    A(ex, ex, ACT.Exp).then_inc(rt_ex.sem, 1)
                    for e in range(NE):
                        act.wait_ge(rt_bc.sem, e + 1)
                        A(comb[:, e, :], ps[:, 4 + e % 2, 0:T], ACT.Copy).then_inc(rt_bce.sem, 1)
                feed_forward(l)
            norm(2 * DEPTH)

        @block.vector
        def _(dve):
            turns = Turns()
            links = [0]
            TT, TSC, STT = dve.tensor_tensor, dve.tensor_scalar, dve.scalar_tensor_tensor
            MUL, ADD, SUB, MAX, MIN = ALU.mult, ALU.add, ALU.subtract, ALU.max, ALU.min

            def link(ins):
                links[0] += 1
                ins.then_inc(dch.sem, 1)
                dve.wait_ge(dch.sem, links[0])

            def mid(ap, n):
                return ap.unsqueeze(1).broadcast_to([ap.shape[0], n, ap.shape[1]])

            def end(ap, n):
                return ap.unsqueeze(len(ap.shape)).broadcast_to(list(ap.shape) + [n])

            def norm(n):
                l = min(n // 2, DEPTH - 1)
                gain = "final" if n == 2 * DEPTH else ("norm_mix", "norm_ffn")[n % 2]
                dve.wait_ge(*nm_ms(n))
                link(TSC(rstd[:, :], ps[:, 4, 0:T], 1.0 / D, NORM_EPS, MUL, ADD))
                dve.reciprocal(rstd[:, :], rstd[:, :]).then_inc(nm_rec.sem, 1)
                dve.wait_ge(*nm_rstd(n))
                for k in range(KT):
                    last = STT(xn[:, k, :], X[:, k, :], V(l, gain, k), rstd[:, :], MUL, MUL)
                last.then_inc(nm_xn.sem, 1)

            def head_norm(q, src, sq, n, eps, finish):
                for j in range(4):
                    dve.wait_ge(hn_c.sem, 4 * q + j + 1)
                    dve.tensor_copy(src[:, j, :], ps[:, 4 + j, 0:T]).then_inc(hn_x.sem, 1)
                for j in range(4):
                    dve.wait_ge(hn_v.sem, 4 * q + j + 1)
                    last = TSC(sq[:, j, :], ps[:, 4 + j, 0:T], 1.0 / n, eps, MUL, ADD)
                link(last)
                dve.reciprocal(sq, sq).then_inc(hn_r.sem, 1)
                dve.wait_ge(*hn_q(0, q + 1))
                finish()

            def histories(l):
                dve.wait_ge(ld_hist.sem, 32 * (l + 1))
                dve.memset(mxp[:, :, 0:XPAD], 0.0)
                dve.memset(z[:, :, 0:1], 0.0)
                for j in range(4):
                    dst = mxp[:, j, XPAD + TP:].rearrange("p (b t) -> p b t", b=SB)[:, :, 0:XPAD]
                    src = hist[:, j * SB * XPAD:(j + 1) * SB * XPAD].rearrange("p (b t) -> p b t", b=SB)
                    dve.tensor_copy(dst, src)
                zc = z[:, :, 1 + TP:].rearrange("p j (b t) -> p j b t", b=SB)[:, :, :, 0]
                link(dve.tensor_copy(zc, prev[:, :].rearrange("p (j b) -> p j b", b=SB)))

            def conv(l):
                for j in range(4):
                    dve.wait_ge(*evac(l, j + 1))
                    smp = mxp[:, j, XPAD + TP:].rearrange("p (b t) -> p b t", b=SB)
                    for k in range(CONV):
                        w = V(l, "conv_w", 4 * k + j)
                        accp, accs = xc[:, j, 0:TP], seq4(xc[:, j, TP:T])
                        inp, ins = mxp[:, j, k:k + TP], smp[:, :, k:k + ST]
                        if k == 0:
                            TSC(accp, inp, w, V(l, "conv_b", j), MUL, ADD)
                            last = TSC(accs, ins, w, V(l, "conv_b", j), MUL, ADD)
                        else:
                            STT(accp, inp, w, accp, MUL, ADD)
                            last = STT(accs, ins, w, accs, MUL, ADD)
                        if k < CONV - 1:
                            link(last)
                last.then_inc(conv_acc.sem, 1)
                if l > 0:
                    dve.wait_ge(st_small.sem, 32 * l)
                dve.tensor_copy(conv_out[:, :, 0:XPAD], mxp[:, :, TP:TP + XPAD])
                src = mxp[:, :, XPAD + TP:].rearrange("p j (b t) -> p j b t", b=SB)[:, :, :, ST:]
                link(dve.tensor_copy(conv_out[:, :, XPAD:].rearrange("p j (b t) -> p j b t", b=SB), src))
                conv_out_ok(l)

            def conv_out_ok(l):
                dve.sem_inc(co_ok.sem, 1)

            def mlstm_gates(l):
                R = [rows[0:NH, k, :] for k in range(4)]
                cum = gate_rows[0:NH, 0, :]
                dve.wait_ge(*evac(l, 6))
                link(TSC(R[2], R[1], -1.0, None, MUL))
                link(TT(R[2], R[2], R[1], MAX))
                TSC(R[1], R[1], 0.0, None, MIN).then_inc(u_abs.sem, 1)
                dve.wait_ge(*u_exp(l))
                link(TT(R[1], R[1], R[2], SUB))
                link(dve.tensor_tensor_scan(R[3], C("reset_mul", T, NH), R[1], 0.0, MUL, ADD))
                link(TT(R[0], R[0], R[3], SUB))
                link(dve.tensor_tensor_scan(cum, C("reset_add", T, NH), R[0], 0.0, ADD, MAX))
                TSC(cum[:, 0:TP], cum[:, 0:TP], 0.0, None, MAX)
                m0b = end(m0[:, l, :], ST)
                link(TT(seq4(cum[:, TP:T]), seq4(cum[:, TP:T]), m0b, MAX))
                TSC(R[1], cum, -1.0, None, MUL)
                TT(R[2], R[3], cum, ADD)
                link(TT(seq4(arow[0:NH, :]), m0b, seq4(cum[:, TP:T]), SUB))
                if l > 0:
                    dve.wait_ge(st_ml.sem, 64 * l)
                dve.tensor_copy(m_out[:, 0:1], R[2][:, TP - 1:TP])
                dve.tensor_copy(m_out[:, 1:1 + SB], seq4(R[2][:, TP:T])[:, :, ST - 1])
                TSC(R[3][:, 0:TP], R[0][:, 0:TP], cum[:, TP - 1:TP], None, SUB)
                lastM = seq4(cum[:, TP:T])[:, :, ST - 1:ST].broadcast_to([NH, SB, ST])
                TT(seq4(R[3][:, TP:T]), seq4(R[0][:, TP:T]), lastM, SUB).then_inc(lf_ok.sem, 1)
                dve.wait_ge(*ml_col(l))
                dve.tensor_copy(gwc[:, 0:16], ps[:, 4, 0:16])
                link(dve.tensor_copy(gwc[0:TS, 16:24], ps[0:TS, 4, 16:24]))
                dve.sem_inc(ml_colv.sem, 1)

            def mlstm_keys(l):
                dve.wait_ge(*mqk_e(l, 11))
                for i, (_, m) in enumerate(TOK):
                    v = mkt[0:m, i, :].rearrange("p (h e) -> p h e", h=NH)
                    last = TT(v, v, end(gwc[0:m, 8 * i + 4:8 * i + 8], P), MUL)
                last.then_inc(kdec_ok.sem, 1)

            def mlstm_head(l, h):
                dve.wait_ge(*ml_bc(l, h + 1))
                dve.tensor_copy(aL[:, :, h], seq4(ps[:, 4, T:T + TS])[:, :, ST - 1])
                link(TT(qa, mq[:, h, TP:T], ps[:, 4, T:T + TS], MUL))
                if h == 0:
                    dve.wait_ge(ld_n0.sem, 16 * (l + 1))
                n0v = end(n0.rearrange("p (b h) -> p b h", b=SB)[:, :, h], ST)
                TT(seq4(nq), seq4(qa), n0v, MUL)
                g = [gwc[:, 8 * i + h:8 * i + h + 1] for i in range(3)]
                STT(ml_W[:, 0:P], ps[:, 4, 0:P], g[0], C("causal_neg", P), ADD, ADD)
                TSC(ml_W[:, P:TP], ps[:, 4, P:TP], g[0], None, ADD)
                STT(ml_W[:, TP:TP + P], ps[:, 4, P:TP], g[1], C("causal_neg", P), ADD, ADD)
                STT(ml_W[0:TS, TP + P:PW], ps[0:TS, 4, TP:T], g[2][0:TS, :], C("sample_neg", TS, TS), ADD, ADD)\
                    .then_inc(ml_wl.sem, 1)
                dve.wait_ge(*ml_ex(l, h + 1))
                dve.wait_ge(*ml_s(l, h + 1))
                TT(ml_PW[:, 0:TP + P], ps[:, 6, 0:TP + P], ml_W[:, 0:TP + P], MUL)
                TT(ml_PW[0:TS, TP + P:PW], ps[0:TS, 6, TP + P:PW], ml_W[0:TS, TP + P:PW], MUL)\
                    .then_inc(ml_pw.sem, 1)
                dve.wait_ge(*ml_ad(l, h + 1))
                link(TT(ml_den, ml_den, ps[:, 5, 0:T], MAX))
                link(dve.reciprocal(ml_den, ml_den))
                TT(ml_o[:, h, :], ps[:, 7, 0:T], ml_den, MUL).then_inc(ml_h.sem, 1)

            def mlstm_state(l):
                dve.wait_ge(*ml_cpe(l))
                for b in range(SB):
                    if b >= 2:
                        dve.wait_ge(*ml_sc(l, b - 1))
                    TSC(kb[0:TS, b % 2, :], mkt[0:TS, 2, :], C("bmask", 1, TS, b), None, MUL).then_inc(ml_kb.sem, 1)
                    if b > 0:
                        update(l, b - 1)
                update(l, SB - 1)
                link(TT(n_out[:, NH:], n0, aL.rearrange("p b h -> p (b h)"), MUL))
                TT(n_out[:, NH:], n_out[:, NH:], ps[:, 5, 8:8 + SB * NH], ADD).then_inc(ml_out.sem, 1)

            def update(l, b):
                link(TT(C0[:, b, :, :], C0[:, b, :, :], end(aL[:, b, :], P), MUL))
                dve.wait_ge(*ml_sc(l, b + 1))
                v = ps[:, 6 + b % 2, :].rearrange("p (h e) -> p h e", h=NH)
                TT(C0[:, b, :, :], C0[:, b, :, :], v, ADD).then_inc(ml_sca.sem, 1)

            def mlstm_finish(l):
                for j in range(4):
                    last = STT(ml_o[:, j, :], ml_o[:, j, :], V(l, "ml_gn", j), ml_sq[:, j, :], MUL, MUL)
                link(last)
                for j in range(4):
                    last = STT(ml_o[:, j, :], xc[:, j, :], V(l, "ml_skip", j), ml_o[:, j, :], MUL, ADD)
                link(last)
                dve.wait_ge(*evac(l, 40))
                TT(y_ml[:, :, :], ml_o, y_ml[:, :, :], MUL).then_inc(hn_y.sem, 1)

            def retention(l):
                TT(qr, rqk, mid(C("cos", T), 4), MUL)
                for j in range(4):
                    dve.wait_ge(*r_sw(l, j + 1))
                    last = TT(rt[:, j, :], ps[:, 4 + j, 0:T], C("sin", T), MUL)
                link(last)
                link(TT(qr, qr, rt, ADD))
                for i in range(2):
                    last = TT(qd[:, i, :], qr[:, i, TP:T], C("qdec", TS, P, TS * i), MUL)
                last.then_inc(r_qr.sem, 1)
                for i, (_, m) in enumerate(TOK):
                    dve.wait_ge(*r_kt(l, i + 1))
                    src = ps[0:m, 4 + i, 0:256].rearrange("p (h e) -> p h e", h=NH)
                    dst = ktd[0:m, i, :].rearrange("p (h e) -> p h e", h=NH)
                    TT(dst, src, end(C("kdec", NH, m, NH * i), DK), MUL).then_inc(r_ktd.sem, 1)
                dve.wait_ge(ld_ret.sem, 32 * (l + 1))
                for h in range(NH):
                    if h >= 2:
                        dve.wait_ge(*r_o(l, h - 1))
                    dve.wait_ge(*r_sc(l, h + 1))
                    TT(rpw[:, h % 2, 0:TP + P], ps[:, 4 + h % 2, 0:TP + P], dec[:, h, 0:TP + P], MUL)
                    TT(rpw[0:TS, h % 2, TP + P:PW], ps[0:TS, 4 + h % 2, TP + P:PW], dec[0:TS, h, TP + P:PW], MUL)\
                        .then_inc(r_pw.sem, 1)
                for b in range(SB):
                    if b >= 2:
                        dve.wait_ge(*r_ss(l, b - 1))
                    TSC(rkb[0:TS, b % 2, :], ktd[0:TS, 2, :], C("bmask", 1, TS, b), None, MUL).then_inc(r_kb.sem, 1)
                    if b > 0:
                        retention_update(l, b - 1)
                retention_update(l, SB - 1)

            def retention_update(l, b):
                dve.wait_ge(*r_ss(l, b + 1))
                for i in range(2):
                    last = STT(S0_ret[:, b, i, :], S0_ret[:, b, i, :], C("g4", 1, P, i),
                               ps[:, 5 + b % 2, P * i:P * i + P], MUL, ADD)
                last.then_inc(r_ssa.sem, 1)

            def retention_finish(l):
                for j in range(4):
                    last = STT(ret_o[:, j, :], ret_o[:, j, :], V(l, "ret_gn", j), ret_sq[:, j, :], MUL, MUL)
                link(last)
                dve.wait_ge(*evac(l, 44))
                TT(y_ret[:, :, :], ret_o, y_ret[:, :, :], MUL).then_inc(hn_y.sem, 1)

            def rwkv_prepare(l):
                dve.wait_ge(st_ml.sem, 64 * (l + 1))
                dve.tensor_copy(shift_out[:, :, 0:1], z[:, :, TP:TP + 1])
                zq = z[:, :, 1 + TP:].rearrange("p j (b t) -> p j b t", b=SB)
                link(dve.tensor_copy(shift_out[:, :, 1:], zq[:, :, :, ST]))
                dve.sem_inc(so_ok.sem, 1)
                link(TT(zs[:, :, 0:TP], z[:, :, 0:TP], z[:, :, 1:1 + TP], SUB))
                for j in range(ZT):
                    b = zq[:, j]
                    d = seq4(zs[:, j, TP:T])
                    TT(d, b[:, :, 0:ST], b[:, :, 1:], SUB)
                    last = STT(zs[:, j, 0:TP], zs[:, j, 0:TP], V(l, "mu", j), z[:, j, 1:1 + TP], MUL, ADD)
                link(last)
                for j in range(ZT):
                    d = seq4(zs[:, j, TP:T])
                    last = STT(d, d, V(l, "mu", j), zq[:, j][:, :, 1:], MUL, ADD)
                last.then_inc(w_zs.sem, 1)
                dve.wait_ge(*w_zs(l))
                for j in range(4):
                    last = TSC(rw_kk[:, j, :], zs[:, 4 + j, :], V(l, "kk", j), None, MUL)
                link(last)
                TT(rw_e1, rw_kk, rw_kk, MUL).then_inc(w_sq.sem, 1)
                dve.wait_ge(*w_lorae(l, 12))
                for j in range(4):
                    last = TSC(rw_e2[:, j, :], rw_a[:, j, :], -1.0, V(l, "ka", j), ADD, MUL)
                link(last)
                link(STT(rw_kp, rw_e2, 1.0, zs[:, 4:8, :], ADD, MUL))
                for j in range(4):
                    last = STT(rw_e2[:, j, :], zs[:, j, :], V(l, "rk", j), rw_kp[:, j, :], MUL, MUL)
                for j in range(4):
                    dve.wait_ge(*w_ss(l, j + 1))
                    last = TSC(rw_e1[:, j, :], ps[:, 4 + j, 0:T], 1e-24, None, MAX)
                last.then_inc(w_rk.sem, 1)
                dve.wait_ge(*w_rk(l))
                dve.reciprocal(rw_e1, rw_e1).then_inc(w_ssr.sem, 1)
                dve.wait_ge(*w_ssq(l))
                link(TT(rw_kk, rw_kk, rw_e1, MUL))
                dve.wait_ge(st_ret.sem, 32 * (l + 1))
                for j in range(4):
                    dve.wait_ge(*w_bo(l, j + 1))
                    TT(rw_bv[:, j, :], ps[:, 4 + j, 0:T], zs[:, 8 + j, :], MUL)
                link(TSC(rw_lw, rw_lw, -RW_DECAY, None, MUL))
                for j in range(4):
                    last = dve.tensor_tensor_scan(rw_e1[:, j, :], C("reset64", T), rw_lw[:, j, :], 0.0, MUL, ADD)
                link(last)
                TT(rw_e2, rw_e1, rw_lw, SUB).then_inc(w_F.sem, 1)
                dve.wait_ge(*w_F(l))
                dve.wait_ge(*w_zuv(l, 4))
                link(TT(rw_a, rw_a, rw_kk, MUL))
                dve.wait_ge(*w_E(l))

                def blocks(dst, q, x, y):
                    for j in range(NP4):
                        out = dst[:, j, 0:NC - 1, CH * q:CH * q + CH]
                        TT(out, x[:, j, 0:TP].rearrange("p (c s) -> p c s", c=NC - 1),
                           y[:, j, 0:TP].rearrange("p (c s) -> p c s", c=NC - 1), MUL)
                    return TT(dst[:, :, NC - 1, CH * q:CH * q + TS], x[:, :, TP:T], y[:, :, TP:T], MUL)

                blocks(KR, 0, rw_kk, rw_e2)
                blocks(KR, 1, zs[:, 0:4, :], rw_e1)
                blocks(BK, 0, rw_a, rw_lw)
                blocks(BK, 1, rw_kp, rw_lw)
                dve.tensor_copy(PL[:, :, 0:4], rw_e1[:, :, CH - 1:TP:CH])
                link(dve.tensor_copy(PL[:, :, 4:], rw_e1[:, :, TP + ST - 1:T:ST]))
                dve.sem_inc(w_pre.sem, 1)

            def rwkv_gram(l):
                for c in range(NC):
                    mask = C("gram_p" if c < NC - 1 else "gram_s", P)
                    for p in range(2):
                        n = 2 * c + p
                        dve.wait_ge(*w_g1(l, n + 1))
                        TT(G[:, c, p, :].rearrange("p (j e) -> p j e", j=4),
                           ps[:, n % 4, :].rearrange("p (j e) -> p j e", j=4), mid(mask, 4), MUL)\
                            .then_inc(w_g1e.sem, 1)
                dve.wait_ge(*w_zab(l, 2))
                for n in range(6):
                    p, c0 = n % 2, 2 * (n // 2)
                    r = slice(CH * p, CH * p + CH)
                    dve.wait_ge(*w_g2(l, n + 1))
                    for c in range(c0, min(c0 + 2, NC)):
                        src = ps[r, 4 + n % 4, 256 * (c - c0):256 * (c - c0) + 256].rearrange("p (j e) -> p j e", j=4)
                        mask = con[r, CON["a_p" if c < NC - 1 else "a_s"]:][:, 0:CH]
                        last = TT(Abd[r, 4 * c:4 * c + 4, CH * p:CH * p + CH], src, mid(mask, 4), MUL)
                    last.then_inc(w_g2e.sem, 1)
                dve.wait_ge(*w_g2e(l, 6))
                for p in range(2):
                    r = slice(CH * p, CH * p + CH)
                    m0_, m0t = con[0:CH, CON["join0"]:][:, 0:CH], con[r, CON["join0t"]:][:, 0:CH]
                    for c in range(NC):
                        TT(Xc[r, 4 * c:4 * c + 4, :],
                           G[0:CH, c, p, :].rearrange("p (j e) -> p j e", j=4)[:, :, 0:CH], mid(m0_, 4), MUL)
                    dg = slice(CH * p, CH * p + CH)
                    link(TT(Xbd[r, :, dg], Abd[r, :, dg], mid(m0t, NU), MUL))
                    eye = con[r, CON["ident64"]:][:, 0:CH]
                    TT(Xc[r, :, :], Xc[r, :, :], mid(eye, NU), ADD)
                    last = TT(Xbd[r, :, dg], Xbd[r, :, dg], mid(eye, NU), ADD)
                last.then_inc(w_x0.sem, 1)
                dve.wait_ge(*w_x0(l))

            def rwkv_invert(l):
                for m in range(len(LEVELS)):
                    for g in range(3):
                        n = min(8, NU - 8 * g)
                        us = slice(8 * g, 8 * g + n)
                        dve.wait_ge(*w_p(l, 3 * m + g + 1))
                        src = ps[:, 3 + g, 0:CH * n].rearrange("p (a b) -> p a b", a=n)
                        link(TT(Yc[:, us, :], src, mid(C("joins", CH, P, CH * m), n), MUL))
                        TT(Xc[:, us, :], Xc[:, us, :], Yc[:, us, :], ADD).then_inc(w_pe.sem, 1)
                    if m < len(LEVELS) - 1:
                        for q in (1, 3):
                            dve.wait_ge(*w_t(l, 5 * m + q + 1))
                            src = ps[0:CH, (6, 7, 0, 1, 2)[q], :].rearrange("p (a b) -> p a b", a=4)
                            dve.tensor_copy(Xbd[0:CH, 4 * q:4 * q + 4, 0:CH], src[:, :, 0:CH])
                            dve.tensor_copy(Xbd[CH:P, 4 * q:4 * q + 4, CH:P], src[:, :, CH:P]).then_inc(w_to.sem, 1)
                dve.wait_ge(*w_pe(l, 15))
                dve.tensor_copy(XT[0:CH, :, CH:P], Xc[CH:P, :, :]).then_inc(w_xt.sem, 1)
                dve.memset(Sbd, 0.0).then_inc(w_sz.sem, 1)
                dve.wait_ge(*w_sz(l))

            def rwkv_chunks(l):
                for c in range(NC):
                    dve.wait_ge(*w_r(l, c + 1))
                    if c == NC - 1:
                        link(TSC(Rn[0:CH, :], ps[0:CH, 0, :], -1.0, None, MUL))
                        dve.wait_ge(*w_ct(l))
                        TT(Rn[0:TS, :], Rn[0:TS, :], ps[0:TS, 3, :], SUB).then_inc(w_rn.sem, 1)
                        dve.wait_ge(*w_ob(l, c + 1))
                        dve.wait_ge(*w_cxe(l))
                        src = ps[:, 4 + c % 2, 0:256].rearrange("p (a b) -> p a b", a=4)[:, :, 0:TS]
                        TT(rw_o[:, :, TP:T], src, CX[:, :, 1, :], ADD).then_inc(w_oe.sem, 1)
                        continue
                    TSC(Rn[0:CH, :], ps[0:CH, 0, :], -1.0, None, MUL).then_inc(w_rn.sem, 1)
                    dve.wait_ge(*w_s(l, c + 1))
                    for p in range(2):
                        r, dg = slice(CH * p, CH * p + CH), slice(CH * p, CH * p + CH)
                        src = ps[r, 2, :].rearrange("p (j e) -> p j e", j=4)[:, :, dg]
                        last = TT(Sbd[r, :, dg], Sbd[r, :, dg], src, ADD)
                    link(last)
                    for p in range(2):
                        r, dg = slice(CH * p, CH * p + CH), slice(CH * p, CH * p + CH)
                        last = TT(Sbd[r, :, dg], Sbd[r, :, dg], end(PL[r, :, c], CH), MUL)
                    last.then_inc(w_su.sem, 1)
                for b in range(SB):
                    if b >= 2:
                        dve.wait_ge(*w_st(l, b - 1))
                    TSC(KBm[b % 2], BKt[:, NC - 1, :], C("bmask2", 1, P, b), None, MUL).then_inc(w_kb.sem, 1)
                    if b > 0:
                        rwkv_update(l, b - 1)
                rwkv_update(l, SB - 1)

            def rwkv_update(l, b):
                dve.wait_ge(*w_st(l, b + 1))
                src = ps[:, 1 + b % 2, :].rearrange("p (j e) -> p j e", j=4)
                link(TT(S0bd[:, b, :, :], S0bd[:, b, :, :], src, ADD))
                TT(S0bd[:, b, :, :], S0bd[:, b, :, :], end(PL[:, :, 4 + b], P), MUL).then_inc(w_sta.sem, 1)

            def rwkv_finish(l):
                for j in range(4):
                    last = STT(rw_o[:, j, :], rw_o[:, j, :], V(l, "gn_w", j), rw_sq[:, j, :], MUL, MUL)
                link(last)
                for j in range(4):
                    last = STT(rw_o[:, j, :], rw_o[:, j, :], V(l, "gn_b", j), rw_bv[:, j, :], ADD, ADD)
                last.then_inc(hn_y.sem, 1)
                dve.wait_ge(*hn_y(l, 3))
                TT(y_rw[:, :, :], rw_o, rw_g, MUL).then_inc(rw_y.sem, 1)

            def closing(l):
                turns.pass_over(len(EARLY))
                with dve.Fori(0, KT // 2) as i:
                    inner = turns.loop(i, 5)
                    for _ in range(3):
                        inner.take()
                    for dd in range(2):
                        s, used = inner.take()
                        for n in range(3):
                            q = 3 * dd + n
                            dve.wait_ge(f_zs.sem, i * 6 + (3 + 24 * l + 2 * n + dd + 1))
                            if n == 2:
                                dve.wait_ge(slot_fr[s].sem, used + 1)
                            else:
                                dve.wait_ge(f_br.sem, i * 4 + (16 * l + 2 * dd + n + 1))
                            dst = mixed[:, bass.ds(i * 2 + dd, 1), :].rearrange("p a n -> p (a n)") if n == 0 \
                                else gtmp[:, n, :]
                            TT(dst, ps[:, 3 + q % 3, 0:T], gates[:, 2 * n + dd, :], MUL).then_inc(f_mul.sem, 1)
                            dve.wait_ge(f_mul.sem, i * 6 + (6 + 24 * l + q + 1))
                            acc = mixed[:, bass.ds(i * 2 + dd, 1), :].rearrange("p a n -> p (a n)")
                            if n == 0:
                                dve.sem_inc(f_gm.sem, 1)
                            else:
                                TT(acc, acc, gtmp[:, n, :], ADD).then_inc(f_gm.sem, 1)
                                dve.wait_ge(f_gm.sem, i * 6 + (3 + 24 * l + q + 1))
                turns.after(KT // 2, 5)
                for d in range(KT):
                    if d % 2 == 0:
                        s, used = turns.take()
                        dve.wait_ge(*f_out(l, d // 2 + 1))
                    else:
                        dve.wait_ge(slot_fr[s].sem, used + 1)
                    TT(X[:, d, :], X[:, d, :], ps[:, 6 + d % 2, 0:T], ADD).then_inc(x_mix.sem, 1)

            def route(l):
                link(dve.memset(lg, 0.0))
                dve.wait_ge(rt_lg.sem, 1)
                dve.tensor_copy(lg[:, 0:2, :], ps[:, 6, 0:16].rearrange("p (i e) -> p i e", i=2))
                link(dve.tensor_copy(lg[0:TS, 2, :], ps[0:TS, 6, 16:24]))
                for i in range(3):
                    last = dve.max(top[:, i, :], lg[:, i, :])
                link(last)
                v1 = top[:, :, 1:2].broadcast_to([P, 3, NE])
                TT(gt, lg, v1, ALU.is_gt)
                TT(eq, lg, v1, ALU.is_equal)
                link(TT(ex, lg, top[:, :, 0:1].broadcast_to([P, 3, NE]), SUB))
                dve.sem_inc(rt_e.sem, 1)
                for i in range(3):
                    dve.tensor_tensor_scan(cum[:, i, :], eq[:, i, :], eq[:, i, :], 0.0, ADD, ALU.bypass)
                link(dve.reduce_sum(cnt, gt, AX_X))
                link(TSC(cnt, cnt, -1.0, 2.0, MUL, ADD))
                link(TT(cum, cum, end(cnt, NE), ALU.is_le))
                link(TT(eq, eq, cum, MUL))
                link(TT(gt, gt, eq, ADD))
                dve.wait_ge(rt_ex.sem, 1)
                link(TT(ex, ex, gt, MUL))
                link(dve.reduce_sum(cnt2, ex, AX_X))
                link(dve.reciprocal(cnt2, cnt2))
                TT(ex, ex, end(cnt2, NE), MUL).then_inc(rt_cb.sem, 1)
                dve.wait_ge(rt_ct.sem, 1)
                dve.tensor_copy(crow[0:NE, :], ps[0:NE, 7, 0:T]).then_inc(rt_cr.sem, 1)
                dve.wait_ge(rt_bce.sem, NE)

            def feed_forward(l):
                with dve.Fori(0, PASSES[l]) as e:
                    inner = turns.loop(e, FT + KT, 1)
                    for f in range(FT):
                        s, used = inner.take()
                        dve.wait_ge(s_done.sem, e * FT + (h_base(l) + f + 1))
                        dve.wait_ge(slot_fr[s].sem, used + 1)
                        TT(hid[:, f, :], ps[:, 2 * (f % 3) + 1, 0:T], sil[:, f % 3, :], MUL).then_inc(h_done.sem, 1)
                    for d in range(KT):
                        s, used = inner.take()
                        dve.wait_ge(slot_fr[s].sem, used + 1)
                        if l == 0:
                            TT(X[:, d, :], X[:, d, :], ps[:, 6 + d % 2, 0:T], ADD).then_inc(y_done.sem, 1)
                            continue
                        c = comb[:, bass.ds(e, 1), :].rearrange("p a n -> p (a n)")
                        TT(ytmp[:, d % 2, :], ps[:, 6 + d % 2, 0:T], c, MUL).then_inc(y_mul.sem, 1)
                        dve.wait_ge(y_mul.sem, e * KT + (d + 1))
                        TT(X[:, d, :], X[:, d, :], ytmp[:, d % 2, :], ADD).then_inc(y_done.sem, 1)
                turns.after(PASSES[l], FT + KT, 1)

            for k in range(3):
                dve.sem_inc(f_gm.sem, 1)
                dve.sem_inc(h_done.sem, 1)
            for k in range(6):
                dve.sem_inc(f_mul.sem, 1)
            for k in range(2):
                dve.sem_inc(y_done.sem, 1)
            dve.wait_ge(ld_con.sem, 64)
            for l in range(DEPTH):
                norm(2 * l)
                histories(l)
                conv(l)
                mlstm_gates(l)
                mlstm_keys(l)
                for h in range(NH):
                    mlstm_head(l, h)
                mlstm_state(l)
                head_norm(3 * l, ml_o, ml_sq, P, GN_EPS, lambda: mlstm_finish(l))
                dve.wait_ge(*hn_y(l, 1))
                retention(l)
                head_norm(3 * l + 1, ret_o, ret_sq, P, GN_EPS, lambda: retention_finish(l))
                dve.wait_ge(*hn_y(l, 2))
                rwkv_prepare(l)
                rwkv_gram(l)
                rwkv_invert(l)
                rwkv_chunks(l)
                head_norm(3 * l + 2, rw_o, rw_sq, CH, RW_GN_EPS, lambda: rwkv_finish(l))
                closing(l)
                norm(2 * l + 1)
                if l == 1:
                    route(l)
                feed_forward(l)
            norm(2 * DEPTH)

        @block.gpsimd
        def _(pool):
            for l in range(DEPTH):
                if l > 0:
                    pool.wait_ge(y_done.sem, CREDIT_Y + KT * NDENSE)
                    pool.wait_ge(*w_zs(l - 1))
                pool.dma_start(hist[:, :], a["hist"][l]).then_inc(ld_hist.sem, 16)
                pool.dma_start(prev[:, :], a["prev"][l]).then_inc(ld_hist.sem, 16)
                pool.dma_start(C0, a["C"][l]).then_inc(ld_c0.sem, 16)
                pool.dma_start(n0, a["n"][l]).then_inc(ld_n0.sem, 16)
                pool.wait_ge(*co_ok(l))
                pool.dma_start(o["conv"][l], conv_out[:, :, :]).then_inc(st_small.sem, 16)
                pool.wait_ge(*ml_out(l))
                pool.wait_ge(*ml_cpe(l))
                pool.dma_start(o["m"][l], m_out[:, :]).then_inc(st_ml.sem, 16)
                pool.dma_start(o["n"][l], n_out[:, :]).then_inc(st_ml.sem, 16)
                pool.dma_start(o["C_p"][l], Cp).then_inc(st_ml.sem, 16)
                pool.dma_start(o["C_s"][l], C0).then_inc(st_ml.sem, 16)
                pool.wait_ge(*hn_y(l, 1))
                pool.dma_start(dec, a["dec"].rearrange("p (h w) -> p h w", h=NH)).then_inc(ld_ret.sem, 16)
                pool.dma_start(S0_ret, a["ret"][l]).then_inc(ld_ret.sem, 16)
                pool.wait_ge(*r_spe(l))
                pool.dma_start(o["ret_p"][l], Sp_ret).then_inc(st_ret.sem, 16)
                pool.wait_ge(*r_ssa(l, 8))
                pool.dma_start(o["ret_s"][l], S0_ret).then_inc(st_ret.sem, 16)
                pool.wait_ge(*hn_y(l, 2))
                pool.wait_ge(st_ml.sem, 64 * (l + 1))
                pool.wait_ge(st_ret.sem, 32 * (l + 1))
                pool.memset(UV[0:CH, :, :], 0.0).then_inc(w_zuv.sem, 1)
                pool.wait_ge(*w_zuv(l, 1))
                pool.memset(UV[CH:P, NC - 1, :], 0.0).then_inc(w_zuv.sem, 1)
                for k, t in enumerate((BK, KR)):
                    pool.wait_ge(*w_zuv(l, 2 + k))
                    v = t[:, :, NC - 1, :].rearrange("p j (q s) -> p j q s", q=2)[:, :, :, TS:]
                    pool.memset(v, 0.0).then_inc(w_zuv.sem, 1)
                pool.wait_ge(*so_ok(l))
                pool.dma_start(o["shift"][l], shift_out[:, :, :]).then_inc(st_small.sem, 16)
                pool.wait_ge(*w_pre(l))
                pool.memset(Abd, 0.0).then_inc(w_zab.sem, 1)
                pool.memset(Xbd, 0.0).then_inc(w_zab.sem, 1)
                pool.wait_ge(*w_bt(l, 5))
                pool.wait_ge(*w_xt(l, 2))
                pool.dma_start(S0bd, a["rw"][l]).then_inc(ld_rw.sem, 16)
                pool.wait_ge(*w_su(l, 4))
                pool.dma_start(o["rw_p"][l], Sbd).then_inc(st_rw.sem, 16)
                pool.wait_ge(*w_sta(l, 8))
                pool.dma_start(o["rw_s"][l], S0bd).then_inc(st_rw.sem, 16)
            for s, n in ((st_small, 32), (st_ml, 64), (st_ret, 32), (st_rw, 32)):
                pool.wait_ge(s.sem, n * DEPTH)


def kernel(**inputs):
    import numpy as _np
    import concourse.bacc as _bacc
    from concourse.bass_utils import run_bass_kernel_spmd as _run

    f = {k: _np.asarray(v) for k, v in inputs.items()}
    tiles = lambda v: v.reshape(v.shape[0], -1, P).transpose(0, 2, 1)

    x = _np.concatenate([f["x_prompt"].reshape(TP, D), f["x_sample"].reshape(TS, D)], 0)
    arrays = {"x": x.reshape(T, KT, P).transpose(2, 1, 0)}
    con, dec = shape_constants()
    arrays["con"], arrays["dec"] = con, dec
    vec = [f["norm_mix"], f["norm_ffn"], f["ret_gn"], f["ml_conv_w"].reshape(DEPTH, -1), f["ml_conv_b"], f["ml_gn"],
           f["ml_skip"], f["rw_mu"], f["rw_w0"], f["rw_a0"], f["rw_kk"], f["rw_ka"], f["rw_rk"], f["rw_gn_w"],
           f["rw_gn_b"], _np.stack([f["final_norm"]] * DEPTH)]
    arrays["vec"] = _np.concatenate([tiles(v) for v in vec], 2).transpose(1, 0, 2)
    arrays["bias"] = _np.stack([f["ml_bi"], f["ml_bf"]], 2).transpose(1, 0, 2)
    arrays["m0"] = f["state_mlstm_m"].transpose(2, 0, 1)
    rows_of = lambda w: w.reshape(w.shape[0], -1, P, w.shape[-1]).transpose(0, 2, 1, 3)
    router = _np.concatenate([_np.zeros((DEPTH - 1, D, NE), _np.float32), f["moe_router"]], 0)
    w_in = rows_of(f["w_in"])
    arrays["lw"] = _np.concatenate([
        w_in[..., 2560:2568].reshape(DEPTH, P, -1),
        f["ml_wq"].transpose(0, 2, 1, 3).reshape(DEPTH, P, -1), f["ml_wk"].transpose(0, 2, 1, 3).reshape(DEPTH, P, -1),
        _np.concatenate([f["rw_w2"], f["rw_a2"]], 1), f["rw_g2"], rows_of(router).reshape(DEPTH, P, -1)], 2)
    first = {"rq": 0, "rk": 256, "rv": 512, "rg": 1024, "mx": 1536, "mv": 2048, "mo": 2568, "zrw": 3080}
    mix = _np.zeros((DEPTH, NSLAB, P, SLOT), _np.float32)
    w_br = f["w_branch"].reshape(DEPTH, 3, 4, P, D)
    w_out = rows_of(f["w_out"])
    for n, (kind, j) in enumerate(EARLY + LATE + OUTS):
        if kind == "gate":
            c0 = 4872 + (j % 3) * D + (j // 3) * 256
            mix[:, n] = w_in[..., c0:c0 + 256].reshape(DEPTH, P, SLOT)
        elif kind == "branch":
            mix[:, n, :, 0:12 * P] = w_br[..., P * j:P * j + P].transpose(0, 3, 1, 2, 4).reshape(DEPTH, P, 12 * P)
        elif kind == "out":
            mix[:, n] = w_out[..., 256 * j:256 * j + 256].reshape(DEPTH, P, SLOT)
        else:
            c0 = first[kind] + 256 * j
            mix[:, n] = w_in[..., c0:c0 + 256].reshape(DEPTH, P, SLOT)
    arrays["mix"] = mix
    half = lambda w, ax: _np.stack(_np.split(w[0], 2, ax))
    wg = _np.concatenate([half(f["ffn_w_gate"], 1), f["moe_w_gate"][0]], 0)
    wu = _np.concatenate([half(f["ffn_w_up"], 1), f["moe_w_up"][0]], 0)
    wd = _np.concatenate([half(f["ffn_w_down"], 0), f["moe_w_down"][0]], 0)
    ne = NDENSE + NE
    cut = lambda w: w.reshape(ne, KT, P, FT, P).transpose(0, 3, 2, 1, 4).reshape(ne * FT, P, KT * P)
    arrays["gu"] = _np.concatenate([cut(wg), cut(wu)], 2)
    arrays["down"] = wd.reshape(ne, FT, P, KT, P).transpose(0, 3, 2, 1, 4).reshape(ne * KT, P, FT * P)
    arrays["hist"] = f["state_mlstm_conv"].reshape(DEPTH, SB, XPAD, 4, P).transpose(0, 4, 3, 1, 2)\
        .reshape(DEPTH, P, -1)
    arrays["prev"] = f["state_rwkv_shift"].reshape(DEPTH, SB, ZT, P).transpose(0, 3, 2, 1).reshape(DEPTH, P, -1)
    arrays["C"] = f["state_mlstm_C"].transpose(0, 3, 1, 2, 4)
    arrays["n"] = f["state_mlstm_n"].transpose(0, 3, 1, 2).reshape(DEPTH, P, -1)
    arrays["ret"] = f["state_ret"].reshape(DEPTH, SB, 2, 2, DK, P).transpose(0, 3, 4, 1, 2, 5)\
        .reshape(DEPTH, P, SB, 2, P)
    s0 = f["state_rwkv"].reshape(DEPTH, SB, NP4, 2, DK, DK)
    rw = _np.zeros((DEPTH, 2, DK, SB, NP4, 2, DK), _np.float32)
    for p in range(2):
        rw[:, p, :, :, :, p, :] = s0[:, :, :, p].transpose(0, 4, 1, 2, 3)
    arrays["rw"] = rw.reshape(DEPTH, P, SB, NP4, P)
    arrays = {"in_" + k: _np.ascontiguousarray(v) for k, v in arrays.items()}

    nc = _bacc.Bacc("TRN2", target_bir_lowering=False, num_devices=1)
    a = {k[3:]: nc.dram_tensor(k, v.shape, F32, kind="ExternalInput").ap() for k, v in arrays.items()}
    shapes = {"y": (P, KT, T), "conv": (DEPTH, P, 4, 27), "shift": (DEPTH, P, ZT, 9), "m": (DEPTH, NH, 9),
              "n": (DEPTH, P, NH + SB * NH), "C_p": (DEPTH, P, 512), "C_s": (DEPTH, P, SB, NH, P),
              "ret_p": (DEPTH, P, 256), "ret_s": (DEPTH, P, SB, 2, P), "rw_p": (DEPTH, P, NP4, P),
              "rw_s": (DEPTH, P, SB, NP4, P)}
    o = {k: nc.dram_tensor("out_" + k, s, F32, kind="ExternalOutput").ap() for k, s in shapes.items()}
    build(nc, a, o)
    res = _run(nc, [arrays], core_ids=[0]).results[0]
    r = {k: _np.asarray(res["out_" + k]) for k in shapes}

    y = r["y"].transpose(2, 1, 0).reshape(T, D)
    ret_p = r["ret_p"].reshape(DEPTH, 2, DK, 2, P).transpose(0, 3, 1, 2, 4).reshape(DEPTH, 1, NH, DK, P)
    ret_s = r["ret_s"].reshape(DEPTH, 2, DK, SB, 2, P).transpose(0, 3, 4, 1, 2, 5).reshape(DEPTH, SB, NH, DK, P)
    C_p = r["C_p"].reshape(DEPTH, P, NH, P).transpose(0, 2, 1, 3)[:, None]
    C_s = r["C_s"].transpose(0, 2, 3, 1, 4)
    n_p = r["n"][:, :, 0:NH].transpose(0, 2, 1)[:, None]
    n_s = r["n"][:, :, NH:].reshape(DEPTH, P, SB, NH).transpose(0, 2, 3, 1)
    m_p, m_s = r["m"][:, :, 0][:, None], r["m"][:, :, 1:].transpose(0, 2, 1)
    conv_p = r["conv"][..., 0:3].transpose(0, 3, 2, 1).reshape(DEPTH, 1, 3, 512)
    conv_s = r["conv"][..., 3:].reshape(DEPTH, P, 4, SB, 3).transpose(0, 3, 4, 2, 1).reshape(DEPTH, SB, 3, 512)
    shift = r["shift"].transpose(0, 3, 2, 1).reshape(DEPTH, 9, -1)

    def heads(v, n):
        v = v.reshape(DEPTH, 2, DK, n, NP4, 2, DK)
        v = _np.stack([v[:, p, :, :, :, p, :] for p in range(2)], 1)
        return v.transpose(0, 3, 4, 1, 5, 2).reshape(DEPTH, n, 2 * NP4, DK, DK)

    rw_p, rw_s = heads(r["rw_p"], 1), heads(r["rw_s"], SB)
    out = (y[:TP].reshape(1, TP, D), y[TP:].reshape(SB, ST, D), ret_p, C_p, n_p, m_p, conv_p, rw_p, shift[:, 0:1],
           ret_s, C_s, n_s, m_s, conv_s, rw_s, shift[:, 1:])
    return tuple(_np.ascontiguousarray(v) for v in out)
```

```python
from contextlib import ExitStack

import concourse.bass as bass
import numpy as np
from concourse import mybir

F32 = mybir.dt.float32
ACT = mybir.ActivationFunctionType
ALU = mybir.AluOpType
AX_X = mybir.AxisListType.X

P = 128
DEPTH = 2
D = 1024
KT = D // P
TP, SB, ST = 256, 8, 4
TS = SB * ST
T = TP + TS
PAST = 2048
NH = 4
DK = 64
CONV = 4
ZT = 14
ZP = 1 + TP + SB * (1 + ST)
XPAD = CONV - 1
XW = XPAD + TP + SB * (XPAD + ST)
FT = 11
NE = 8
NDENSE = 2
MB = 128
MAXB = -(-T // MB)
MAXEXTRA = (2 * T - 1) // MB
DSL = (FT + 1) // 2
CH = 64
NC = TP // CH + 1
NP4 = 4
NU = NC * NP4
PW = 2 * P + P + TS
RING = 5
SLOT = 2048
NORM_EPS, GN_EPS, RW_GN_EPS = 1e-6, 1e-5, 64e-5
RW_DECAY = 0.606531
NEG = -1.0e30
LEVELS = (2, 4, 8, 16, 32)

VEC = {}
_at = 0
for _n, _w in (("norm_mix", 8), ("norm_ffn", 8), ("ret_gn", 4), ("conv_w", 16), ("conv_b", 4), ("ml_gn", 4),
               ("ml_skip", 4), ("mu", 14), ("w0", 4), ("a0", 4), ("kk", 4), ("ka", 4), ("rk", 4), ("gn_w", 4),
               ("gn_b", 4), ("final", 8)):
    VEC[_n] = _at
    _at += _w
NVEC = _at

LW = {}
_at = 0
for _n, _w in (("if", KT * 8), ("wq", 512), ("wk", 512), ("lora", 512), ("g2", 512), ("router", KT * NE)):
    LW[_n] = _at
    _at += _w
NLW = _at

CON = {}
_at = 0
for _n, _w in (("ident", 128), ("ones", 128), ("swap", 128), ("cent128", 128), ("cent64", 128), ("ones64", 128),
               ("cos", T), ("sin", T), ("causal_neg", 128), ("sample_neg", TS), ("reset64", T), ("reset_mul", T),
               ("reset_add", T), ("gram_p", 128), ("gram_s", 128), ("a_p", 64), ("a_s", 64), ("ident64", 64),
               ("join0", 64), ("join0t", 64), ("joins", 5 * 64), ("kdec", 12), ("qdec", 2 * TS), ("g4", 2),
               ("bmask", 8), ("bmask2", 8), ("sel", 1024)):
    CON[_n] = _at
    _at += _w
NCON = _at


def shape_constants():
    c = np.zeros((P, NCON), np.float32)
    r = np.arange(P)

    def put(name, a):
        a = np.asarray(a, np.float32)
        c[:a.shape[0], CON[name]:CON[name] + a.shape[1]] = a

    put("ident", np.eye(P))
    put("ones", np.ones((P, P)))
    half = DK // 2
    other = r // DK * DK + (r % DK + half) % DK
    put("swap", (other[:, None] == r[None, :]))
    put("cent128", np.eye(P) - 1.0 / P)
    same = (r[:, None] // DK == r[None, :] // DK)
    put("cent64", np.eye(P) - same / DK)
    put("ones64", same)
    pos = np.concatenate([np.arange(TP), np.tile(PAST + np.arange(ST), SB)]).astype(np.float32)
    inv = (10000.0 ** (-np.arange(half, dtype=np.float64) / half)).astype(np.float32)
    ang = (pos[None, :] * inv[r % half][:, None]).astype(np.float32).astype(np.float64)
    put("cos", np.cos(ang))
    put("sin", np.sin(ang) * np.where(r % DK < half, -1.0, 1.0)[:, None])
    put("causal_neg", np.where(r[:, None] <= r[None, :], 0.0, NEG))
    s = np.arange(TS)
    seq = s[:, None] // ST == s[None, :] // ST
    put("sample_neg", np.where(seq & (s[:, None] <= s[None, :]), 0.0, NEG))
    col = np.arange(T)
    starts = (col >= TP) & ((col - TP) % ST == 0)
    put("reset64", np.tile(~(starts | ((col < TP) & (col % CH == 0))), (P, 1)))
    put("reset_mul", np.tile(~(starts | (col == 0)), (P, 1)))
    put("reset_add", np.tile(np.where(starts | (col == 0), NEG, 0.0), (P, 1)))
    t = np.arange(CH)
    blk = (t[:, None] // ST == t[None, :] // ST) & (t[:, None] < TS) & (t[None, :] < TS)
    for name, ok in (("p", np.ones((CH, CH), bool)), ("s", blk)):
        strict, incl = (t[:, None] < t[None, :]) & ok, (t[:, None] <= t[None, :]) & ok
        put("gram_" + name, np.tile(np.concatenate([strict, incl], 1), (2, 1)))
        put("a_" + name, np.tile((t[None, :] < t[:, None]) & ok, (2, 1)))
    put("ident64", np.tile(np.eye(CH), (2, 1)))

    def join(m):
        return np.where((t[:, None] // m + 1 == t[None, :] // m) & (t[:, None] // (2 * m) == t[None, :] // (2 * m)), -1.0, 0.0)

    put("join0", np.tile(join(1), (2, 1)))
    put("join0t", np.tile(join(1).T, (2, 1)))
    put("joins", np.tile(np.concatenate([join(m) for m in LEVELS], 1), (2, 1)))
    lg = np.log1p(-(2.0 ** (-5.0 - np.arange(NH))))
    tok = np.arange(P)[:, None]
    kd = [np.exp((TP - 1 - tok) * lg), np.exp((TP - 1 - tok - P) * lg), np.exp((ST - 1 - tok % ST) * lg)]
    put("kdec", np.concatenate(kd, 1))
    head = r // DK
    put("qdec", np.concatenate([np.exp((s % ST + 1)[None, :] * lg[2 * i + head][:, None]) for i in range(2)], 1))
    put("g4", np.stack([np.exp(ST * lg[2 * i + head]) for i in range(2)], 1))
    put("bmask", r[:, None] // ST == np.arange(SB)[None, :])
    put("bmask2", (r % CH)[:, None] // ST == np.arange(SB)[None, :])
    put("sel", np.repeat(np.eye(8), P, 1))
    dec = np.zeros((P, NH, PW), np.float32)
    for h in range(NH):
        d0 = np.arange(TP)[None, :] - r[:, None]
        d1 = d0[:, :P]
        ds = s[None, :] - s[:, None]
        dec[:, h, 0:TP] = np.where(d0 >= 0, np.exp(np.maximum(d0, 0) * lg[h]), 0)
        dec[:, h, TP:TP + P] = np.where(d1 >= 0, np.exp(np.maximum(d1, 0) * lg[h]), 0)
        dec[:TS, h, TP + P:] = np.where(seq & (ds >= 0), np.exp(np.maximum(ds, 0) * lg[h]), 0)
    return c, dec.reshape(P, NH * PW)


PLAN_N = 2 * (NE + MAXEXTRA + 1) + 1
PC = {}
_at = 0
for _n, _w in (("tri", 128), ("iota", MAXB * MB), ("iotac", MAXB), ("first", PLAN_N), ("more", (MAXB - 1) * NE),
               ("rank", MAXEXTRA * (MAXB - 1) * NE), ("expert", MAXEXTRA * (MAXB - 1) * NE),
               ("block", MAXEXTRA * (MAXB - 1) * NE)):
    PC[_n] = _at
    _at += _w
NPC = _at


def plan_constants():
    c = np.zeros((P, NPC), np.float32)
    r = np.arange(P)

    def put(name, a):
        a = np.asarray(a, np.float32)
        c[:, PC[name]:PC[name] + a.shape[-1]] = a

    put("tri", r[:, None] < r[None, :])
    put("iota", 1 + np.arange(MAXB * MB))
    put("iotac", 1 + r[:, None] + MB * np.arange(MAXB)[None, :])
    first = np.zeros(PLAN_N)
    first[0:NE], first[-1] = np.arange(NE), NE
    put("first", first)
    slots = np.arange((MAXB - 1) * NE)
    put("more", MB * (1 + slots // NE))
    put("rank", np.repeat(1 + np.arange(MAXEXTRA), len(slots)))
    put("expert", np.tile(slots % NE, MAXEXTRA))
    put("block", np.tile(1 + slots // NE, MAXEXTRA))
    return c


def mixer_slabs():
    early = [("mx", 0), ("mx", 1), ("mv", 0), ("mv", 1)] + [("zrw", i) for i in range(7)]
    early += [("rq", 0), ("rk", 0), ("rv", 0), ("rv", 1), ("mo", 0), ("mo", 1), ("rg", 0), ("rg", 1)]
    late = []
    for j in range(KT // 2):
        late += [("gate", 3 * j + n) for n in range(3)] + [("branch", 2 * j), ("branch", 2 * j + 1)]
    return early, late, [("out", j) for j in range(4)]


EARLY, LATE, OUTS = mixer_slabs()
NSLAB = len(EARLY) + len(LATE) + len(OUTS)


class Signal:

    def __init__(self, sem, per_layer=1):
        self.sem, self.per = sem, per_layer

    def __call__(self, layer, k=1):
        return self.sem, layer * self.per + k


class Part:

    def __init__(self, whole, offset):
        self.sem, self.whole, self.offset = whole.sem, whole, offset

    def __call__(self, layer, k=1):
        return self.whole(layer, self.offset + k)


class Turns:

    def __init__(self):
        self.turn, self.used = 0, [0] * RING

    def take(self):
        s = self.turn % RING
        n = self.used[s]
        self.turn, self.used[s] = self.turn + 1, n + 1
        return s, n

    def pass_over(self, n):
        for _ in range(n):
            self.take()

    def loop(self, i, turns, padded=0):
        inner = Turns()
        inner.turn = self.turn
        per = [0] * RING
        for k in range(turns):
            per[(self.turn + k) % RING] += 1
        inner.used = [self.used[s] + i * per[s] for s in range(RING)]
        return inner

    def after(self, passes, turns, padded=0):
        for k in range(turns):
            self.used[(self.turn + k) % RING] += passes
        self.turn += passes * (turns + padded)


GROUPS = ([("mx", j) for j in range(4)] + [("mi", 0), ("mf", 0)] + [("mv", j) for j in range(6)] +
          [("zrw", j) for j in range(ZT)] + [("rq", j) for j in range(2)] + [("rk", j) for j in range(2)] +
          [("rv", j) for j in range(6)] + [("mo", j) for j in range(4)] + [("rg", j) for j in range(4)])
NG = len(GROUPS)


def piece_of(kind, j):
    if kind in ("mi", "mf"):
        return None, 0, False
    if kind in ("mv", "rv"):
        return j // 3, j % 3, j % 3 == 2
    return j // 2, j % 2, j % 2 == 1


NPROJ = sum(not piece_of(*g)[2] for g in GROUPS)


def seq4(ap):
    return ap.rearrange("p (b t) -> p b t", t=ST)


def build(nc, a, o):
    with ExitStack() as ctx:
        def sb(name, shape):
            return ctx.enter_context(nc.sbuf_tensor(name, shape, F32))

        def sig(name, per_layer=1):
            return Signal(ctx.enter_context(nc.semaphore(name)), per_layer)

        ps = ctx.enter_context(nc.psum_tensor("ps", [P, 8, 512], F32))
        X = sb("X", [P, KT, T])
        xn = sb("xn", [P, KT, T])
        ring = sb("ring", [P, RING, SLOT])
        lw = sb("lw", [P, NLW])
        vec = sb("vec", [P, DEPTH, NVEC])
        con = sb("con", [P, NCON])
        y_ret, y_ml, y_rw = sb("y_ret", [P, 4, T]), sb("y_ml", [P, 4, T]), sb("y_rw", [P, 4, T])
        rstd = sb("rstd", [P, T])
        gate_bias = sb("gate_bias", [NH, DEPTH, 2])
        m0 = sb("m0", [NH, DEPTH, SB])
        hist = sb("hist", [P, 4 * SB * XPAD])
        prev = sb("prev", [P, ZT * SB])
        conv_out = sb("conv_out", [P, 4, (1 + SB) * XPAD])
        shift_out = sb("shift_out", [P, ZT, 1 + SB])
        m_out = sb("m_out", [NH, 1 + SB])
        n_out = sb("n_out", [P, NH + SB * NH])
        gate_rows = sb("gate_rows", [NH, 1, T])
        ARENA = 26900
        arena = sb("arena", [P, ARENA])

        def at(start, *dims):
            n = int(np.prod(dims))
            assert start + n <= ARENA, (start, dims)
            v = arena[:, start:start + n]
            if len(dims) == 2:
                v = v.rearrange("p (a b) -> p a b", a=dims[0])
            if len(dims) == 3:
                v = v.rearrange("p (a b c) -> p a b c", a=dims[0], b=dims[1])
            if len(dims) == 4:
                v = v.rearrange("p (a b c d) -> p a b c d", a=dims[0], b=dims[1], c=dims[2])
            return v

        def C(name, w, rows=P, off=0):
            return con[0:rows, CON[name] + off:CON[name] + off + w]

        def V(l, name, j=0):
            return vec[:, l, VEC[name] + j:VEC[name] + j + 1]

        norm_sq = at(4158, KT, T)
        z = at(0, ZT, ZP)
        mxp = at(4158, 4, XW)
        ml_o = at(4158, 4, T)
        xc = at(5418, 4, T)
        mq = at(6570, 4, T)
        mk = at(7722, 4, T)
        mkt = at(8874, 3, 512)
        mvt = at(10410, 3, 512)
        C0 = at(11946, SB, NH, P)
        kb = at(16042, 2, 512)
        rows = at(17066, 4, T)
        ml_W = at(18218, PW)
        ml_PW = at(18634, PW)
        ml_sq = at(19050, 4, T)
        ml_den = at(20202, T)
        gwc = at(20490, 24)
        qa = at(20514, TS)
        nq = at(20546, TS)
        aL = at(20578, SB, NH)
        n0 = at(20610, SB * NH)
        Cp = at(20642, 512)
        arow = at(21154, TS)
        rqk = at(21186, 4, T)
        rvt = at(22338, 3, 512)
        qr = at(4158, 4, T)
        rt = at(5310, 4, T)
        ktd = at(6462, 3, 256)
        qd = at(7230, 2, TS)
        rpw = at(7294, 2, PW)
        rkb = at(8126, 2, 256)
        Sp_ret = at(8638, 256)
        ret_o = at(8894, 4, T)
        ret_sq = at(10046, 4, T)
        dec = at(16042, NH, PW)
        S0_ret = at(17706, SB, 2, P)
        zs = at(4158, ZT, T)
        rw_lw = at(8190, 4, T)
        rw_a = at(9342, 4, T)
        rw_kk = at(10494, 4, T)
        rw_kp = at(11646, 4, T)
        rw_e1 = at(12798, 4, T)
        rw_e2 = at(13950, 4, T)
        lora_in = at(15102, T)
        lora_g = at(15390, T)
        rw_g = at(15678, 4, T)
        rw_bv = at(16830, 4, T)
        BK = at(17982, NP4, NC, 2 * CH)
        KR = at(20542, NP4, NC, 2 * CH)
        UV = at(23102, NC, 512)
        PL = at(25662, NP4, 4 + SB)
        rw_o = at(25710, 4, T)
        G = at(0, NC, 2, NP4 * P)
        XT = at(5120, NU, 2 * CH)
        Abd = at(7680, NU, P)
        Xbd = at(10240, NU, P)
        Xc = at(12800, NU, CH)
        Yc = at(14080, NU, CH)
        BKt = at(7680, NC, 512)
        S0bd = at(10240, SB, NP4, P)
        Sbd = at(14336, NP4, P)
        Rn = at(14848, 512)
        CX = at(15360, NP4, 2, TS)
        KBm = [at(14848, 512), at(5120, 512)]
        rw_sq = at(0, 4, T)
        gates = at(0, 6, T)
        gtmp = at(1728, 3, T)
        mixed = at(2592, KT, T)
        hid = at(7000, FT, T)
        sil = at(10200, 3, T)
        xt = at(7000, 3, D)
        xg = at(10072, KT, MB)
        ehid = at(11096, FT, MB)
        esil = at(12504, 3, MB)
        pick_in = at(12888, 3, MB)
        pick_out = at(13272, T)
        yg = at(13560, D)
        comb, posb = at(14600, NE, T), at(16904, NE, T)
        pcon = at(19208, NPC)
        lg, top, gt, eq, cum, ex, posn = (at(20100 + 24 * k, 3, NE) for k in range(7))
        cnt, cnt2 = at(20270, 3), at(20274, 3)
        crow, prow = at(20300, T), at(20600, T)
        slots_n = (MAXB - 1) * NE
        need, rank = at(20900, slots_n), at(20916, slots_n)
        hits, hits2 = at(20940, MAXEXTRA, slots_n), at(21020, MAXEXTRA, slots_n)
        draft = at(21100, PLAN_N)
        plan = ctx.enter_context(nc.sbuf_tensor("plan", [1, PLAN_N], mybir.dt.int32))

        def PCON(name, w, rows=P, off=0):
            return pcon[0:rows, PC[name] + off:PC[name] + off + w]

        slot_ld = [sig(f"slot_loaded{s}") for s in range(RING)]
        slot_fr = [sig(f"slab_used{s}") for s in range(RING)]
        ld_con, ld_x, ld_lw, ld_hist = sig("ld_con"), sig("ld_x"), sig("ld_lw"), sig("ld_hist")
        ld_c0, ld_n0, ld_ret, ld_rw = sig("ld_c0"), sig("ld_n0"), sig("ld_ret"), sig("ld_rw")
        st_ml, st_small, st_ret, st_rw, st_y = sig("st_ml"), sig("st_small"), sig("st_ret"), sig("st_rw"), sig("st_y")
        dch, ach, gch = sig("vector_chain"), sig("scalar_chain"), sig("pool_chain")
        nm_sq, nm_ms, nm_rec, nm_rstd, nm_xn = (sig(n) for n in ("nm_sq", "nm_ms", "nm_rec", "nm_rstd", "nm_xn"))
        proj, evac = sig("proj", NPROJ), sig("evac", NG)
        pads = sig("pads")
        conv_acc, xc_ok = sig("conv_acc"), sig("xc_ok")
        gate_v, gate_s = sig("gate_rows_vector", 2), sig("gate_rows_scalar", 3)
        u_abs, lf_ok = Part(gate_v, 0), Part(gate_v, 1)
        u_exp, gr_ok, er_ok = Part(gate_s, 0), Part(gate_s, 1), Part(gate_s, 2)
        ml_col, ml_colv = sig("ml_col"), sig("ml_colv")
        mqk_p, mqk_e, kdec_ok = sig("mqk_p", 11), sig("mqk_e", 11), sig("kdec_ok")
        ml_bc, ml_wl, ml_ex, ml_pw = sig("ml_bc", 4), sig("ml_wl", 4), sig("ml_ex", 4), sig("ml_pw", 4)
        ml_s = sig("ml_scores", 4)
        ml_nd, ml_ad, ml_h = sig("ml_nd", 4), sig("ml_ad", 4), sig("ml_h", 4)
        ml_cp, ml_cpe, ml_kb, ml_sc, ml_sca = sig("ml_cp"), sig("ml_cpe"), sig("ml_kb", 8), sig("ml_sc", 8), sig("ml_sca", 8)
        ml_out, co_ok, so_ok = sig("ml_out"), sig("conv_out_ok"), sig("shift_out_ok")
        hn_c, hn_s, hn_x, hn_v = sig("hn_c", 12), sig("hn_s", 12), sig("hn_x", 12), sig("hn_v", 12)
        hn_r, hn_q, hn_y = sig("hn_r", 3), sig("hn_q", 3), sig("hn_y", 3)
        r_sw, r_qr, r_kt, r_ktd = sig("r_sw", 4), sig("r_qr"), sig("r_kt", 3), sig("r_ktd", 3)
        r_sc, r_pw, r_o, r_oe = sig("r_sc", 4), sig("r_pw", 4), sig("r_o", 4), sig("r_oe", 4)
        r_sp, r_spe, r_kb, r_ss, r_ssa = sig("r_sp"), sig("r_spe"), sig("r_kb", 8), sig("r_ss", 8), sig("r_ssa", 8)
        w_zs, w_thl, w_lora, w_lorae = sig("w_zs"), sig("w_thl"), sig("w_lora", 12), sig("w_lorae", 12)
        w_sq, w_ss, w_rk, w_bo = sig("w_sq"), sig("w_ss", 4), sig("w_rk"), sig("w_bo", 4)
        w_ssr, w_ssq, w_F, w_E, w_vt, w_vte = sig("w_ssr"), sig("w_ssq"), sig("w_F"), sig("w_E"), sig("w_vt", 5), sig("w_vte", 5)
        w_pre, w_sz, w_zero, rw_y, w_ob = sig("w_pre"), sig("w_sz"), sig("w_zero", 6), sig("rw_y"), sig("w_ob", 5)
        w_zuv, w_zab = Part(w_zero, 0), Part(w_zero, 4)
        w_g1, w_g1e, w_g2, w_g2e = sig("w_g1", 10), sig("w_g1e", 10), sig("w_g2", 6), sig("w_g2e", 6)
        w_x0 = sig("w_x0")
        w_y, w_ye, w_p, w_pe, w_t, w_te = (sig("w_y", 15), sig("w_ye", 15), sig("w_p", 15), sig("w_pe", 15),
                                           sig("w_t", 20), sig("w_te", 12))
        w_to = sig("w_to", 8)
        w_xt, w_bt, w_bte = sig("w_xt", 2), sig("w_bt", 5), sig("w_bte", 5)
        w_r, w_rn, w_u, w_ue, w_s, w_su, w_oc = (sig("w_r", 5), sig("w_rn", 5), sig("w_u", 5), sig("w_ue", 5),
                                                 sig("w_s", 4), sig("w_su", 4), sig("w_oc", 5))
        w_oe = sig("w_oe", 5)
        w_cx, w_cxe, w_ct = sig("w_cx"), sig("w_cxe"), sig("w_ct")
        w_kb, w_st, w_sta = sig("w_kb", 8), sig("w_st", 8), sig("w_sta", 8)
        f_zg, f_zs, f_br = sig("f_zg", 12), sig("f_zs", 24), sig("f_br", 16)
        f_gm, f_out, x_mix = sig("f_gm", 24), sig("f_out", 4), sig("x_mix", 8)
        f_mul = sig("f_mul", 24)
        g_done, s_done, h_done = sig("g_done"), sig("s_done"), sig("h_done")
        y_done = sig("y_done")
        rt_p, rt_v = sig("route_tensor", 3), sig("route_vector", 5)
        rt_lg, rt_pos, rt_ct = Part(rt_p, 0), Part(rt_p, 1), Part(rt_p, 2)
        rt_e, rt_sel, rt_cb, rt_cr, plan_ok = (Part(rt_v, k) for k in range(5))
        rt_ex, rt_bc, rt_cbe, rt_pbe = sig("rt_ex"), sig("rt_bc"), sig("rt_cbe"), sig("rt_pbe")
        xt_p, xt_a, xt_d = sig("xt_p"), sig("xt_a"), sig("xt_d")
        in_ok, out_ok = sig("pick_in_ok"), sig("pick_out_ok")
        ga_p, ga_a, ga_d = sig("gather_p"), sig("gather_a"), sig("gather_d")
        do_p, yg_a, yg_d = sig("down_p"), sig("yg_a"), sig("yg_d")
        sc_p, sc_e = sig("scatter_p"), sig("scatter_e")
        ETURNS, EPAD = FT + DSL, -(FT + DSL) % RING
        CREDIT_H, CREDIT_Y = 3, 2

        TOK = ((0, P), (P, P), (TP, TS))

        block = ctx.enter_context(nc.Block())

        @block.sync
        def _(sp):
            turns = Turns()

            def load(turns, src, width):
                s, n = turns.take()
                if not isinstance(n, int) or n > 0:
                    sp.wait_ge(slot_fr[s].sem, n)
                sp.dma_start(ring[:, s, 0:width], src).then_inc(slot_ld[s].sem, 16)

            sp.dma_start(X[:, :, :], a["x"]).then_inc(ld_x.sem, 16)
            sp.dma_start(con[:, :], a["con"]).then_inc(ld_con.sem, 16)
            sp.dma_start(vec[:, :, :], a["vec"]).then_inc(ld_con.sem, 16)
            sp.dma_start(gate_bias[:, :, :], a["bias"]).then_inc(ld_con.sem, 16)
            sp.dma_start(m0[:, :, :], a["m0"]).then_inc(ld_con.sem, 16)
            for l in range(DEPTH):
                if l > 0:
                    sp.wait_ge(*x_mix(l - 1, 8))
                    sp.wait_ge(*nm_xn(2 * l - 1))
                sp.dma_start(lw[:, :], a["lw"][l]).then_inc(ld_lw.sem, 16)
                for k in range(len(EARLY)):
                    load(turns, a["mix"][l, k], SLOT)
                with sp.Fori(0, KT // 2) as j:
                    inner = turns.loop(j, 5)
                    for k in range(5):
                        slab = a["mix"][l, bass.ds(j * 5 + (len(EARLY) + k), 1)].rearrange("a p n -> p (a n)")
                        load(inner, slab, SLOT)
                turns.after(KT // 2, 5)
                for k in range(4):
                    load(turns, a["mix"][l, len(EARLY) + len(LATE) + k], SLOT)
                if l == 0:
                    with sp.Fori(0, NDENSE) as e:
                        inner = turns.loop(e, FT + KT, 1)
                        for f in range(FT):
                            load(inner, a["gu"][bass.ds(e * FT + f, 1)].rearrange("a p n -> p (a n)"), SLOT)
                        for d in range(KT):
                            load(inner, a["down"][bass.ds(e * KT + d, 1)].rearrange("a p n -> p (a n)"), FT * P)
                    turns.after(NDENSE, FT + KT, 1)
                    continue

                def expert(i, e):
                    inner = turns.loop(i, ETURNS, EPAD)
                    for f in range(FT):
                        load(inner, a["egu"][bass.ds(e * FT + f, 1)].rearrange("a p n -> p (a n)"), SLOT)
                    for k in range(DSL):
                        width = D * min(2, FT - 2 * k)
                        load(inner, a["edown"][bass.ds(e * DSL + k, 1), :, 0:width].rearrange("a p n -> p (a n)"), width)

                sp.wait_ge(*rw_y(l))
                sp.dma_start(pcon, a["pcon"]).then_inc(ld_con.sem, 16)
                expert(0, 0)
                sp.wait_ge(*plan_ok(0))
                npass = sp.value_load(plan[0:1, PLAN_N - 1:PLAN_N], min_val=NE, max_val=NE + MAXEXTRA)
                with sp.Fori(1, npass) as i:
                    expert(i, sp.value_load(plan[0:1, bass.ds(i, 1)], min_val=0, max_val=NE - 1))
            sp.wait_ge(*nm_xn(2 * DEPTH))
            sp.dma_start(o["y"], xn[:, :, :]).then_inc(st_y.sem, 16)
            sp.wait_ge(st_y.sem, 16)

        @block.tensor
        def _(pe):
            turns = Turns()
            mm = pe.matmul

            def slab(turns):
                s, n = turns.take()
                pe.wait_ge(slot_ld[s].sem, (n + 1) * 16)
                return s

            def norm(n):
                pe.wait_ge(*nm_sq(n))
                for k in range(KT):
                    last = mm(ps[:, 4, 0:T], C("ones", P), norm_sq[:, k, :], start=(k == 0), stop=(k == KT - 1))
                last.then_inc(nm_ms.sem, 1)
                pe.wait_ge(*nm_xn(n))

            current = [None, None]

            def groups(l, first, end):
                for n in range(first, end):
                    kind, j = GROUPS[n]
                    if n >= 4:
                        pe.wait_ge(*evac(l, n - 3))
                    bank = ps[:, n % 4, :]
                    if kind in ("mi", "mf"):
                        if kind == "mi":
                            pe.wait_ge(ld_lw.sem, 16 * (l + 1))
                        off = LW["if"] + (4 if kind == "mf" else 0)
                        for k in range(KT):
                            last = mm(bank[0:NH, 0:T], lw[:, off + 8 * k:off + 8 * k + 4], xn[:, k, :],
                                      start=(k == 0), stop=(k == KT - 1))
                        last.then_inc(proj.sem, 1)
                        continue
                    tokens = kind in ("mv", "rv")
                    piece, part, is_last = piece_of(kind, j)
                    if current[0] != (l, kind, piece):
                        current[0], current[1] = (l, kind, piece), slab(turns)
                    s = current[1]
                    for k in range(KT):
                        if tokens:
                            c0, m = TOK[part]
                            last = mm(bank[0:m, 0:256], xn[:, k, c0:c0 + m], ring[:, s, 256 * k:256 * k + 256],
                                      start=(k == 0), stop=(k == KT - 1))
                        else:
                            w0 = 256 * k + P * part
                            last = mm(bank[:, 0:T], ring[:, s, w0:w0 + P], xn[:, k, :],
                                      start=(k == 0), stop=(k == KT - 1))
                    if is_last:
                        last.then_inc(slot_fr[s].sem, 1)
                    else:
                        last.then_inc(proj.sem, 1)

            def head_norm(q, src, sq, centre, ones):
                for j in range(4):
                    last = mm(ps[:, 4 + j, 0:T], centre, src[:, j, :], start=True, stop=True)
                    last.then_inc(hn_c.sem, 1)
                for j in range(4):
                    pe.wait_ge(hn_s.sem, 4 * q + j + 1)
                    pe.wait_ge(hn_x.sem, 4 * q + j + 1)
                    mm(ps[:, 4 + j, 0:T], ones, sq[:, j, :], start=True, stop=True).then_inc(hn_v.sem, 1)

            def mlstm_columns(l):
                pe.wait_ge(*gr_ok(l))
                for i, (c0, m) in enumerate(TOK):
                    for r in range(2):
                        last = pe.transpose(ps[0:m, 4, 8 * i + 4 * r:8 * i + 4 * r + 4],
                                            (rows[0:NH, 0, c0:c0 + m], rows[0:NH, 3, c0:c0 + m])[r],
                                            C("ident", NH, NH))
                last.then_inc(ml_col.sem, 1)

            def mlstm_qk(l):
                pe.wait_ge(*xc_ok(l))
                for n in range(8):
                    h, which = n // 2, ("wq", "wk")[n % 2]
                    if n >= 2:
                        pe.wait_ge(*mqk_e(l, n - 1))
                    mm(ps[:, 5 + n % 2, 0:T], lw[:, LW[which] + P * h:LW[which] + P * h + P], xc[:, h, :],
                       start=True, stop=True).then_inc(mqk_p.sem, 1)
                for i, (c0, m) in enumerate(TOK):
                    pe.wait_ge(*mqk_e(l, 8 + i - 1))
                    for h in range(NH):
                        last = mm(ps[0:m, 5 + i % 2, P * h:P * h + P], xc[:, h, c0:c0 + m],
                                  lw[:, LW["wk"] + P * h:LW["wk"] + P * h + P], start=True, stop=True)
                    last.then_inc(mqk_p.sem, 1)

            def mlstm_head(l, h):
                if h == 0:
                    pe.wait_ge(*ml_colv(l))
                    pe.wait_ge(*mqk_e(l, 11))
                    pe.wait_ge(*er_ok(l))
                    pe.wait_ge(*evac(l, 12))
                    pe.wait_ge(ld_c0.sem, 16 * (l + 1))
                else:
                    pe.wait_ge(*ml_h(l, h))
                pick = con[0:NH, CON["sel"] + P * h:CON["sel"] + P * h + P]
                mm(ps[:, 4, 0:T], pick, rows[0:NH, 1, :], start=True, stop=True)
                mm(ps[:, 4, T:T + TS], pick, arow[0:NH, :], start=True, stop=True)
                mm(ps[:, 5, 0:T], pick, rows[0:NH, 2, :], start=True, stop=True).then_inc(ml_bc.sem, 1)
                mm(ps[:, 6, 0:TP], mk[:, h, 0:P], mq[:, h, 0:TP], start=True, stop=True)
                mm(ps[:, 6, TP:TP + P], mk[:, h, P:TP], mq[:, h, P:TP], start=True, stop=True)
                mm(ps[0:TS, 6, TP + P:PW], mk[:, h, TP:T], mq[:, h, TP:T], start=True, stop=True).then_inc(ml_s.sem, 1)
                pe.wait_ge(*ml_pw(l, h + 1))
                for bank, part in ((7, "num"), (4, "den")):
                    def left(i):
                        rows_ = TOK[i][1]
                        return mvt[0:rows_, i, P * h:P * h + P] if part == "num" else C("ones", P, rows_)
                    mm(ps[:, bank, 0:TP], left(0), ml_PW[:, 0:TP], start=True, stop=False, skip_group_check=True)
                    mm(ps[:, bank, P:TP], left(1), ml_PW[:, TP:TP + P], start=False, stop=False,
                       skip_group_check=True)
                    last = mm(ps[:, bank, TP:T], left(2), ml_PW[0:TS, TP + P:PW], start=False, stop=False,
                              skip_group_check=True)
                    if part == "num":
                        for b in range(SB):
                            cs = slice(ST * b, ST * b + ST)
                            mm(ps[:, bank, TP + ST * b:TP + ST * b + ST], C0[:, b, h, :], qa[:, cs],
                               start=False, stop=(b == SB - 1), skip_group_check=True)
                    else:
                        mm(ps[:, bank, TP:T], C("ones", P), nq, start=False, stop=True,
                           skip_group_check=True).then_inc(ml_nd.sem, 1)

            def mlstm_state(l):
                pe.wait_ge(*kdec_ok(l))
                pe.wait_ge(*ml_h(l, 4))
                for h in range(NH):
                    for i in range(2):
                        mm(ps[:, 4, P * h:P * h + P], mkt[:, i, P * h:P * h + P], mvt[:, i, P * h:P * h + P],
                           start=(i == 0), stop=(i == 1))
                for h in range(NH):
                    for i in range(2):
                        last = mm(ps[:, 5, h:h + 1], mkt[:, i, P * h:P * h + P], C("ones", 1),
                                  start=(i == 0), stop=(i == 1))
                last.then_inc(ml_cp.sem, 1)
                for b in range(SB):
                    pe.wait_ge(*ml_kb(l, b + 1))
                    if b >= 2:
                        pe.wait_ge(*ml_sca(l, b - 1))
                    for h in range(NH):
                        mm(ps[:, 6 + b % 2, P * h:P * h + P], kb[0:TS, b % 2, P * h:P * h + P],
                           mvt[0:TS, 2, P * h:P * h + P], start=True, stop=True)
                        last = mm(ps[:, 5, 8 + NH * b + h:9 + NH * b + h], kb[0:TS, b % 2, P * h:P * h + P],
                                  C("ones", 1, TS), start=True, stop=True)
                    last.then_inc(ml_sc.sem, 1)

            def retention_rotate(l):
                pe.wait_ge(*evac(l, 30))
                for j in range(4):
                    mm(ps[:, 4 + j, 0:T], C("swap", P), rqk[:, j, :], start=True, stop=True).then_inc(r_sw.sem, 1)

            def retention_keys(l):
                pe.wait_ge(*r_qr(l))
                for i, (c0, m) in enumerate(TOK):
                    for j in range(2):
                        last = pe.transpose(ps[0:m, 4 + i, P * j:P * j + P], qr[:, 2 + j, c0:c0 + m], C("ident", P))
                    last.then_inc(r_kt.sem, 1)

            def retention_scores(l, h):
                i, p0 = h // 2, DK * (h % 2)
                if h == 0:
                    pe.wait_ge(*r_ktd(l, 3))
                if h >= 2:
                    pe.wait_ge(*r_pw(l, h - 1))
                bank, r = 4 + h % 2, slice(p0, p0 + DK)
                mm(ps[:, bank, 0:TP], qr[r, 2 + i, 0:P], qr[r, i, 0:TP], start=True, stop=True)
                mm(ps[:, bank, TP:TP + P], qr[r, 2 + i, P:TP], qr[r, i, P:TP], start=True, stop=True)
                mm(ps[0:TS, bank, TP + P:PW], qr[r, 2 + i, TP:T], qr[r, i, TP:T], start=True,
                   stop=True).then_inc(r_sc.sem, 1)

            def retention_values(l, h):
                i, p0 = h // 2, DK * (h % 2)
                r = slice(p0, p0 + DK)
                if h == 0:
                    pe.wait_ge(*evac(l, 36))
                    pe.wait_ge(ld_ret.sem, 32 * (l + 1))
                if h >= 2:
                    pe.wait_ge(*r_oe(l, h - 1))
                pe.wait_ge(*r_pw(l, h + 1))
                bank, w = 6 + h % 2, rpw[:, h % 2, :]
                mm(ps[:, bank, 0:TP], rvt[:, 0, P * h:P * h + P], w[:, 0:TP], start=True, stop=False,
                   skip_group_check=True)
                mm(ps[:, bank, P:TP], rvt[:, 1, P * h:P * h + P], w[:, TP:TP + P], start=False, stop=False,
                   skip_group_check=True)
                mm(ps[:, bank, TP:T], rvt[0:TS, 2, P * h:P * h + P], w[0:TS, TP + P:PW], start=False, stop=False,
                   skip_group_check=True)
                for b in range(SB):
                    last = mm(ps[:, bank, TP + ST * b:TP + ST * b + ST], S0_ret[r, b, i, :],
                              qd[r, i, ST * b:ST * b + ST], start=False, stop=(b == SB - 1), skip_group_check=True)
                last.then_inc(r_o.sem, 1)

            def retention_state(l):
                pe.wait_ge(*r_pw(l, 4))
                pe.wait_ge(*r_oe(l, 4))
                for h in range(NH):
                    i, p0 = h // 2, DK * (h % 2)
                    for t in range(2):
                        last = mm(ps[p0:p0 + DK, 4, P * i:P * i + P], ktd[:, t, DK * h:DK * h + DK],
                                  rvt[:, t, P * h:P * h + P], start=(t == 0), stop=(t == 1))
                last.then_inc(r_sp.sem, 1)
                for b in range(SB):
                    pe.wait_ge(*r_kb(l, b + 1))
                    if b >= 2:
                        pe.wait_ge(*r_ssa(l, b - 1))
                    for h in range(NH):
                        i, p0 = h // 2, DK * (h % 2)
                        last = mm(ps[p0:p0 + DK, 5 + b % 2, P * i:P * i + P], rkb[0:TS, b % 2, DK * h:DK * h + DK],
                                  rvt[0:TS, 2, P * h:P * h + P], start=True, stop=True)
                    last.then_inc(r_ss.sem, 1)

            def rwkv_prepare(l):
                pe.wait_ge(*w_thl(l))
                pe.wait_ge(*hn_y(l, 2))
                for n in range(12):
                    which, j = n // 4, n % 4
                    if n >= 2:
                        pe.wait_ge(*w_lorae(l, n - 1))
                    r = (slice(0, DK), slice(DK, P), slice(0, P))[which]
                    off = LW["g2" if which == 2 else "lora"] + P * j
                    mm(ps[:, 4 + n % 2, 0:T], lw[r, off:off + P], (lora_g if which == 2 else lora_in)[r, :],
                       start=True, stop=True).then_inc(w_lora.sem, 1)
                pe.wait_ge(*w_lorae(l, 12))
                pe.wait_ge(*w_sq(l))
                for j in range(4):
                    mm(ps[:, 4 + j, 0:T], C("ones64", P), rw_e1[:, j, :], start=True, stop=True)\
                        .then_inc(w_ss.sem, 1)
                pe.wait_ge(*w_rk(l))
                for j in range(4):
                    mm(ps[:, 4 + j, 0:T], C("ones64", P), rw_e2[:, j, :], start=True, stop=True)\
                        .then_inc(w_bo.sem, 1)
                for c in range(NC):
                    w = CH if c < NC - 1 else TS
                    for j in range(4):
                        last = pe.transpose(ps[0:w, c % 4, P * j:P * j + P], zs[:, 8 + j, CH * c:CH * c + w],
                                            C("ident", P))
                    last.then_inc(w_vt.sem, 1)
                    if c == NC - 2:
                        pe.wait_ge(*w_vte(l, 1))
                pe.wait_ge(*w_vte(l, 5))

            def rwkv_gram(l):
                pe.wait_ge(*w_pre(l))
                for c in range(NC):
                    for p in range(2):
                        n, r = 2 * c + p, slice(CH * p, CH * p + CH)
                        if n >= 4:
                            pe.wait_ge(*w_g1e(l, n - 3))
                        for j in range(NP4):
                            last = mm(ps[:, n % 4, P * j:P * j + P], BK[r, j, c, :], KR[r, j, c, :],
                                      start=True, stop=True)
                        last.then_inc(w_g1.sem, 1)
                for n in range(6):
                    p, c0 = n % 2, 2 * (n // 2)
                    r = slice(CH * p, CH * p + CH)
                    if n >= 4:
                        pe.wait_ge(*w_g2e(l, n - 3))
                    for c in range(c0, min(c0 + 2, NC)):
                        for j in range(NP4):
                            at_ = 256 * (c - c0) + CH * j
                            last = mm(ps[r, 4 + n % 4, at_:at_ + CH], KR[r, j, c, 0:CH], BK[r, j, c, 0:CH],
                                      start=True, stop=True)
                    last.then_inc(w_g2.sem, 1)

            def rwkv_invert(l):
                pe.wait_ge(*w_x0(l))
                pe.wait_ge(*w_g2e(l, 6))
                pe.wait_ge(*w_g1e(l, 10))
                for m in range(len(LEVELS)):
                    for g in range(3):
                        us = range(8 * g, min(8 * g + 8, NU))
                        if m > 0:
                            pe.wait_ge(*w_te(l, 3 * m))
                            pe.wait_ge(*w_to(l, 2 * m))
                        for u in us:
                            last = mm(ps[:, g, CH * (u - 8 * g):CH * (u - 8 * g) + CH], Abd[:, u, :], Xc[:, u, :],
                                      start=True, stop=True)
                        last.then_inc(w_y.sem, 1)
                    for g in range(3):
                        us = range(8 * g, min(8 * g + 8, NU))
                        pe.wait_ge(*w_ye(l, 3 * m + g + 1))
                        for u in us:
                            last = mm(ps[:, 3 + g, CH * (u - 8 * g):CH * (u - 8 * g) + CH], Xbd[:, u, :],
                                      Yc[:, u, :], start=True, stop=True)
                        last.then_inc(w_p.sem, 1)
                    if m < len(LEVELS) - 1:
                        for q in range(5):
                            pe.wait_ge(*w_pe(l, 3 * m + q // 2 + 1))
                            for k in range(4):
                                u = 4 * q + k
                                last = pe.transpose(ps[0:CH, (6, 7, 0, 1, 2)[q], P * k:P * k + P], Xc[:, u, :],
                                                    C("ident", P))
                            last.then_inc(w_t.sem, 1)

            def rwkv_tokens(l):
                pe.wait_ge(*w_pe(l, 15))
                for c in range(NC):
                    for j in range(NP4):
                        last = pe.transpose(ps[:, c, P * j:P * j + P], BK[:, j, c, :], C("ident", P))
                    last.then_inc(w_bt.sem, 1)

            def head_cols(h):
                return slice(CH * h, CH * h + CH)

            def rwkv_chunk(l, c):
                sample = c == NC - 1
                if c == 0:
                    pe.wait_ge(*w_xt(l, 2))
                    pe.wait_ge(*w_bte(l, 5))
                    pe.wait_ge(*w_sz(l))
                if sample:
                    pe.wait_ge(ld_rw.sem, 16 * (l + 1))
                    for j in range(NP4):
                        for b in range(SB):
                            dst = ps[:, 6, :].rearrange("p (j q n) -> p j q n", j=8, q=2)[:, j, :, ST * b:ST * b + ST]
                            src = KR[:, j, c, :].rearrange("p (q n) -> p q n", q=2)[:, :, ST * b:ST * b + ST]
                            last = mm(dst, S0bd[:, b, j, :], src, start=True, stop=True)
                    last.then_inc(w_cx.sem, 1)
                for h in range(2 * NP4):
                    j, p = h // 2, h % 2
                    last = mm(ps[0:CH, 0, head_cols(h)], G[:, c, p, P * j:P * j + CH], UV[:, c, head_cols(h)],
                              start=(h == 0), stop=False, skip_group_check=True)
                if not sample:
                    if c > 0:
                        pe.wait_ge(*w_su(l, c))
                    for j in range(NP4):
                        last = mm(ps[0:CH, 0, P * j:P * j + P], KR[:, j, c, 0:CH], Sbd[:, j, :], start=False,
                                  stop=(j == NP4 - 1), skip_group_check=True)
                last.then_inc(w_r.sem, 1)
                obank = 4 + c % 2
                if c >= 2:
                    pe.wait_ge(*w_oe(l, c - 1))
                if sample:
                    pe.wait_ge(*w_cxe(l))
                    for j in range(NP4):
                        last = pe.transpose(ps[0:TS, 3, P * j:P * j + P], CX[:, j, 0, :], C("ident", P))
                    last.then_inc(w_ct.sem, 1)
                else:
                    for j in range(NP4):
                        last = mm(ps[:, obank, CH * j:CH * j + CH], Sbd[:, j, :], KR[:, j, c, CH:2 * CH],
                                  start=(j == 0), stop=False, skip_group_check=True)
                    last.then_inc(w_oc.sem, 1)
                pe.wait_ge(*w_rn(l, c + 1))
                for h in range(2 * NP4):
                    j, p = h // 2, h % 2
                    last = mm(ps[0:CH, 1, head_cols(h)], XT[0:CH, NP4 * c + j, CH * p:CH * p + CH],
                              Rn[0:CH, head_cols(h)], start=True, stop=True)
                last.then_inc(w_u.sem, 1)
                pe.wait_ge(*w_ue(l, c + 1))
                if not sample:
                    for j in range(NP4):
                        last = mm(ps[:, 2, P * j:P * j + P], BKt[:, c, P * j:P * j + P], UV[:, c, P * j:P * j + P],
                                  start=True, stop=True)
                    last.then_inc(w_s.sem, 1)
                for h in range(2 * NP4):
                    j, p = h // 2, h % 2
                    last = mm(ps[CH * p:CH * p + CH, obank, CH * j:CH * j + CH], UV[:, c, head_cols(h)],
                              G[:, c, p, P * j + CH:P * j + P], start=(sample and h < 2), stop=True,
                              skip_group_check=True)
                last.then_inc(w_ob.sem, 1)

            def rwkv_sample_state(l):
                for b in range(SB):
                    pe.wait_ge(*w_kb(l, b + 1))
                    if b >= 2:
                        pe.wait_ge(*w_sta(l, b - 1))
                    for j in range(NP4):
                        last = mm(ps[:, 1 + b % 2, P * j:P * j + P], KBm[b % 2][:, P * j:P * j + P],
                                  UV[:, NC - 1, P * j:P * j + P], start=True, stop=True)
                    last.then_inc(w_st.sem, 1)

            def closing(l):
                pe.wait_ge(*hn_y(l, 3))
                pe.wait_ge(*rw_y(l))
                pe.wait_ge(*w_sta(l, 8))
                with pe.Fori(0, KT // 2) as i:
                    inner = turns.loop(i, 5)
                    for n in range(3):
                        s = slab(inner)
                        for dd in range(2):
                            q = 2 * n + dd
                            pe.wait_ge(f_zs.sem, i * 6 + (24 * l + q + 1))
                            for k in range(KT):
                                w0 = 256 * k + P * dd
                                last = mm(ps[:, q % 3, 0:T], ring[:, s, w0:w0 + P], xn[:, k, :],
                                          start=(k == 0), stop=(k == KT - 1))
                            last.then_inc((slot_fr[s] if dd else f_zg).sem, 1)
                    for dd in range(2):
                        s = slab(inner)
                        for n, y in enumerate((y_ret, y_ml, y_rw)):
                            q = 3 * dd + n
                            pe.wait_ge(f_gm.sem, i * 6 + (24 * l + q + 1))
                            for k in range(4):
                                w0 = P * (4 * n + k)
                                last = mm(ps[:, 3 + q % 3, 0:T], ring[:, s, w0:w0 + P], y[:, k, :],
                                          start=(k == 0), stop=(k == 3))
                            last.then_inc((slot_fr[s] if n == 2 else f_br).sem, 1)
                turns.after(KT // 2, 5)
                pe.wait_ge(f_gm.sem, 3 + 24 * (l + 1))
                for d in range(KT):
                    if d % 2 == 0:
                        s = slab(turns)
                    if d >= 2:
                        pe.wait_ge(*x_mix(l, d - 1))
                    for k in range(KT):
                        w0 = 256 * k + P * (d % 2)
                        last = mm(ps[:, 6 + d % 2, 0:T], ring[:, s, w0:w0 + P], mixed[:, k, :],
                                  start=(k == 0), stop=(k == KT - 1))
                    last.then_inc((slot_fr[s] if d % 2 else f_out).sem, 1)

            def route():
                for i, (c0, m) in enumerate(TOK):
                    for k in range(KT):
                        last = mm(ps[0:m, 6, NE * i:NE * i + NE], xn[:, k, c0:c0 + m],
                                  lw[:, LW["router"] + NE * k:LW["router"] + NE * k + NE],
                                  start=(k == 0), stop=(k == KT - 1))
                last.then_inc(rt_lg.sem, 1)
                for n in range(6):
                    c0, m = TOK[n // 2]
                    for k in range(4):
                        last = pe.transpose(ps[0:m, n, P * k:P * k + P], xn[:, 4 * (n % 2) + k, c0:c0 + m], C("ident", P))
                    last.then_inc(xt_p.sem, 1)
                pe.wait_ge(ld_con.sem, 80)
                pe.wait_ge(*rt_sel(0))
                for i, (c0, m) in enumerate(TOK):
                    for k in range(i + 1):
                        mask = PCON("tri", m, TOK[k][1]) if k == i else C("ones", m, TOK[k][1])
                        mm(ps[0:m, 7, NE * i:NE * i + NE], mask, gt[0:TOK[k][1], k, :], start=(k == 0), stop=(k == i))
                for k, (c0, m) in enumerate(TOK):
                    last = mm(ps[0:1, 7, 32:32 + NE], C("ones", 1, m), gt[0:m, k, :], start=(k == 0), stop=(k == 2))
                last.then_inc(rt_pos.sem, 1)
                pe.wait_ge(*rt_cb(0))
                for bank, src in ((6, ex), (7, posn)):
                    for i, (c0, m) in enumerate(TOK):
                        last = pe.transpose(ps[0:NE, bank, c0:c0 + m], src[0:m, i, :], C("ident", m, m))
                last.then_inc(rt_ct.sem, 1)

            def broadcast_rows():
                pe.wait_ge(*rt_cr(0))
                for n in range(2 * NE):
                    e, which = n // 2, n % 2
                    if e >= 2:
                        pe.wait_ge((rt_cbe, rt_pbe)[which].sem, e - 1)
                    mm(ps[:, 2 * which + e % 2, 0:T], con[0:NE, CON["sel"] + P * e:CON["sel"] + P * e + P],
                       (crow, prow)[which][0:NE, :], start=True, stop=True).then_inc(rt_bc.sem, 1)
                pe.wait_ge(rt_cbe.sem, NE)
                pe.wait_ge(rt_pbe.sem, NE)

            def gather(n):
                pe.wait_ge(in_ok.sem, n + 1)
                for k in range(KT):
                    for i, (c0, m) in enumerate(TOK):
                        last = mm(ps[:, 4 + k // 4, P * (k % 4):P * (k % 4) + MB], xt[0:m, i, P * k:P * k + P],
                                  pick_in[0:m, i, :], start=(i == 0), stop=(i == 2))
                    if k % 4 == 3:
                        last.then_inc(ga_p.sem, 1)

            def scatter(n):
                pe.wait_ge(yg_a.sem, n + 1)
                pe.wait_ge(yg_d.sem, n + 1)
                pe.wait_ge(out_ok.sem, n + 1)
                for d in range(KT):
                    if d >= 2:
                        pe.wait_ge(sc_e.sem, n * KT + (d - 1))
                    mm(ps[:, 4 + d % 2, 0:T], yg[:, P * d:P * d + P], pick_out, start=True, stop=True)\
                        .then_inc(sc_p.sem, 1)

            def experts():
                base = FT * NDENSE + CREDIT_H
                pe.wait_ge(xt_a.sem, 3)
                pe.wait_ge(xt_d.sem, 3)
                gather(0)
                broadcast_rows()
                pe.wait_ge(*plan_ok(0))
                npass = pe.value_load(plan[0:1, PLAN_N - 1:PLAN_N], min_val=NE, max_val=NE + MAXEXTRA)
                with pe.Fori(0, npass) as i:
                    inner = turns.loop(i, ETURNS, EPAD)
                    pe.wait_ge(ga_a.sem, i + 1)
                    pe.wait_ge(ga_d.sem, i + 1)
                    for f in range(FT):
                        if f == 3:
                            scatter(i)
                        s = slab(inner)
                        pe.wait_ge(h_done.sem, i * FT + (base + max(f - 1, 0)))
                        for w in range(2):
                            for k in range(KT):
                                w0 = P * (KT * w + k)
                                last = mm(ps[:, 2 * (f % 2) + w, 0:MB], ring[:, s, w0:w0 + P], xg[:, k, :],
                                          start=(k == 0), stop=(k == KT - 1))
                            last.then_inc((slot_fr[s] if w else g_done).sem, 1)
                    pe.wait_ge(sc_e.sem, i * KT + KT)
                    gather(i + 1)
                    for f in range(FT):
                        if f % 2 == 0:
                            s = slab(inner)
                        pe.wait_ge(h_done.sem, i * FT + (base + f + 1))
                        for w in range(2):
                            w0 = D * (f % 2) + 512 * w
                            last = mm(ps[:, 6 + w, :], ehid[:, f, :], ring[:, s, w0:w0 + 512],
                                      start=(f == 0), stop=(f == FT - 1))
                            if f == FT - 1 and w == 0:
                                last.then_inc(do_p.sem, 1)
                        if f % 2 == 1 or f == FT - 1:
                            last.then_inc(slot_fr[s].sem, 1)
                pe.wait_ge(ga_a.sem, npass + 1)
                pe.wait_ge(ga_d.sem, npass + 1)
                scatter(npass)

            def feed_forward():
                with pe.Fori(0, NDENSE) as e:
                    inner = turns.loop(e, FT + KT, 1)
                    for f in range(FT):
                        s = slab(inner)
                        pe.wait_ge(h_done.sem, e * FT + (f + (2 if f < 2 else 1)))
                        for w in range(2):
                            for k in range(KT):
                                w0 = P * (KT * w + k)
                                last = mm(ps[:, 2 * (f % 3) + w, 0:T], ring[:, s, w0:w0 + P], xn[:, k, :],
                                          start=(k == 0), stop=(k == KT - 1))
                            last.then_inc((slot_fr[s] if w else g_done).sem, 1)
                    for d in range(KT):
                        s = slab(inner)
                        pe.wait_ge(y_done.sem, e * KT + (d + 1))
                        for f in range(FT):
                            if d == 0:
                                pe.wait_ge(h_done.sem, e * FT + (CREDIT_H + f + 1))
                            last = mm(ps[:, 6 + d % 2, 0:T], ring[:, s, P * f:P * f + P], hid[:, f, :],
                                      start=(f == 0), stop=(f == FT - 1))
                        last.then_inc(slot_fr[s].sem, 1)
                turns.after(NDENSE, FT + KT, 1)

            pe.wait_ge(ld_con.sem, 64)
            for l in range(DEPTH):
                norm(2 * l)
                groups(l, 0, 26)
                mlstm_columns(l)
                mlstm_qk(l)
                for h in range(NH):
                    mlstm_head(l, h)
                    groups(l, 26 + 4 * h, 30 + 4 * h)
                mlstm_state(l)
                groups(l, 42, NG)
                pe.wait_ge(*ml_sca(l, 8))
                pe.wait_ge(*ml_cpe(l))
                pe.wait_ge(*ml_out(l))
                head_norm(3 * l, ml_o, ml_sq, C("cent128", P), C("ones", P))
                pe.wait_ge(*hn_r(l, 1))
                retention_rotate(l)
                retention_keys(l)
                retention_scores(l, 0)
                for h in range(NH):
                    if h < NH - 1:
                        retention_scores(l, h + 1)
                    retention_values(l, h)
                retention_state(l)
                pe.wait_ge(*r_ssa(l, 8))
                pe.wait_ge(*r_spe(l))
                head_norm(3 * l + 1, ret_o, ret_sq, C("cent128", P), C("ones", P))
                rwkv_prepare(l)
                rwkv_gram(l)
                rwkv_invert(l)
                rwkv_tokens(l)
                for c in range(NC):
                    rwkv_chunk(l, c)
                rwkv_sample_state(l)
                pe.wait_ge(*w_oe(l, 5))
                head_norm(3 * l + 2, rw_o, rw_sq, C("cent64", P), C("ones64", P))
                closing(l)
                norm(2 * l + 1)
                if l == 0:
                    feed_forward()
                else:
                    route()
                    experts()
            norm(2 * DEPTH)

        @block.scalar
        def _(act):
            turns = Turns()
            A = act.activation
            links = [0]

            def link(ins):
                links[0] += 1
                ins.then_inc(ach.sem, 1)
                act.wait_ge(ach.sem, links[0])

            def norm(n):
                if n == 0:
                    act.wait_ge(ld_x.sem, 16)
                elif n % 2 == 1:
                    act.wait_ge(*x_mix(n // 2, 8))
                    act.wait_ge(st_rw.sem, 32 * (n // 2 + 1))
                elif n == 2:
                    act.wait_ge(y_done.sem, CREDIT_Y + KT * NDENSE)
                A(norm_sq, X[:, :, :], ACT.Square).then_inc(nm_sq.sem, 1)
                act.wait_ge(*nm_rec(n))
                A(rstd[:, :], rstd[:, :], ACT.Sqrt).then_inc(nm_rstd.sem, 1)

            current = [None, 0, 0]

            def projections(l, first, end):
                for n in range(first, end):
                    kind, j = GROUPS[n]
                    piece, part, is_last = piece_of(kind, j)
                    if piece is not None and current[0] != (l, kind, piece):
                        current[0] = (l, kind, piece)
                        current[1:] = turns.take()
                    if is_last:
                        act.wait_ge(slot_fr[current[1]].sem, current[2] + 1)
                    else:
                        act.wait_ge(*proj(l, sum(not piece_of(*g)[2] for g in GROUPS[:n + 1])))
                    src = ps[:, n % 4, 0:T]
                    if kind == "mx":
                        A(mxp[:, j, XPAD:XPAD + TP], src[:, 0:TP], ACT.Copy)
                        dst = mxp[:, j, XPAD + TP:].rearrange("p (b t) -> p b t", b=SB)[:, :, XPAD:]
                        last = A(dst, seq4(src[:, TP:T]), ACT.Copy)
                    elif kind == "zrw":
                        A(z[:, j, 1:1 + TP], src[:, 0:TP], ACT.Copy)
                        dst = z[:, j, 1 + TP:].rearrange("p (b t) -> p b t", b=SB)[:, :, 1:]
                        last = A(dst, seq4(src[:, TP:T]), ACT.Copy)
                    elif kind in ("mi", "mf"):
                        w = 0 if kind == "mi" else 1
                        last = A(rows[0:NH, w, :], src[0:NH, :], ACT.Identity, bias=gate_bias[:, l, w:w + 1])
                    elif kind in ("mv", "rv"):
                        m = TOK[part][1]
                        dst = (mvt if kind == "mv" else rvt)[0:m, part, 256 * piece:256 * piece + 256]
                        last = A(dst, ps[0:m, n % 4, 0:256], ACT.Copy)
                    elif kind in ("rq", "rk"):
                        last = A(rqk[:, j + (2 if kind == "rk" else 0), :], src, ACT.Copy,
                                 scale=1.0 if kind == "rq" else DK ** -0.5)
                    elif kind == "mo":
                        last = A(y_ml[:, j, :], src, ACT.Sigmoid)
                    else:
                        last = A(y_ret[:, j, :], src, ACT.Silu)
                    last.then_inc(evac.sem, 1)

            def head_norm(q, src, sq):
                for j in range(4):
                    act.wait_ge(hn_x.sem, 4 * q + j + 1)
                    A(sq[:, j, :], src[:, j, :], ACT.Square).then_inc(hn_s.sem, 1)
                act.wait_ge(*hn_r(0, q + 1))
                A(sq, sq, ACT.Sqrt).then_inc(hn_q.sem, 1)

            def mlstm_gates(l):
                act.wait_ge(*u_abs(l))
                link(A(rows[0:NH, 2, :], rows[0:NH, 2, :], ACT.Exp, scale=-1.0))
                A(rows[0:NH, 2, :], rows[0:NH, 2, :], ACT.Ln, bias=1.0).then_inc(u_exp.sem, 1)
                act.wait_ge(*lf_ok(l))
                A(rows[0:NH, 3, :], rows[0:NH, 3, :], ACT.Exp)
                A(arow[0:NH, :], arow[0:NH, :], ACT.Exp).then_inc(gr_ok.sem, 1)
                A(rows[0:NH, 2, :], rows[0:NH, 2, :], ACT.Exp, scale=-1.0).then_inc(er_ok.sem, 1)

            def mlstm_qk(l):
                for n in range(11):
                    act.wait_ge(*mqk_p(l, n + 1))
                    if n < 8:
                        h = n // 2
                        last = A((mq, mk)[n % 2][:, h, :], ps[:, 5 + n % 2, 0:T], ACT.Copy,
                                 scale=(1.0, P ** -0.5)[n % 2])
                    else:
                        m = TOK[n - 8][1]
                        last = A(mkt[0:m, n - 8, :], ps[0:m, 5 + n % 2, :], ACT.Copy, scale=P ** -0.5)
                    last.then_inc(mqk_e.sem, 1)

            def mlstm_head(l, h):
                act.wait_ge(*ml_wl(l, h + 1))
                A(ml_W[:, 0:TP + P], ml_W[:, 0:TP + P], ACT.Exp)
                A(ml_W[0:TS, TP + P:PW], ml_W[0:TS, TP + P:PW], ACT.Exp).then_inc(ml_ex.sem, 1)
                act.wait_ge(*ml_nd(l, h + 1))
                A(ml_den, ps[:, 4, 0:T], ACT.Abs).then_inc(ml_ad.sem, 1)

            def mlstm_state(l):
                act.wait_ge(*ml_cp(l))
                if l > 0:
                    act.wait_ge(st_ml.sem, 64 * l)
                A(Cp, ps[:, 4, :], ACT.Copy)
                A(n_out[:, 0:NH], ps[:, 5, 0:NH], ACT.Copy).then_inc(ml_cpe.sem, 1)

            def retention(l):
                for h in range(NH):
                    act.wait_ge(*r_o(l, h + 1))
                    A(ret_o[:, h, :], ps[:, 6 + h % 2, 0:T], ACT.Copy).then_inc(r_oe.sem, 1)
                act.wait_ge(*r_sp(l))
                A(Sp_ret, ps[:, 4, 0:256], ACT.Copy).then_inc(r_spe.sem, 1)

            def rwkv_prepare(l):
                act.wait_ge(*w_zs(l))
                A(lora_in[0:DK, :], zs[0:DK, 12, :], ACT.Tanh)
                A(lora_in[DK:P, :], zs[DK:P, 12, :], ACT.Copy)
                A(lora_g, zs[:, 13, :], ACT.Sigmoid).then_inc(w_thl.sem, 1)
                act.wait_ge(st_ret.sem, 32 * (l + 1))
                for n in range(12):
                    which, j = n // 4, n % 4
                    act.wait_ge(*w_lora(l, n + 1))
                    src = ps[:, 4 + n % 2, 0:T]
                    if which == 2:
                        last = A(rw_g[:, j, :], src, ACT.Copy)
                    else:
                        last = A((rw_lw, rw_a)[which][:, j, :], src, ACT.Sigmoid,
                                 bias=V(l, ("w0", "a0")[which], j))
                    last.then_inc(w_lorae.sem, 1)
                act.wait_ge(*w_ssr(l))
                A(rw_e1, rw_e1, ACT.Sqrt).then_inc(w_ssq.sem, 1)
                act.wait_ge(*w_F(l))
                A(rw_e2, rw_e2, ACT.Exp)
                A(rw_lw, rw_e1, ACT.Exp, scale=-1.0)
                A(rw_e1, rw_e1, ACT.Exp).then_inc(w_E.sem, 1)
                for c in range(NC):
                    act.wait_ge(*w_vt(l, c + 1))
                    if c == 0:
                        act.wait_ge(*w_zuv(l, 4))
                    w = CH if c < NC - 1 else TS
                    A(UV[CH:CH + w, c, :], ps[0:w, c % 4, :], ACT.Copy).then_inc(w_vte.sem, 1)

            def rwkv_invert(l):
                for m in range(len(LEVELS)):
                    for g in range(3):
                        n = min(8, NU - 8 * g)
                        act.wait_ge(*w_y(l, 3 * m + g + 1))
                        A(Yc[:, 8 * g:8 * g + n, :], ps[:, g, 0:CH * n].rearrange("p (a b) -> p a b", a=n),
                          ACT.Copy).then_inc(w_ye.sem, 1)
                    if m < len(LEVELS) - 1:
                        for q in (0, 2, 4):
                            act.wait_ge(*w_t(l, 5 * m + q + 1))
                            src = ps[0:CH, (6, 7, 0, 1, 2)[q], :].rearrange("p (a b) -> p a b", a=4)
                            A(Xbd[0:CH, 4 * q:4 * q + 4, 0:CH], src[:, :, 0:CH], ACT.Copy)
                            A(Xbd[CH:P, 4 * q:4 * q + 4, CH:P], src[:, :, CH:P], ACT.Copy).then_inc(w_te.sem, 1)
                act.wait_ge(*w_pe(l, 15))
                A(XT[0:CH, :, 0:CH], Xc[0:CH, :, :], ACT.Copy).then_inc(w_xt.sem, 1)
                for c in range(NC):
                    act.wait_ge(*w_bt(l, c + 1))
                    A(BKt[:, c, :], ps[:, c, :], ACT.Copy).then_inc(w_bte.sem, 1)

            def rwkv_chunks(l):
                for c in range(NC):
                    if c == NC - 1:
                        act.wait_ge(*w_cx(l))
                        A(CX, ps[:, 6, 0:256].rearrange("p (j q n) -> p j q n", j=4, q=2), ACT.Copy)\
                            .then_inc(w_cxe.sem, 1)
                    act.wait_ge(*w_u(l, c + 1))
                    A(UV[0:CH, c, :], ps[0:CH, 1, :], ACT.Copy).then_inc(w_ue.sem, 1)
                    if c < NC - 1:
                        act.wait_ge(*w_ob(l, c + 1))
                        A(rw_o[:, :, CH * c:CH * c + CH],
                          ps[:, 4 + c % 2, 0:256].rearrange("p (a b) -> p a b", a=4), ACT.Copy).then_inc(w_oe.sem, 1)

            def closing(l):
                with act.Fori(0, KT // 2) as i:
                    inner = turns.loop(i, 5)
                    for n in range(3):
                        s, used = inner.take()
                        for dd in range(2):
                            q = 2 * n + dd
                            if dd:
                                act.wait_ge(slot_fr[s].sem, used + 1)
                            else:
                                act.wait_ge(f_zg.sem, i * 3 + (12 * l + n + 1))
                            act.wait_ge(f_mul.sem, i * 6 + (24 * l + 3 * dd + n + 1))
                            A(gates[:, q, :], ps[:, q % 3, 0:T], ACT.Sigmoid).then_inc(f_zs.sem, 1)
                turns.after(KT // 2, 5)
                turns.pass_over(len(OUTS))

            def feed_forward():
                with act.Fori(0, NDENSE) as e:
                    for f in range(FT):
                        act.wait_ge(g_done.sem, e * FT + (f + 1))
                        A(sil[:, f % 3, :], ps[:, 2 * (f % 3), 0:T], ACT.Silu).then_inc(s_done.sem, 1)
                turns.after(NDENSE, FT + KT, 1)

            def gathered(n):
                act.wait_ge(ga_p.sem, n * 2 + 1)
                A(xg[:, 0:4, :], ps[:, 4, :].rearrange("p (k n) -> p k n", k=4), ACT.Copy).then_inc(ga_a.sem, 1)

            def experts():
                act.wait_ge(*rt_e(0))
                A(ex, ex, ACT.Exp).then_inc(rt_ex.sem, 1)
                for n in (0, 2, 4):
                    act.wait_ge(xt_p.sem, n + 1)
                    m = TOK[n // 2][1]
                    A(xt[0:m, n // 2, 0:512], ps[0:m, n, :], ACT.Copy).then_inc(xt_a.sem, 1)
                gathered(0)
                for e in range(NE):
                    act.wait_ge(rt_bc.sem, 2 * e + 1)
                    A(comb[:, e, :], ps[:, e % 2, 0:T], ACT.Copy).then_inc(rt_cbe.sem, 1)
                act.wait_ge(*plan_ok(0))
                npass = act.value_load(plan[0:1, PLAN_N - 1:PLAN_N], min_val=NE, max_val=NE + MAXEXTRA)
                with act.Fori(0, npass) as i:
                    for f in range(FT):
                        act.wait_ge(g_done.sem, i * FT + (FT * NDENSE + f + 1))
                        A(esil[:, f % 3, :], ps[:, 2 * (f % 2), 0:MB], ACT.Silu).then_inc(s_done.sem, 1)
                    gathered(i + 1)
                    act.wait_ge(do_p.sem, i + 1)
                    A(yg[:, 0:512], ps[:, 6, :], ACT.Copy).then_inc(yg_a.sem, 1)
                act.wait_ge(sc_e.sem, npass * KT + KT)

            act.wait_ge(ld_con.sem, 64)
            for _ in range(3):
                act.sem_inc(f_zs.sem, 1)
            for l in range(DEPTH):
                norm(2 * l)
                projections(l, 0, 16)
                act.wait_ge(*conv_acc(l))
                A(xc, xc, ACT.Silu).then_inc(xc_ok.sem, 1)
                projections(l, 16, 20)
                mlstm_gates(l)
                projections(l, 20, 26)
                mlstm_qk(l)
                for h in range(NH):
                    mlstm_head(l, h)
                    projections(l, 26 + 4 * h, 30 + 4 * h)
                mlstm_state(l)
                projections(l, 42, NG)
                head_norm(3 * l, ml_o, ml_sq)
                retention(l)
                head_norm(3 * l + 1, ret_o, ret_sq)
                rwkv_prepare(l)
                rwkv_invert(l)
                rwkv_chunks(l)
                head_norm(3 * l + 2, rw_o, rw_sq)
                closing(l)
                norm(2 * l + 1)
                if l == 0:
                    feed_forward()
                else:
                    experts()
            norm(2 * DEPTH)

        @block.vector
        def _(dve):
            turns = Turns()
            links = [0]
            TT, TSC, STT = dve.tensor_tensor, dve.tensor_scalar, dve.scalar_tensor_tensor
            MUL, ADD, SUB, MAX, MIN = ALU.mult, ALU.add, ALU.subtract, ALU.max, ALU.min

            def link(ins):
                links[0] += 1
                ins.then_inc(dch.sem, 1)
                dve.wait_ge(dch.sem, links[0])

            def mid(ap, n):
                return ap.unsqueeze(1).broadcast_to([ap.shape[0], n, ap.shape[1]])

            def end(ap, n):
                return ap.unsqueeze(len(ap.shape)).broadcast_to(list(ap.shape) + [n])

            def norm(n):
                l = min(n // 2, DEPTH - 1)
                gain = "final" if n == 2 * DEPTH else ("norm_mix", "norm_ffn")[n % 2]
                dve.wait_ge(*nm_ms(n))
                link(TSC(rstd[:, :], ps[:, 4, 0:T], 1.0 / D, NORM_EPS, MUL, ADD))
                dve.reciprocal(rstd[:, :], rstd[:, :]).then_inc(nm_rec.sem, 1)
                dve.wait_ge(*nm_rstd(n))
                for k in range(KT):
                    last = STT(xn[:, k, :], X[:, k, :], V(l, gain, k), rstd[:, :], MUL, MUL)
                last.then_inc(nm_xn.sem, 1)

            def head_norm(q, src, sq, n, eps, finish):
                for j in range(4):
                    dve.wait_ge(hn_c.sem, 4 * q + j + 1)
                    dve.tensor_copy(src[:, j, :], ps[:, 4 + j, 0:T]).then_inc(hn_x.sem, 1)
                for j in range(4):
                    dve.wait_ge(hn_v.sem, 4 * q + j + 1)
                    last = TSC(sq[:, j, :], ps[:, 4 + j, 0:T], 1.0 / n, eps, MUL, ADD)
                link(last)
                dve.reciprocal(sq, sq).then_inc(hn_r.sem, 1)
                dve.wait_ge(*hn_q(0, q + 1))
                finish()

            def histories(l):
                dve.wait_ge(ld_hist.sem, 32 * (l + 1))
                dve.memset(mxp[:, :, 0:XPAD], 0.0)
                dve.memset(z[:, :, 0:1], 0.0)
                for j in range(4):
                    dst = mxp[:, j, XPAD + TP:].rearrange("p (b t) -> p b t", b=SB)[:, :, 0:XPAD]
                    src = hist[:, j * SB * XPAD:(j + 1) * SB * XPAD].rearrange("p (b t) -> p b t", b=SB)
                    dve.tensor_copy(dst, src)
                zc = z[:, :, 1 + TP:].rearrange("p j (b t) -> p j b t", b=SB)[:, :, :, 0]
                link(dve.tensor_copy(zc, prev[:, :].rearrange("p (j b) -> p j b", b=SB)))

            def conv(l):
                for j in range(4):
                    dve.wait_ge(*evac(l, j + 1))
                    smp = mxp[:, j, XPAD + TP:].rearrange("p (b t) -> p b t", b=SB)
                    for k in range(CONV):
                        w = V(l, "conv_w", 4 * k + j)
                        accp, accs = xc[:, j, 0:TP], seq4(xc[:, j, TP:T])
                        inp, ins = mxp[:, j, k:k + TP], smp[:, :, k:k + ST]
                        if k == 0:
                            TSC(accp, inp, w, V(l, "conv_b", j), MUL, ADD)
                            last = TSC(accs, ins, w, V(l, "conv_b", j), MUL, ADD)
                        else:
                            STT(accp, inp, w, accp, MUL, ADD)
                            last = STT(accs, ins, w, accs, MUL, ADD)
                        if k < CONV - 1:
                            link(last)
                last.then_inc(conv_acc.sem, 1)
                if l > 0:
                    dve.wait_ge(st_small.sem, 32 * l)
                dve.tensor_copy(conv_out[:, :, 0:XPAD], mxp[:, :, TP:TP + XPAD])
                src = mxp[:, :, XPAD + TP:].rearrange("p j (b t) -> p j b t", b=SB)[:, :, :, ST:]
                link(dve.tensor_copy(conv_out[:, :, XPAD:].rearrange("p j (b t) -> p j b t", b=SB), src))
                conv_out_ok(l)

            def conv_out_ok(l):
                dve.sem_inc(co_ok.sem, 1)

            def mlstm_gates(l):
                R = [rows[0:NH, k, :] for k in range(4)]
                cum = gate_rows[0:NH, 0, :]
                dve.wait_ge(*evac(l, 6))
                link(TSC(R[2], R[1], -1.0, None, MUL))
                link(TT(R[2], R[2], R[1], MAX))
                TSC(R[1], R[1], 0.0, None, MIN).then_inc(u_abs.sem, 1)
                dve.wait_ge(*u_exp(l))
                link(TT(R[1], R[1], R[2], SUB))
                link(dve.tensor_tensor_scan(R[3], C("reset_mul", T, NH), R[1], 0.0, MUL, ADD))
                link(TT(R[0], R[0], R[3], SUB))
                link(dve.tensor_tensor_scan(cum, C("reset_add", T, NH), R[0], 0.0, ADD, MAX))
                TSC(cum[:, 0:TP], cum[:, 0:TP], 0.0, None, MAX)
                m0b = end(m0[:, l, :], ST)
                link(TT(seq4(cum[:, TP:T]), seq4(cum[:, TP:T]), m0b, MAX))
                TSC(R[1], cum, -1.0, None, MUL)
                TT(R[2], R[3], cum, ADD)
                link(TT(seq4(arow[0:NH, :]), m0b, seq4(cum[:, TP:T]), SUB))
                if l > 0:
                    dve.wait_ge(st_ml.sem, 64 * l)
                dve.tensor_copy(m_out[:, 0:1], R[2][:, TP - 1:TP])
                dve.tensor_copy(m_out[:, 1:1 + SB], seq4(R[2][:, TP:T])[:, :, ST - 1])
                TSC(R[3][:, 0:TP], R[0][:, 0:TP], cum[:, TP - 1:TP], None, SUB)
                lastM = seq4(cum[:, TP:T])[:, :, ST - 1:ST].broadcast_to([NH, SB, ST])
                TT(seq4(R[3][:, TP:T]), seq4(R[0][:, TP:T]), lastM, SUB).then_inc(lf_ok.sem, 1)
                dve.wait_ge(*ml_col(l))
                dve.tensor_copy(gwc[:, 0:16], ps[:, 4, 0:16])
                link(dve.tensor_copy(gwc[0:TS, 16:24], ps[0:TS, 4, 16:24]))
                dve.sem_inc(ml_colv.sem, 1)

            def mlstm_keys(l):
                dve.wait_ge(*mqk_e(l, 11))
                for i, (_, m) in enumerate(TOK):
                    v = mkt[0:m, i, :].rearrange("p (h e) -> p h e", h=NH)
                    last = TT(v, v, end(gwc[0:m, 8 * i + 4:8 * i + 8], P), MUL)
                last.then_inc(kdec_ok.sem, 1)

            def mlstm_head(l, h):
                dve.wait_ge(*ml_bc(l, h + 1))
                dve.tensor_copy(aL[:, :, h], seq4(ps[:, 4, T:T + TS])[:, :, ST - 1])
                link(TT(qa, mq[:, h, TP:T], ps[:, 4, T:T + TS], MUL))
                if h == 0:
                    dve.wait_ge(ld_n0.sem, 16 * (l + 1))
                n0v = end(n0.rearrange("p (b h) -> p b h", b=SB)[:, :, h], ST)
                TT(seq4(nq), seq4(qa), n0v, MUL)
                g = [gwc[:, 8 * i + h:8 * i + h + 1] for i in range(3)]
                STT(ml_W[:, 0:P], ps[:, 4, 0:P], g[0], C("causal_neg", P), ADD, ADD)
                TSC(ml_W[:, P:TP], ps[:, 4, P:TP], g[0], None, ADD)
                STT(ml_W[:, TP:TP + P], ps[:, 4, P:TP], g[1], C("causal_neg", P), ADD, ADD)
                STT(ml_W[0:TS, TP + P:PW], ps[0:TS, 4, TP:T], g[2][0:TS, :], C("sample_neg", TS, TS), ADD, ADD)\
                    .then_inc(ml_wl.sem, 1)
                dve.wait_ge(*ml_ex(l, h + 1))
                dve.wait_ge(*ml_s(l, h + 1))
                TT(ml_PW[:, 0:TP + P], ps[:, 6, 0:TP + P], ml_W[:, 0:TP + P], MUL)
                TT(ml_PW[0:TS, TP + P:PW], ps[0:TS, 6, TP + P:PW], ml_W[0:TS, TP + P:PW], MUL)\
                    .then_inc(ml_pw.sem, 1)
                dve.wait_ge(*ml_ad(l, h + 1))
                link(TT(ml_den, ml_den, ps[:, 5, 0:T], MAX))
                link(dve.reciprocal(ml_den, ml_den))
                TT(ml_o[:, h, :], ps[:, 7, 0:T], ml_den, MUL).then_inc(ml_h.sem, 1)

            def mlstm_state(l):
                dve.wait_ge(*ml_cpe(l))
                for b in range(SB):
                    if b >= 2:
                        dve.wait_ge(*ml_sc(l, b - 1))
                    TSC(kb[0:TS, b % 2, :], mkt[0:TS, 2, :], C("bmask", 1, TS, b), None, MUL).then_inc(ml_kb.sem, 1)
                    if b > 0:
                        update(l, b - 1)
                update(l, SB - 1)
                link(TT(n_out[:, NH:], n0, aL.rearrange("p b h -> p (b h)"), MUL))
                TT(n_out[:, NH:], n_out[:, NH:], ps[:, 5, 8:8 + SB * NH], ADD).then_inc(ml_out.sem, 1)

            def update(l, b):
                link(TT(C0[:, b, :, :], C0[:, b, :, :], end(aL[:, b, :], P), MUL))
                dve.wait_ge(*ml_sc(l, b + 1))
                v = ps[:, 6 + b % 2, :].rearrange("p (h e) -> p h e", h=NH)
                TT(C0[:, b, :, :], C0[:, b, :, :], v, ADD).then_inc(ml_sca.sem, 1)

            def mlstm_finish(l):
                for j in range(4):
                    last = STT(ml_o[:, j, :], ml_o[:, j, :], V(l, "ml_gn", j), ml_sq[:, j, :], MUL, MUL)
                link(last)
                for j in range(4):
                    last = STT(ml_o[:, j, :], xc[:, j, :], V(l, "ml_skip", j), ml_o[:, j, :], MUL, ADD)
                link(last)
                dve.wait_ge(*evac(l, 40))
                TT(y_ml[:, :, :], ml_o, y_ml[:, :, :], MUL).then_inc(hn_y.sem, 1)

            def retention(l):
                TT(qr, rqk, mid(C("cos", T), 4), MUL)
                for j in range(4):
                    dve.wait_ge(*r_sw(l, j + 1))
                    last = TT(rt[:, j, :], ps[:, 4 + j, 0:T], C("sin", T), MUL)
                link(last)
                link(TT(qr, qr, rt, ADD))
                for i in range(2):
                    last = TT(qd[:, i, :], qr[:, i, TP:T], C("qdec", TS, P, TS * i), MUL)
                last.then_inc(r_qr.sem, 1)
                for i, (_, m) in enumerate(TOK):
                    dve.wait_ge(*r_kt(l, i + 1))
                    src = ps[0:m, 4 + i, 0:256].rearrange("p (h e) -> p h e", h=NH)
                    dst = ktd[0:m, i, :].rearrange("p (h e) -> p h e", h=NH)
                    TT(dst, src, end(C("kdec", NH, m, NH * i), DK), MUL).then_inc(r_ktd.sem, 1)
                dve.wait_ge(ld_ret.sem, 32 * (l + 1))
                for h in range(NH):
                    if h >= 2:
                        dve.wait_ge(*r_o(l, h - 1))
                    dve.wait_ge(*r_sc(l, h + 1))
                    TT(rpw[:, h % 2, 0:TP + P], ps[:, 4 + h % 2, 0:TP + P], dec[:, h, 0:TP + P], MUL)
                    TT(rpw[0:TS, h % 2, TP + P:PW], ps[0:TS, 4 + h % 2, TP + P:PW], dec[0:TS, h, TP + P:PW], MUL)\
                        .then_inc(r_pw.sem, 1)
                for b in range(SB):
                    if b >= 2:
                        dve.wait_ge(*r_ss(l, b - 1))
                    TSC(rkb[0:TS, b % 2, :], ktd[0:TS, 2, :], C("bmask", 1, TS, b), None, MUL).then_inc(r_kb.sem, 1)
                    if b > 0:
                        retention_update(l, b - 1)
                retention_update(l, SB - 1)

            def retention_update(l, b):
                dve.wait_ge(*r_ss(l, b + 1))
                for i in range(2):
                    last = STT(S0_ret[:, b, i, :], S0_ret[:, b, i, :], C("g4", 1, P, i),
                               ps[:, 5 + b % 2, P * i:P * i + P], MUL, ADD)
                last.then_inc(r_ssa.sem, 1)

            def retention_finish(l):
                for j in range(4):
                    last = STT(ret_o[:, j, :], ret_o[:, j, :], V(l, "ret_gn", j), ret_sq[:, j, :], MUL, MUL)
                link(last)
                dve.wait_ge(*evac(l, 44))
                TT(y_ret[:, :, :], ret_o, y_ret[:, :, :], MUL).then_inc(hn_y.sem, 1)

            def rwkv_prepare(l):
                dve.wait_ge(st_ml.sem, 64 * (l + 1))
                dve.tensor_copy(shift_out[:, :, 0:1], z[:, :, TP:TP + 1])
                zq = z[:, :, 1 + TP:].rearrange("p j (b t) -> p j b t", b=SB)
                link(dve.tensor_copy(shift_out[:, :, 1:], zq[:, :, :, ST]))
                dve.sem_inc(so_ok.sem, 1)
                link(TT(zs[:, :, 0:TP], z[:, :, 0:TP], z[:, :, 1:1 + TP], SUB))
                for j in range(ZT):
                    b = zq[:, j]
                    d = seq4(zs[:, j, TP:T])
                    TT(d, b[:, :, 0:ST], b[:, :, 1:], SUB)
                    last = STT(zs[:, j, 0:TP], zs[:, j, 0:TP], V(l, "mu", j), z[:, j, 1:1 + TP], MUL, ADD)
                link(last)
                for j in range(ZT):
                    d = seq4(zs[:, j, TP:T])
                    last = STT(d, d, V(l, "mu", j), zq[:, j][:, :, 1:], MUL, ADD)
                last.then_inc(w_zs.sem, 1)
                dve.wait_ge(*w_zs(l))
                for j in range(4):
                    last = TSC(rw_kk[:, j, :], zs[:, 4 + j, :], V(l, "kk", j), None, MUL)
                link(last)
                TT(rw_e1, rw_kk, rw_kk, MUL).then_inc(w_sq.sem, 1)
                dve.wait_ge(*w_lorae(l, 12))
                for j in range(4):
                    last = TSC(rw_e2[:, j, :], rw_a[:, j, :], -1.0, V(l, "ka", j), ADD, MUL)
                link(last)
                link(STT(rw_kp, rw_e2, 1.0, zs[:, 4:8, :], ADD, MUL))
                for j in range(4):
                    last = STT(rw_e2[:, j, :], zs[:, j, :], V(l, "rk", j), rw_kp[:, j, :], MUL, MUL)
                for j in range(4):
                    dve.wait_ge(*w_ss(l, j + 1))
                    last = TSC(rw_e1[:, j, :], ps[:, 4 + j, 0:T], 1e-24, None, MAX)
                last.then_inc(w_rk.sem, 1)
                dve.wait_ge(*w_rk(l))
                dve.reciprocal(rw_e1, rw_e1).then_inc(w_ssr.sem, 1)
                dve.wait_ge(*w_ssq(l))
                link(TT(rw_kk, rw_kk, rw_e1, MUL))
                dve.wait_ge(st_ret.sem, 32 * (l + 1))
                for j in range(4):
                    dve.wait_ge(*w_bo(l, j + 1))
                    TT(rw_bv[:, j, :], ps[:, 4 + j, 0:T], zs[:, 8 + j, :], MUL)
                link(TSC(rw_lw, rw_lw, -RW_DECAY, None, MUL))
                for j in range(4):
                    last = dve.tensor_tensor_scan(rw_e1[:, j, :], C("reset64", T), rw_lw[:, j, :], 0.0, MUL, ADD)
                link(last)
                TT(rw_e2, rw_e1, rw_lw, SUB).then_inc(w_F.sem, 1)
                dve.wait_ge(*w_F(l))
                dve.wait_ge(*w_zuv(l, 4))
                link(TT(rw_a, rw_a, rw_kk, MUL))
                dve.wait_ge(*w_E(l))

                def blocks(dst, q, x, y):
                    for j in range(NP4):
                        out = dst[:, j, 0:NC - 1, CH * q:CH * q + CH]
                        TT(out, x[:, j, 0:TP].rearrange("p (c s) -> p c s", c=NC - 1),
                           y[:, j, 0:TP].rearrange("p (c s) -> p c s", c=NC - 1), MUL)
                    return TT(dst[:, :, NC - 1, CH * q:CH * q + TS], x[:, :, TP:T], y[:, :, TP:T], MUL)

                blocks(KR, 0, rw_kk, rw_e2)
                blocks(KR, 1, zs[:, 0:4, :], rw_e1)
                blocks(BK, 0, rw_a, rw_lw)
                blocks(BK, 1, rw_kp, rw_lw)
                dve.tensor_copy(PL[:, :, 0:4], rw_e1[:, :, CH - 1:TP:CH])
                link(dve.tensor_copy(PL[:, :, 4:], rw_e1[:, :, TP + ST - 1:T:ST]))
                dve.sem_inc(w_pre.sem, 1)

            def rwkv_gram(l):
                for c in range(NC):
                    mask = C("gram_p" if c < NC - 1 else "gram_s", P)
                    for p in range(2):
                        n = 2 * c + p
                        dve.wait_ge(*w_g1(l, n + 1))
                        TT(G[:, c, p, :].rearrange("p (j e) -> p j e", j=4),
                           ps[:, n % 4, :].rearrange("p (j e) -> p j e", j=4), mid(mask, 4), MUL)\
                            .then_inc(w_g1e.sem, 1)
                dve.wait_ge(*w_zab(l, 2))
                for n in range(6):
                    p, c0 = n % 2, 2 * (n // 2)
                    r = slice(CH * p, CH * p + CH)
                    dve.wait_ge(*w_g2(l, n + 1))
                    for c in range(c0, min(c0 + 2, NC)):
                        src = ps[r, 4 + n % 4, 256 * (c - c0):256 * (c - c0) + 256].rearrange("p (j e) -> p j e", j=4)
                        mask = con[r, CON["a_p" if c < NC - 1 else "a_s"]:][:, 0:CH]
                        last = TT(Abd[r, 4 * c:4 * c + 4, CH * p:CH * p + CH], src, mid(mask, 4), MUL)
                    last.then_inc(w_g2e.sem, 1)
                dve.wait_ge(*w_g2e(l, 6))
                for p in range(2):
                    r = slice(CH * p, CH * p + CH)
                    m0_, m0t = con[0:CH, CON["join0"]:][:, 0:CH], con[r, CON["join0t"]:][:, 0:CH]
                    for c in range(NC):
                        TT(Xc[r, 4 * c:4 * c + 4, :],
                           G[0:CH, c, p, :].rearrange("p (j e) -> p j e", j=4)[:, :, 0:CH], mid(m0_, 4), MUL)
                    dg = slice(CH * p, CH * p + CH)
                    link(TT(Xbd[r, :, dg], Abd[r, :, dg], mid(m0t, NU), MUL))
                    eye = con[r, CON["ident64"]:][:, 0:CH]
                    TT(Xc[r, :, :], Xc[r, :, :], mid(eye, NU), ADD)
                    last = TT(Xbd[r, :, dg], Xbd[r, :, dg], mid(eye, NU), ADD)
                last.then_inc(w_x0.sem, 1)
                dve.wait_ge(*w_x0(l))

            def rwkv_invert(l):
                for m in range(len(LEVELS)):
                    for g in range(3):
                        n = min(8, NU - 8 * g)
                        us = slice(8 * g, 8 * g + n)
                        dve.wait_ge(*w_p(l, 3 * m + g + 1))
                        src = ps[:, 3 + g, 0:CH * n].rearrange("p (a b) -> p a b", a=n)
                        link(TT(Yc[:, us, :], src, mid(C("joins", CH, P, CH * m), n), MUL))
                        TT(Xc[:, us, :], Xc[:, us, :], Yc[:, us, :], ADD).then_inc(w_pe.sem, 1)
                    if m < len(LEVELS) - 1:
                        for q in (1, 3):
                            dve.wait_ge(*w_t(l, 5 * m + q + 1))
                            src = ps[0:CH, (6, 7, 0, 1, 2)[q], :].rearrange("p (a b) -> p a b", a=4)
                            dve.tensor_copy(Xbd[0:CH, 4 * q:4 * q + 4, 0:CH], src[:, :, 0:CH])
                            dve.tensor_copy(Xbd[CH:P, 4 * q:4 * q + 4, CH:P], src[:, :, CH:P]).then_inc(w_to.sem, 1)
                dve.wait_ge(*w_pe(l, 15))
                dve.tensor_copy(XT[0:CH, :, CH:P], Xc[CH:P, :, :]).then_inc(w_xt.sem, 1)
                dve.memset(Sbd, 0.0).then_inc(w_sz.sem, 1)
                dve.wait_ge(*w_sz(l))

            def rwkv_chunks(l):
                for c in range(NC):
                    dve.wait_ge(*w_r(l, c + 1))
                    if c == NC - 1:
                        link(TSC(Rn[0:CH, :], ps[0:CH, 0, :], -1.0, None, MUL))
                        dve.wait_ge(*w_ct(l))
                        TT(Rn[0:TS, :], Rn[0:TS, :], ps[0:TS, 3, :], SUB).then_inc(w_rn.sem, 1)
                        dve.wait_ge(*w_ob(l, c + 1))
                        dve.wait_ge(*w_cxe(l))
                        src = ps[:, 4 + c % 2, 0:256].rearrange("p (a b) -> p a b", a=4)[:, :, 0:TS]
                        TT(rw_o[:, :, TP:T], src, CX[:, :, 1, :], ADD).then_inc(w_oe.sem, 1)
                        continue
                    TSC(Rn[0:CH, :], ps[0:CH, 0, :], -1.0, None, MUL).then_inc(w_rn.sem, 1)
                    dve.wait_ge(*w_s(l, c + 1))
                    for p in range(2):
                        r, dg = slice(CH * p, CH * p + CH), slice(CH * p, CH * p + CH)
                        src = ps[r, 2, :].rearrange("p (j e) -> p j e", j=4)[:, :, dg]
                        last = TT(Sbd[r, :, dg], Sbd[r, :, dg], src, ADD)
                    link(last)
                    for p in range(2):
                        r, dg = slice(CH * p, CH * p + CH), slice(CH * p, CH * p + CH)
                        last = TT(Sbd[r, :, dg], Sbd[r, :, dg], end(PL[r, :, c], CH), MUL)
                    last.then_inc(w_su.sem, 1)
                for b in range(SB):
                    if b >= 2:
                        dve.wait_ge(*w_st(l, b - 1))
                    TSC(KBm[b % 2], BKt[:, NC - 1, :], C("bmask2", 1, P, b), None, MUL).then_inc(w_kb.sem, 1)
                    if b > 0:
                        rwkv_update(l, b - 1)
                rwkv_update(l, SB - 1)

            def rwkv_update(l, b):
                dve.wait_ge(*w_st(l, b + 1))
                src = ps[:, 1 + b % 2, :].rearrange("p (j e) -> p j e", j=4)
                link(TT(S0bd[:, b, :, :], S0bd[:, b, :, :], src, ADD))
                TT(S0bd[:, b, :, :], S0bd[:, b, :, :], end(PL[:, :, 4 + b], P), MUL).then_inc(w_sta.sem, 1)

            def rwkv_finish(l):
                for j in range(4):
                    last = STT(rw_o[:, j, :], rw_o[:, j, :], V(l, "gn_w", j), rw_sq[:, j, :], MUL, MUL)
                link(last)
                for j in range(4):
                    last = STT(rw_o[:, j, :], rw_o[:, j, :], V(l, "gn_b", j), rw_bv[:, j, :], ADD, ADD)
                last.then_inc(hn_y.sem, 1)
                dve.wait_ge(*hn_y(l, 3))
                TT(y_rw[:, :, :], rw_o, rw_g, MUL).then_inc(rw_y.sem, 1)

            def closing(l):
                turns.pass_over(len(EARLY))
                with dve.Fori(0, KT // 2) as i:
                    inner = turns.loop(i, 5)
                    for _ in range(3):
                        inner.take()
                    for dd in range(2):
                        s, used = inner.take()
                        for n in range(3):
                            q = 3 * dd + n
                            dve.wait_ge(f_zs.sem, i * 6 + (3 + 24 * l + 2 * n + dd + 1))
                            if n == 2:
                                dve.wait_ge(slot_fr[s].sem, used + 1)
                            else:
                                dve.wait_ge(f_br.sem, i * 4 + (16 * l + 2 * dd + n + 1))
                            dst = mixed[:, bass.ds(i * 2 + dd, 1), :].rearrange("p a n -> p (a n)") if n == 0 \
                                else gtmp[:, n, :]
                            TT(dst, ps[:, 3 + q % 3, 0:T], gates[:, 2 * n + dd, :], MUL).then_inc(f_mul.sem, 1)
                            dve.wait_ge(f_mul.sem, i * 6 + (6 + 24 * l + q + 1))
                            acc = mixed[:, bass.ds(i * 2 + dd, 1), :].rearrange("p a n -> p (a n)")
                            if n == 0:
                                dve.sem_inc(f_gm.sem, 1)
                            else:
                                TT(acc, acc, gtmp[:, n, :], ADD).then_inc(f_gm.sem, 1)
                                dve.wait_ge(f_gm.sem, i * 6 + (3 + 24 * l + q + 1))
                turns.after(KT // 2, 5)
                for d in range(KT):
                    if d % 2 == 0:
                        s, used = turns.take()
                        dve.wait_ge(*f_out(l, d // 2 + 1))
                    else:
                        dve.wait_ge(slot_fr[s].sem, used + 1)
                    TT(X[:, d, :], X[:, d, :], ps[:, 6 + d % 2, 0:T], ADD).then_inc(x_mix.sem, 1)

            def route():
                dve.memset(posn, 0.0)
                dve.memset(pick_out, 0.0).then_inc(out_ok.sem, 1)
                dve.memset(yg[:, 0:512], 0.0).then_inc(yg_a.sem, 1)
                dve.memset(yg[:, 512:D], 0.0).then_inc(yg_d.sem, 1)
                link(dve.memset(lg, 0.0))
                dve.wait_ge(*rt_lg(0))
                dve.tensor_copy(lg[:, 0:2, :], ps[:, 6, 0:16].rearrange("p (i e) -> p i e", i=2))
                link(dve.tensor_copy(lg[0:TS, 2, :], ps[0:TS, 6, 16:24]))
                for i in range(3):
                    last = dve.max(top[:, i, :], lg[:, i, :])
                link(last)
                v1 = top[:, :, 1:2].broadcast_to([P, 3, NE])
                TT(gt, lg, v1, ALU.is_gt)
                TT(eq, lg, v1, ALU.is_equal)
                link(TT(ex, lg, top[:, :, 0:1].broadcast_to([P, 3, NE]), SUB))
                dve.sem_inc(rt_e.sem, 1)
                for i in range(3):
                    dve.tensor_tensor_scan(cum[:, i, :], eq[:, i, :], eq[:, i, :], 0.0, ADD, ALU.bypass)
                link(dve.reduce_sum(cnt, gt, AX_X))
                link(TSC(cnt, cnt, -1.0, 2.0, MUL, ADD))
                link(TT(cum, cum, end(cnt, NE), ALU.is_le))
                link(TT(eq, eq, cum, MUL))
                link(TT(gt, gt, eq, ADD))
                dve.sem_inc(rt_sel.sem, 1)
                dve.wait_ge(rt_ex.sem, 1)
                link(TT(ex, ex, gt, MUL))
                link(dve.reduce_sum(cnt2, ex, AX_X))
                link(dve.reciprocal(cnt2, cnt2))
                TT(ex, ex, end(cnt2, NE), MUL)
                dve.wait_ge(*rt_pos(0))
                STT(posn[:, 0:2, :], ps[:, 7, 0:16].rearrange("p (i e) -> p i e", i=2), 1.0, gt[:, 0:2, :], ADD, MUL)
                STT(posn[0:TS, 2, :], ps[0:TS, 7, 16:24], 1.0, gt[0:TS, 2, :], ADD, MUL)
                counts = ps[0:1, 7, 32:32 + NE].unsqueeze(1).broadcast_to([1, MAXB - 1, NE])
                link(TT(need[0:1, :].rearrange("p (b e) -> p b e", e=NE), counts,
                        PCON("more", slots_n, 1).rearrange("p (b e) -> p b e", e=NE), ALU.is_gt))
                dve.sem_inc(rt_cb.sem, 1)
                pick_tokens(0, 0)
                for n in (1, 3, 5):
                    dve.wait_ge(xt_p.sem, n + 1)
                    m = TOK[n // 2][1]
                    dve.tensor_copy(xt[0:m, n // 2, 512:D], ps[0:m, n, :]).then_inc(xt_d.sem, 1)
                dve.wait_ge(*rt_ct(0))
                dve.tensor_copy(crow[0:NE, :], ps[0:NE, 6, 0:T])
                dve.tensor_copy(prow[0:NE, :], ps[0:NE, 7, 0:T]).then_inc(rt_cr.sem, 1)
                dve.tensor_copy(draft[0:1, :], PCON("first", PLAN_N, 1))
                link(dve.tensor_tensor_scan(rank[0:1, :], need[0:1, :], need[0:1, :], 0.0, ADD, ALU.bypass))
                TT(draft[0:1, PLAN_N - 1:PLAN_N], draft[0:1, PLAN_N - 1:PLAN_N], rank[0:1, slots_n - 1:slots_n], ADD)
                link(TT(need[0:1, :], rank[0:1, :], need[0:1, :], MUL))

                def table(name):
                    return PCON(name, MAXEXTRA * slots_n, 1).rearrange("p (k s) -> p k s", k=MAXEXTRA)

                link(TT(hits[0:1], mid(need[0:1, :], MAXEXTRA), table("rank"), ALU.is_equal))
                TT(hits2[0:1], hits[0:1], table("block"), MUL)
                link(TT(hits[0:1], hits[0:1], table("expert"), MUL))
                dve.reduce_sum(draft[0:1, NE:NE + MAXEXTRA], hits[0:1], AX_X)
                at_ = NE + MAXEXTRA + 1 + NE
                link(dve.reduce_sum(draft[0:1, at_:at_ + MAXEXTRA], hits2[0:1], AX_X))
                link(dve.tensor_copy(plan[:, :], draft[0:1, :]))
                dve.sem_inc(plan_ok.sem, 1)

            def pick_tokens(e, b):
                for i, (c0, m) in enumerate(TOK):
                    if isinstance(b, int):
                        places = PCON("iota", MB, m, MB * b)
                        scalar = posn[0:m, i, e:e + 1]
                    else:
                        places = pcon[0:m, bass.ds(b * MB + PC["iota"], MB)]
                        scalar = posn[0:m, i, bass.ds(e, 1)]
                    last = TSC(pick_in[0:m, i, :], places, scalar, None, ALU.is_equal)
                last.then_inc(in_ok.sem, 1)

            def gathered(n):
                dve.wait_ge(ga_p.sem, n * 2 + 2)
                dve.tensor_copy(xg[:, 4:8, :], ps[:, 5, :].rearrange("p (k n) -> p k n", k=4)).then_inc(ga_d.sem, 1)

            def scattered(n):
                for d in range(KT):
                    dve.wait_ge(sc_p.sem, n * KT + (d + 1))
                    TT(X[:, d, :], X[:, d, :], ps[:, 4 + d % 2, 0:T], ADD).then_inc(sc_e.sem, 1)

            def experts():
                gathered(0)
                for e in range(NE):
                    dve.wait_ge(rt_bc.sem, 2 * e + 2)
                    dve.tensor_copy(posb[:, e, :], ps[:, 2 + e % 2, 0:T]).then_inc(rt_pbe.sem, 1)
                dve.wait_ge(rt_pbe.sem, NE)
                dve.wait_ge(rt_cbe.sem, NE)
                blocks = NE + MAXEXTRA + 1
                npass = dve.value_load(plan[0:1, PLAN_N - 1:PLAN_N], min_val=NE, max_val=NE + MAXEXTRA)
                with dve.Fori(0, npass) as i:
                    inner = turns.loop(i, ETURNS, EPAD)
                    e = dve.value_load(plan[0:1, bass.ds(i, 1)], min_val=0, max_val=NE - 1)
                    b = dve.value_load(plan[0:1, bass.ds(i + blocks, 1)], min_val=0, max_val=MAXB - 1)
                    e1 = dve.value_load(plan[0:1, bass.ds(i + 1, 1)], min_val=0, max_val=NE - 1)
                    b1 = dve.value_load(plan[0:1, bass.ds(i + (blocks + 1), 1)], min_val=0, max_val=MAXB - 1)
                    for f in range(FT):
                        if f == 3:
                            scattered(i)
                            STT(pick_out, posb[:, bass.ds(e, 1), :].rearrange("p a n -> p (a n)"),
                                pcon[:, bass.ds(b + PC["iotac"], 1)],
                                comb[:, bass.ds(e, 1), :].rearrange("p a n -> p (a n)"), ALU.is_equal, MUL)\
                                .then_inc(out_ok.sem, 1)
                            pick_tokens(e1, b1)
                        s, used = inner.take()
                        dve.wait_ge(s_done.sem, i * FT + (FT * NDENSE + f + 1))
                        dve.wait_ge(slot_fr[s].sem, used + 1)
                        TT(ehid[:, f, :], ps[:, 2 * (f % 2) + 1, 0:MB], esil[:, f % 3, :], MUL).then_inc(h_done.sem, 1)
                    gathered(i + 1)
                    for k in range(DSL):
                        s, used = inner.take()
                    dve.wait_ge(slot_fr[s].sem, used + 1)
                    dve.tensor_copy(yg[:, 512:D], ps[:, 7, :]).then_inc(yg_d.sem, 1)
                scattered(npass)

            def feed_forward():
                with dve.Fori(0, NDENSE) as e:
                    inner = turns.loop(e, FT + KT, 1)
                    for f in range(FT):
                        s, used = inner.take()
                        dve.wait_ge(s_done.sem, e * FT + (f + 1))
                        dve.wait_ge(slot_fr[s].sem, used + 1)
                        TT(hid[:, f, :], ps[:, 2 * (f % 3) + 1, 0:T], sil[:, f % 3, :], MUL).then_inc(h_done.sem, 1)
                    for d in range(KT):
                        s, used = inner.take()
                        dve.wait_ge(slot_fr[s].sem, used + 1)
                        TT(X[:, d, :], X[:, d, :], ps[:, 6 + d % 2, 0:T], ADD).then_inc(y_done.sem, 1)
                turns.after(NDENSE, FT + KT, 1)

            for k in range(3):
                dve.sem_inc(f_gm.sem, 1)
                dve.sem_inc(h_done.sem, 1)
            for k in range(6):
                dve.sem_inc(f_mul.sem, 1)
            for k in range(2):
                dve.sem_inc(y_done.sem, 1)
            dve.wait_ge(ld_con.sem, 64)
            for l in range(DEPTH):
                norm(2 * l)
                histories(l)
                conv(l)
                mlstm_gates(l)
                mlstm_keys(l)
                for h in range(NH):
                    mlstm_head(l, h)
                mlstm_state(l)
                head_norm(3 * l, ml_o, ml_sq, P, GN_EPS, lambda: mlstm_finish(l))
                dve.wait_ge(*hn_y(l, 1))
                retention(l)
                head_norm(3 * l + 1, ret_o, ret_sq, P, GN_EPS, lambda: retention_finish(l))
                dve.wait_ge(*hn_y(l, 2))
                rwkv_prepare(l)
                rwkv_gram(l)
                rwkv_invert(l)
                rwkv_chunks(l)
                head_norm(3 * l + 2, rw_o, rw_sq, CH, RW_GN_EPS, lambda: rwkv_finish(l))
                closing(l)
                norm(2 * l + 1)
                if l == 0:
                    feed_forward()
                else:
                    route()
                    experts()
            norm(2 * DEPTH)

        @block.gpsimd
        def _(pool):
            for l in range(DEPTH):
                if l > 0:
                    pool.wait_ge(y_done.sem, CREDIT_Y + KT * NDENSE)
                    pool.wait_ge(*w_zs(l - 1))
                pool.dma_start(hist[:, :], a["hist"][l]).then_inc(ld_hist.sem, 16)
                pool.dma_start(prev[:, :], a["prev"][l]).then_inc(ld_hist.sem, 16)
                pool.dma_start(C0, a["C"][l]).then_inc(ld_c0.sem, 16)
                pool.dma_start(n0, a["n"][l]).then_inc(ld_n0.sem, 16)
                pool.wait_ge(*co_ok(l))
                pool.dma_start(o["conv"][l], conv_out[:, :, :]).then_inc(st_small.sem, 16)
                pool.wait_ge(*ml_out(l))
                pool.wait_ge(*ml_cpe(l))
                pool.dma_start(o["m"][l], m_out[:, :]).then_inc(st_ml.sem, 16)
                pool.dma_start(o["n"][l], n_out[:, :]).then_inc(st_ml.sem, 16)
                pool.dma_start(o["C_p"][l], Cp).then_inc(st_ml.sem, 16)
                pool.dma_start(o["C_s"][l], C0).then_inc(st_ml.sem, 16)
                pool.wait_ge(*hn_y(l, 1))
                pool.dma_start(dec, a["dec"].rearrange("p (h w) -> p h w", h=NH)).then_inc(ld_ret.sem, 16)
                pool.dma_start(S0_ret, a["ret"][l]).then_inc(ld_ret.sem, 16)
                pool.wait_ge(*r_spe(l))
                pool.dma_start(o["ret_p"][l], Sp_ret).then_inc(st_ret.sem, 16)
                pool.wait_ge(*r_ssa(l, 8))
                pool.dma_start(o["ret_s"][l], S0_ret).then_inc(st_ret.sem, 16)
                pool.wait_ge(*hn_y(l, 2))
                pool.wait_ge(st_ml.sem, 64 * (l + 1))
                pool.wait_ge(st_ret.sem, 32 * (l + 1))
                pool.memset(UV[0:CH, :, :], 0.0).then_inc(w_zuv.sem, 1)
                pool.wait_ge(*w_zuv(l, 1))
                pool.memset(UV[CH:P, NC - 1, :], 0.0).then_inc(w_zuv.sem, 1)
                for k, t in enumerate((BK, KR)):
                    pool.wait_ge(*w_zuv(l, 2 + k))
                    v = t[:, :, NC - 1, :].rearrange("p j (q s) -> p j q s", q=2)[:, :, :, TS:]
                    pool.memset(v, 0.0).then_inc(w_zuv.sem, 1)
                pool.wait_ge(*so_ok(l))
                pool.dma_start(o["shift"][l], shift_out[:, :, :]).then_inc(st_small.sem, 16)
                pool.wait_ge(*w_pre(l))
                pool.memset(Abd, 0.0).then_inc(w_zab.sem, 1)
                pool.memset(Xbd, 0.0).then_inc(w_zab.sem, 1)
                pool.wait_ge(*w_bt(l, 5))
                pool.wait_ge(*w_xt(l, 2))
                pool.dma_start(S0bd, a["rw"][l]).then_inc(ld_rw.sem, 16)
                pool.wait_ge(*w_su(l, 4))
                pool.dma_start(o["rw_p"][l], Sbd).then_inc(st_rw.sem, 16)
                pool.wait_ge(*w_sta(l, 8))
                pool.dma_start(o["rw_s"][l], S0bd).then_inc(st_rw.sem, 16)
            for s, n in ((st_small, 32), (st_ml, 64), (st_ret, 32), (st_rw, 32)):
                pool.wait_ge(s.sem, n * DEPTH)


def kernel(**inputs):
    import numpy as _np
    import concourse.bacc as _bacc
    from concourse.bass_utils import run_bass_kernel_spmd as _run

    f = {k: _np.asarray(v) for k, v in inputs.items()}
    tiles = lambda v: v.reshape(v.shape[0], -1, P).transpose(0, 2, 1)

    x = _np.concatenate([f["x_prompt"].reshape(TP, D), f["x_sample"].reshape(TS, D)], 0)
    arrays = {"x": x.reshape(T, KT, P).transpose(2, 1, 0)}
    con, dec = shape_constants()
    arrays["con"], arrays["dec"] = con, dec
    vec = [f["norm_mix"], f["norm_ffn"], f["ret_gn"], f["ml_conv_w"].reshape(DEPTH, -1), f["ml_conv_b"], f["ml_gn"],
           f["ml_skip"], f["rw_mu"], f["rw_w0"], f["rw_a0"], f["rw_kk"], f["rw_ka"], f["rw_rk"], f["rw_gn_w"],
           f["rw_gn_b"], _np.stack([f["final_norm"]] * DEPTH)]
    arrays["vec"] = _np.concatenate([tiles(v) for v in vec], 2).transpose(1, 0, 2)
    arrays["bias"] = _np.stack([f["ml_bi"], f["ml_bf"]], 2).transpose(1, 0, 2)
    arrays["m0"] = f["state_mlstm_m"].transpose(2, 0, 1)
    rows_of = lambda w: w.reshape(w.shape[0], -1, P, w.shape[-1]).transpose(0, 2, 1, 3)
    router = _np.concatenate([_np.zeros((DEPTH - 1, D, NE), _np.float32), f["moe_router"]], 0)
    w_in = rows_of(f["w_in"])
    arrays["lw"] = _np.concatenate([
        w_in[..., 2560:2568].reshape(DEPTH, P, -1),
        f["ml_wq"].transpose(0, 2, 1, 3).reshape(DEPTH, P, -1), f["ml_wk"].transpose(0, 2, 1, 3).reshape(DEPTH, P, -1),
        _np.concatenate([f["rw_w2"], f["rw_a2"]], 1), f["rw_g2"], rows_of(router).reshape(DEPTH, P, -1)], 2)
    first = {"rq": 0, "rk": 256, "rv": 512, "rg": 1024, "mx": 1536, "mv": 2048, "mo": 2568, "zrw": 3080}
    mix = _np.zeros((DEPTH, NSLAB, P, SLOT), _np.float32)
    w_br = f["w_branch"].reshape(DEPTH, 3, 4, P, D)
    w_out = rows_of(f["w_out"])
    for n, (kind, j) in enumerate(EARLY + LATE + OUTS):
        if kind == "gate":
            c0 = 4872 + (j % 3) * D + (j // 3) * 256
            mix[:, n] = w_in[..., c0:c0 + 256].reshape(DEPTH, P, SLOT)
        elif kind == "branch":
            mix[:, n, :, 0:12 * P] = w_br[..., P * j:P * j + P].transpose(0, 3, 1, 2, 4).reshape(DEPTH, P, 12 * P)
        elif kind == "out":
            mix[:, n] = w_out[..., 256 * j:256 * j + 256].reshape(DEPTH, P, SLOT)
        else:
            c0 = first[kind] + 256 * j
            mix[:, n] = w_in[..., c0:c0 + 256].reshape(DEPTH, P, SLOT)
    arrays["mix"] = mix
    half = lambda w, ax: _np.stack(_np.split(w[0], 2, ax))
    cut = lambda w: w.reshape(-1, KT, P, FT, P).transpose(0, 3, 2, 1, 4).reshape(-1, P, KT * P)
    arrays["gu"] = _np.concatenate([cut(half(f["ffn_w_gate"], 1)), cut(half(f["ffn_w_up"], 1))], 2)
    arrays["down"] = half(f["ffn_w_down"], 0).reshape(NDENSE, FT, P, KT, P).transpose(0, 3, 2, 1, 4)\
        .reshape(NDENSE * KT, P, FT * P)
    arrays["egu"] = _np.concatenate([cut(f["moe_w_gate"][0]), cut(f["moe_w_up"][0])], 2)
    ed = _np.zeros((NE, 2 * DSL, P, D), _np.float32)
    ed[:, 0:FT] = f["moe_w_down"][0].reshape(NE, FT, P, D)
    arrays["edown"] = ed.reshape(NE, DSL, 2, P, D).transpose(0, 1, 3, 2, 4).reshape(NE * DSL, P, 2 * D)
    arrays["pcon"] = plan_constants()
    arrays["hist"] = f["state_mlstm_conv"].reshape(DEPTH, SB, XPAD, 4, P).transpose(0, 4, 3, 1, 2)\
        .reshape(DEPTH, P, -1)
    arrays["prev"] = f["state_rwkv_shift"].reshape(DEPTH, SB, ZT, P).transpose(0, 3, 2, 1).reshape(DEPTH, P, -1)
    arrays["C"] = f["state_mlstm_C"].transpose(0, 3, 1, 2, 4)
    arrays["n"] = f["state_mlstm_n"].transpose(0, 3, 1, 2).reshape(DEPTH, P, -1)
    arrays["ret"] = f["state_ret"].reshape(DEPTH, SB, 2, 2, DK, P).transpose(0, 3, 4, 1, 2, 5)\
        .reshape(DEPTH, P, SB, 2, P)
    s0 = f["state_rwkv"].reshape(DEPTH, SB, NP4, 2, DK, DK)
    rw = _np.zeros((DEPTH, 2, DK, SB, NP4, 2, DK), _np.float32)
    for p in range(2):
        rw[:, p, :, :, :, p, :] = s0[:, :, :, p].transpose(0, 4, 1, 2, 3)
    arrays["rw"] = rw.reshape(DEPTH, P, SB, NP4, P)
    arrays = {"in_" + k: _np.ascontiguousarray(v) for k, v in arrays.items()}

    nc = _bacc.Bacc("TRN2", target_bir_lowering=False, num_devices=1)
    a = {k[3:]: nc.dram_tensor(k, v.shape, F32, kind="ExternalInput").ap() for k, v in arrays.items()}
    shapes = {"y": (P, KT, T), "conv": (DEPTH, P, 4, 27), "shift": (DEPTH, P, ZT, 9), "m": (DEPTH, NH, 9),
              "n": (DEPTH, P, NH + SB * NH), "C_p": (DEPTH, P, 512), "C_s": (DEPTH, P, SB, NH, P),
              "ret_p": (DEPTH, P, 256), "ret_s": (DEPTH, P, SB, 2, P), "rw_p": (DEPTH, P, NP4, P),
              "rw_s": (DEPTH, P, SB, NP4, P)}
    o = {k: nc.dram_tensor("out_" + k, s, F32, kind="ExternalOutput").ap() for k, s in shapes.items()}
    build(nc, a, o)
    res = _run(nc, [arrays], core_ids=[0]).results[0]
    r = {k: _np.asarray(res["out_" + k]) for k in shapes}

    y = r["y"].transpose(2, 1, 0).reshape(T, D)
    ret_p = r["ret_p"].reshape(DEPTH, 2, DK, 2, P).transpose(0, 3, 1, 2, 4).reshape(DEPTH, 1, NH, DK, P)
    ret_s = r["ret_s"].reshape(DEPTH, 2, DK, SB, 2, P).transpose(0, 3, 4, 1, 2, 5).reshape(DEPTH, SB, NH, DK, P)
    C_p = r["C_p"].reshape(DEPTH, P, NH, P).transpose(0, 2, 1, 3)[:, None]
    C_s = r["C_s"].transpose(0, 2, 3, 1, 4)
    n_p = r["n"][:, :, 0:NH].transpose(0, 2, 1)[:, None]
    n_s = r["n"][:, :, NH:].reshape(DEPTH, P, SB, NH).transpose(0, 2, 3, 1)
    m_p, m_s = r["m"][:, :, 0][:, None], r["m"][:, :, 1:].transpose(0, 2, 1)
    conv_p = r["conv"][..., 0:3].transpose(0, 3, 2, 1).reshape(DEPTH, 1, 3, 512)
    conv_s = r["conv"][..., 3:].reshape(DEPTH, P, 4, SB, 3).transpose(0, 3, 4, 2, 1).reshape(DEPTH, SB, 3, 512)
    shift = r["shift"].transpose(0, 3, 2, 1).reshape(DEPTH, 9, -1)

    def heads(v, n):
        v = v.reshape(DEPTH, 2, DK, n, NP4, 2, DK)
        v = _np.stack([v[:, p, :, :, :, p, :] for p in range(2)], 1)
        return v.transpose(0, 3, 4, 1, 5, 2).reshape(DEPTH, n, 2 * NP4, DK, DK)

    rw_p, rw_s = heads(r["rw_p"], 1), heads(r["rw_s"], SB)
    out = (y[:TP].reshape(1, TP, D), y[TP:].reshape(SB, ST, D), ret_p, C_p, n_p, m_p, conv_p, rw_p, shift[:, 0:1],
           ret_s, C_s, n_s, m_s, conv_s, rw_s, shift[:, 1:])
    return tuple(_np.ascontiguousarray(v) for v in out)
```

```python
from contextlib import ExitStack

import concourse.bass as bass
import numpy as np
from concourse import mybir

F32 = mybir.dt.float32
ACT = mybir.ActivationFunctionType
ALU = mybir.AluOpType
AX_X = mybir.AxisListType.X

P = 128
DEPTH = 2
D = 1024
KT = D // P
TP, SB, ST = 256, 8, 4
TS = SB * ST
T = TP + TS
PAST = 2048
NH = 4
DK = 64
CONV = 4
ZT = 14
ZP = 1 + TP + SB * (1 + ST)
XPAD = CONV - 1
XW = XPAD + TP + SB * (XPAD + ST)
FT = 11
NE = 8
NDENSE = 2
MB = 128
MAXB = -(-T // MB)
MAXEXTRA = (2 * T - 1) // MB
DOWN = [[f] for f in range(7)] + [[7, 8], [9, 10]]
DSL = len(DOWN)
CH = 64
NC = TP // CH + 1
NP4 = 4
NU = NC * NP4
PW = 2 * P + P + TS
RING = 4
SLOT = 2048
NORM_EPS, GN_EPS, RW_GN_EPS = 1e-6, 1e-5, 64e-5
RW_DECAY = 0.606531
NEG = -1.0e30
LEVELS = (2, 4, 8, 16, 32)
LEVEL_GROUPS = [3 if m < ST else 2 for m in LEVELS]
NJOIN = sum(LEVEL_GROUPS)
assert LEVEL_GROUPS == [3, 2, 2, 2, 2]

VEC = {}
_at = 0
for _n, _w in (("norm_mix", 8), ("norm_ffn", 8), ("ret_gn", 4), ("conv_w", 16), ("conv_b", 4), ("ml_gn", 4),
               ("ml_skip", 4), ("mu", 14), ("w0", 4), ("a0", 4), ("kk", 4), ("ka", 4), ("rk", 4), ("gn_w", 4),
               ("gn_b", 4), ("final", 8)):
    VEC[_n] = _at
    _at += _w
NVEC = _at

IF = 32 + NH

LW = {}
_at = 0
for _n, _w in (("if", KT * IF), ("wq", 512), ("wk", 512), ("lora", 512), ("g2", 512), ("router", KT * NE)):
    LW[_n] = _at
    _at += _w
NLW = _at

CON = {}
_at = 0
for _n, _w in (("ones", 128), ("eps", 3), ("ident", 128), ("swap", 128), ("cent128", 128), ("cent64", 128), ("ones64", 128),
               ("cos", T), ("sin", T), ("causal_neg", 128), ("sample_neg", TS), ("reset64", T), ("reset_mul", T),
               ("reset_add", T), ("gram_p", 128), ("gram_s", 128), ("a_p", 64), ("a_s", 64), ("ident64", 64),
               ("join0", 64), ("join0t", 64), ("joins", 5 * 64), ("kdec", 12), ("qdec", 2 * TS), ("g4", 2),
               ("bmask", 8), ("bmask2", 8), ("sel", 1024)):
    CON[_n] = _at
    _at += _w
NCON = _at
CON_HEAD = CON["ident"]


def shape_constants():
    c = np.zeros((P, NCON), np.float32)
    r = np.arange(P)

    def put(name, a):
        a = np.asarray(a, np.float32)
        c[:a.shape[0], CON[name]:CON[name] + a.shape[1]] = a

    put("ident", np.eye(P))
    put("ones", np.ones((P, P)))
    half = DK // 2
    other = r // DK * DK + (r % DK + half) % DK
    put("swap", (other[:, None] == r[None, :]))
    put("cent128", np.eye(P) - 1.0 / P)
    same = (r[:, None] // DK == r[None, :] // DK)
    put("cent64", np.eye(P) - same / DK)
    put("ones64", same)
    pos = np.concatenate([np.arange(TP), np.tile(PAST + np.arange(ST), SB)]).astype(np.float32)
    inv = (10000.0 ** (-np.arange(half, dtype=np.float64) / half)).astype(np.float32)
    ang = (pos[None, :] * inv[r % half][:, None]).astype(np.float32).astype(np.float64)
    put("cos", np.cos(ang))
    put("sin", np.sin(ang) * np.where(r % DK < half, -1.0, 1.0)[:, None])
    put("causal_neg", np.where(r[:, None] <= r[None, :], 0.0, NEG))
    s = np.arange(TS)
    seq = s[:, None] // ST == s[None, :] // ST
    put("sample_neg", np.where(seq & (s[:, None] <= s[None, :]), 0.0, NEG))
    col = np.arange(T)
    starts = (col >= TP) & ((col - TP) % ST == 0)
    put("reset64", np.tile(~(starts | ((col < TP) & (col % CH == 0))), (P, 1)))
    put("reset_mul", np.tile(~(starts | (col == 0)), (P, 1)))
    put("reset_add", np.tile(np.where(starts | (col == 0), NEG, 0.0), (P, 1)))
    t = np.arange(CH)
    blk = (t[:, None] // ST == t[None, :] // ST) & (t[:, None] < TS) & (t[None, :] < TS)
    for name, ok in (("p", np.ones((CH, CH), bool)), ("s", blk)):
        strict, incl = (t[:, None] < t[None, :]) & ok, (t[:, None] <= t[None, :]) & ok
        put("gram_" + name, np.tile(np.concatenate([strict, incl], 1), (2, 1)))
        put("a_" + name, np.tile((t[None, :] < t[:, None]) & ok, (2, 1)))
    put("ident64", np.tile(np.eye(CH), (2, 1)))

    def join(m):
        return np.where((t[:, None] // m + 1 == t[None, :] // m) & (t[:, None] // (2 * m) == t[None, :] // (2 * m)), -1.0, 0.0)

    put("join0", np.tile(join(1), (2, 1)))
    put("join0t", np.tile(join(1).T, (2, 1)))
    put("joins", np.tile(np.concatenate([join(m) for m in LEVELS], 1), (2, 1)))
    lg = np.log1p(-(2.0 ** (-5.0 - np.arange(NH))))
    tok = np.arange(P)[:, None]
    kd = [np.exp((TP - 1 - tok) * lg), np.exp((TP - 1 - tok - P) * lg), np.exp((ST - 1 - tok % ST) * lg)]
    put("kdec", np.concatenate(kd, 1))
    head = r // DK
    put("qdec", np.concatenate([np.exp((s % ST + 1)[None, :] * lg[2 * i + head][:, None]) for i in range(2)], 1))
    put("g4", np.stack([np.exp(ST * lg[2 * i + head]) for i in range(2)], 1))
    put("bmask", r[:, None] // ST == np.arange(SB)[None, :])
    put("bmask2", (r % CH)[:, None] // ST == np.arange(SB)[None, :])
    put("sel", np.repeat(np.eye(8), P, 1))
    put("eps", np.tile([NORM_EPS, GN_EPS, RW_GN_EPS], (P, 1)))
    dec = np.zeros((P, NH, PW), np.float32)
    for h in range(NH):
        d0 = np.arange(TP)[None, :] - r[:, None]
        d1 = d0[:, :P]
        ds = s[None, :] - s[:, None]
        dec[:, h, 0:TP] = np.where(d0 >= 0, np.exp(np.maximum(d0, 0) * lg[h]), 0)
        dec[:, h, TP:TP + P] = np.where(d1 >= 0, np.exp(np.maximum(d1, 0) * lg[h]), 0)
        dec[:TS, h, TP + P:] = np.where(seq & (ds >= 0), np.exp(np.maximum(ds, 0) * lg[h]), 0)
    return c, dec.reshape(P, NH * PW)


PLAN_N = 2 * (NE + MAXEXTRA + 1) + 1
PC = {}
_at = 0
for _n, _w in (("tri", 128), ("iota", MAXB * MB), ("iotac", MAXB), ("first", PLAN_N), ("more", (MAXB - 1) * NE),
               ("rank", MAXEXTRA * (MAXB - 1) * NE), ("expert", MAXEXTRA * (MAXB - 1) * NE),
               ("block", MAXEXTRA * (MAXB - 1) * NE)):
    PC[_n] = _at
    _at += _w
NPC = _at


def plan_constants():
    c = np.zeros((P, NPC), np.float32)
    r = np.arange(P)

    def put(name, a):
        a = np.asarray(a, np.float32)
        c[:, PC[name]:PC[name] + a.shape[-1]] = a

    put("tri", r[:, None] < r[None, :])
    put("iota", 1 + np.arange(MAXB * MB))
    put("iotac", 1 + r[:, None] + MB * np.arange(MAXB)[None, :])
    first = np.zeros(PLAN_N)
    first[0:NE], first[-1] = np.arange(NE), NE
    put("first", first)
    slots = np.arange((MAXB - 1) * NE)
    put("more", MB * (1 + slots // NE))
    put("rank", np.repeat(1 + np.arange(MAXEXTRA), len(slots)))
    put("expert", np.tile(slots % NE, MAXEXTRA))
    put("block", np.tile(1 + slots // NE, MAXEXTRA))
    return c


def mixer_slabs():
    early = [("mx", 0), ("mx", 1), ("mv", 0), ("mv", 1), ("rq", 0), ("rk", 0), ("rv", 0), ("rv", 1), ("mo", 0),
             ("mo", 1), ("rg", 0), ("rg", 1)] + [("zrw", i) for i in range(7)]
    units = [("unit", (n, d)) for n in (1, 0, 2) for d in range(KT)]
    return early, units, [("out", j) for j in range(4)]


EARLY, UNITS, OUTS = mixer_slabs()
NSLAB = len(EARLY) + len(UNITS) + len(OUTS)
NEARLY_DONE = 2 * KT


class Signal:

    def __init__(self, sem, per_layer=1):
        self.sem, self.per = sem, per_layer

    def __call__(self, layer, k=1):
        return self.sem, layer * self.per + k


class Part:

    def __init__(self, whole, offset):
        self.sem, self.whole, self.offset = whole.sem, whole, offset

    def __call__(self, layer, k=1):
        return self.whole(layer, self.offset + k)


class Turns:

    def __init__(self):
        self.turn, self.used = 0, [0] * RING

    def take(self):
        s = self.turn % RING
        n = self.used[s]
        self.turn, self.used[s] = self.turn + 1, n + 1
        return s, n

    def pass_over(self, n):
        for _ in range(n):
            self.take()

    def loop(self, i, turns):
        inner = Turns()
        inner.turn = self.turn
        per = [0] * RING
        for k in range(turns):
            per[(self.turn + k) % RING] += 1
        inner.used = [self.used[s] + i * per[s] for s in range(RING)]
        return inner

    def after(self, passes, turns, padded=0):
        for k in range(turns):
            self.used[(self.turn + k) % RING] += passes
        self.turn += passes * (turns + padded)


GROUPS = ([("mx", j) for j in range(4)] + [("mif", 0)] + [("mv", j) for j in range(6)] +
          [("rq", j) for j in range(2)] + [("rk", j) for j in range(2)] + [("rv", j) for j in range(6)] +
          [("mo", j) for j in range(4)] + [("rg", j) for j in range(4)] + [("zrw", j) for j in range(ZT)])
NG = len(GROUPS)
AT_CONV, AT_GATES, AT_KEYS, AT_HEADS, AT_STATE, AT_MLNORM, AT_ROTATE, AT_RET, AT_RSTATE = 11, 12, 14, 17, 29, 33, 35, 37, 41


PLACES = [("norm", 24), ("shift", 36), ("lora", 10), ("square", 24), ("bonus", 24), ("pre", 12), ("gram", 6), ("first", 24),
          ("tokens", 2)] + [(f"chunk{c}", 5) for c in range(NC - 2)] + [(f"chunk{NC - 2}", 4), ("samples", 11)]
PRODUCTS = KT + 4
assert sum(n for _, n in PLACES) == PRODUCTS * NEARLY_DONE, sum(n for _, n in PLACES)


def units_at(place, product):
    first = 0
    for name, n in PLACES:
        if name == place:
            return [u for u in range(NEARLY_DONE) if first < PRODUCTS * u + product <= first + n]
        first += n
    return []


def through(kind):
    return 1 + max(n for n, g in enumerate(GROUPS) if g[0] == kind)


def piece_of(kind, j):
    if kind == "mif":
        return None, 0, False
    if kind in ("mv", "rv"):
        return j // 3, j % 3, j % 3 == 2
    return j // 2, j % 2, j % 2 == 1


NPROJ = sum(not piece_of(*g)[2] for g in GROUPS)


def seq4(ap):
    return ap.rearrange("p (b t) -> p b t", t=ST)


def build(nc, a, o):
    with ExitStack() as ctx:
        def sb(name, shape):
            return ctx.enter_context(nc.sbuf_tensor(name, shape, F32))

        def sig(name, per_layer=1):
            return Signal(ctx.enter_context(nc.semaphore(name)), per_layer)

        ps = ctx.enter_context(nc.psum_tensor("ps", [P, 8, 512], F32))
        X = sb("X", [P, KT, T])
        xn = sb("xn", [P, KT, T])
        ring = sb("ring", [P, RING, SLOT])
        lw = sb("lw", [P, NLW])
        vec = sb("vec", [P, DEPTH, NVEC])
        con = sb("con", [P, NCON])
        y_ret, y_ml = sb("y_ret", [P, 4, T]), sb("y_ml", [P, 4, T])
        mixed = sb("mixed", [P, KT, T])
        gate = sb("gate", [P, 2, T])
        rstd = sb("rstd", [P, T])
        gate_bias = sb("gate_bias", [IF, DEPTH])
        m0 = sb("m0", [NH, DEPTH, SB])
        hist = sb("hist", [P, 4 * SB * XPAD])
        prev = sb("prev", [P, ZT * SB])
        conv_out = sb("conv_out", [P, 4, (1 + SB) * XPAD])
        shift_out = sb("shift_out", [P, ZT, 1 + SB])
        m_out = sb("m_out", [NH, 1 + SB])
        n_out = sb("n_out", [P, NH + SB * NH])
        gate_rows = sb("gate_rows", [NH, 1, T])
        ARENA = 26900
        arena = sb("arena", [P, ARENA])

        def at(start, *dims):
            n = int(np.prod(dims))
            assert start + n <= ARENA, (start, dims)
            v = arena[:, start:start + n]
            if len(dims) == 2:
                v = v.rearrange("p (a b) -> p a b", a=dims[0])
            if len(dims) == 3:
                v = v.rearrange("p (a b c) -> p a b c", a=dims[0], b=dims[1])
            if len(dims) == 4:
                v = v.rearrange("p (a b c d) -> p a b c d", a=dims[0], b=dims[1], c=dims[2])
            return v

        def C(name, w, rows=P, off=0):
            return con[0:rows, CON[name] + off:CON[name] + off + w]

        def V(l, name, j=0):
            return vec[:, l, VEC[name] + j:VEC[name] + j + 1]

        norm_sq = at(4158, KT, T)
        z = at(0, ZT, ZP)
        mxp = at(4158, 4, XW)
        ml_o = at(4158, 4, T)
        xc = at(5418, 4, T)
        mq = at(6570, 4, T)
        mk = at(7722, 4, T)
        mkt = at(8874, 3, 512)
        mvt = at(10410, 3, 512)
        C0 = at(11946, SB, NH, P)
        kb = at(16042, 2, 512)
        rows = at(17066, 4, T)
        ml_W = at(18218, PW)
        ml_PW = at(18634, PW)
        ml_sq = at(19050, 4, T)
        ml_den = at(20202, T)
        gwc = at(20490, 24)
        qa = at(20514, TS)
        nq = at(20546, TS)
        aL = at(20578, SB, NH)
        n0 = at(20610, SB * NH)
        Cp = at(20642, 512)
        arow = at(21154, TS)
        rqk = at(21186, 4, T)
        rvt = at(22338, 3, 512)
        qr = at(4158, 4, T)
        rt = at(5310, 4, T)
        ktd = at(6462, 3, 256)
        qd = at(7230, 2, TS)
        rpw = at(7294, 2, PW)
        rkb = at(8126, 2, 256)
        Sp_ret = at(8638, 256)
        ret_o = at(8894, 4, T)
        ret_sq = at(10046, 4, T)
        dec = at(16042, NH, PW)
        S0_ret = at(17706, SB, 2, P)
        zs = at(4158, ZT, T)
        rw_lw = at(8190, 4, T)
        rw_a = at(9342, 4, T)
        rw_kk = at(10494, 4, T)
        rw_kp = at(11646, 4, T)
        rw_e1 = at(12798, 4, T)
        rw_e2 = at(13950, 4, T)
        lora_in = at(15102, T)
        lora_g = at(15390, T)
        rw_g = at(15678, 4, T)
        rw_bv = at(16830, 4, T)
        BK = at(17982, NP4, NC, 2 * CH)
        KR = at(20542, NP4, NC, 2 * CH)
        UV = at(23102, NC, 512)
        PL = at(25662, NP4, 4 + SB)
        rw_o = at(25710, 4, T)
        G = at(0, NC, 2, NP4 * P)
        XT = at(5120, NU, 2 * CH)
        Abd = at(7680, NU, P)
        Xbd = at(10240, NU, P)
        Xc = at(12800, NU, CH)
        Yc = at(14080, NU, CH)
        BKt = at(7680, NC, 512)
        S0bd = at(10240, SB, NP4, P)
        Sbd = at(14336, NP4, P)
        Rn = at(14848, 512)
        CX = at(15360, NP4, 2, TS)
        KBm = [at(14848, 512), at(5120, 512)]
        rw_sq = at(0, 4, T)
        gates = at(1200, 4, T)
        y_rw = at(5700, 4, T)
        hid = at(7000, FT, T)
        sil = at(10200, 3, T)
        xt = at(7000, 3, D)
        xg = at(10072, KT, MB)
        ehid = at(11096, FT, MB)
        esil = at(12504, 3, MB)
        pick_in = at(12888, 3, MB)
        pick_out = at(13272, T)
        yg = at(13560, D)
        comb, posb = at(14600, NE, T), at(16904, NE, T)
        pcon = at(19208, NPC)
        lg, top, gt, eq, cum, ex, posn = (at(20100 + 24 * k, 3, NE) for k in range(7))
        cnt, cnt2 = at(20270, 3), at(20274, 3)
        crow, prow = at(20300, T), at(20600, T)
        slots_n = (MAXB - 1) * NE
        need, rank = at(20900, slots_n), at(20916, slots_n)
        hits, hits2 = at(20940, MAXEXTRA, slots_n), at(21020, MAXEXTRA, slots_n)
        draft = at(21100, PLAN_N)
        plan = ctx.enter_context(nc.sbuf_tensor("plan", [1, PLAN_N], mybir.dt.int32))

        def PCON(name, w, rows=P, off=0):
            return pcon[0:rows, PC[name] + off:PC[name] + off + w]

        slot_ld = [sig(f"slot_loaded{s}") for s in range(RING)]
        slot_fr = [sig(f"slab_used{s}") for s in range(RING)]
        ld_head, ld_con, ld_x, ld_lw, ld_hist = sig("ld_head"), sig("ld_con"), sig("ld_x"), sig("ld_lw"), sig("ld_hist")
        ld_c0, ld_n0, ld_ret, ld_rw = sig("ld_c0"), sig("ld_n0"), sig("ld_ret"), sig("ld_rw")
        st_ml, st_small, st_ret, st_rw, st_y = sig("st_ml"), sig("st_small"), sig("st_ret"), sig("st_rw"), sig("st_y")
        dch, ach = sig("vector_chain"), sig("scalar_chain")
        nm_sq, nm_ms, nm_root, nm_xn = sig("nm_sq", 8), sig("nm_ms"), sig("nm_root"), sig("nm_xn", 8)
        proj, evac = sig("proj", NPROJ), sig("evac", NG)
        pads = sig("pads")
        conv_acc, xc_ok = sig("conv_acc"), sig("xc_ok")
        gate_v, gate_s = sig("gate_rows_vector", 2), sig("gate_rows_scalar", 3)
        u_abs, lf_ok = Part(gate_v, 0), Part(gate_v, 1)
        u_exp, gr_ok, er_ok = Part(gate_s, 0), Part(gate_s, 1), Part(gate_s, 2)
        ml_col, ml_colv = sig("ml_col"), sig("ml_colv")
        mqk_p, mqk_e, kdec_ok = sig("mqk_p", 11), sig("mqk_e", 11), sig("kdec_ok")
        ml_bc, ml_wl, ml_ex, ml_pw = sig("ml_bc", 4), sig("ml_wl", 4), sig("ml_ex", 4), sig("ml_pw", 4)
        ml_s = sig("ml_scores", 4)
        ml_nd, ml_ad, ml_h = sig("ml_nd", 4), sig("ml_ad", 4), sig("ml_h", 4)
        ml_cp, ml_cpe, ml_kb, ml_sc, ml_sca = sig("ml_cp"), sig("ml_cpe"), sig("ml_kb", 8), sig("ml_sc", 8), sig("ml_sca", 8)
        ml_out, co_ok, so_ok = sig("ml_out"), sig("conv_out_ok"), sig("shift_out_ok")
        hn_c, hn_s, hn_x, hn_v = sig("hn_c", 12), sig("hn_s", 12), sig("hn_x", 12), sig("hn_v", 12)
        hn_q, hn_y = sig("hn_q", 12), sig("hn_y", 3)
        r_sw, r_qr, r_kt, r_ktd = sig("r_sw", 4), sig("r_qr"), sig("r_kt", 3), sig("r_ktd", 3)
        r_sc, r_pw, r_o, r_oe = sig("r_sc", 4), sig("r_pw", 4), sig("r_o", 4), sig("r_oe", 4)
        r_sp, r_spe, r_kb, r_ss, r_ssa = sig("r_sp"), sig("r_spe"), sig("r_kb", 8), sig("r_ss", 8), sig("r_ssa", 8)
        w_zs, w_thl, w_lora, w_lorae = sig("w_zs"), sig("w_thl"), sig("w_lora", 12), sig("w_lorae", 12)
        w_sq, w_ss, w_rk, w_bo = sig("w_sq"), sig("w_ss", 4), sig("w_rk"), sig("w_bo", 4)
        w_ssq, w_F, w_E, w_vt, w_vte = sig("w_ssq", 4), sig("w_F"), sig("w_E"), sig("w_vt", 5), sig("w_vte", 5)
        w_pre, w_sz, w_zero, rw_y, w_ob = sig("w_pre"), sig("w_sz"), sig("w_zero", 6), sig("rw_y"), sig("w_ob", 5)
        w_zuv, w_zab = Part(w_zero, 0), Part(w_zero, 4)
        w_g1, w_g1e, w_g2, w_g2e = sig("w_g1", 10), sig("w_g1e", 10), sig("w_g2", 6), sig("w_g2e", 6)
        w_x0 = sig("w_x0")
        w_y, w_ye, w_p, w_pe, w_t, w_te = (sig("w_y", NJOIN), sig("w_ye", NJOIN), sig("w_p", NJOIN), sig("w_pe", NJOIN),
                                           sig("w_t", 16), sig("w_te", 8))

        def join(m, g):
            return sum(LEVEL_GROUPS[:m]) + g + 1

        w_to = sig("w_to", 8)
        w_xt, w_bt, w_bte = sig("w_xt", 2), sig("w_bt", 5), sig("w_bte", 5)
        w_r, w_rn, w_u, w_ue, w_s, w_su, w_oc = (sig("w_r", 5), sig("w_rn", 5), sig("w_u", 5), sig("w_ue", 5),
                                                 sig("w_s", 4), sig("w_su", 4), sig("w_oc", 5))
        w_oe = sig("w_oe", 5)
        w_cx, w_cxe, w_ct = sig("w_cx"), sig("w_cxe"), sig("w_ct")
        w_kb, w_st, w_sta = sig("w_kb", 8), sig("w_st", 8), sig("w_sta", 8)
        u_gate, u_sig, u_mul, u_add = sig("unit_gate", 24), sig("unit_sigmoid", 24), sig("unit_product", 24), sig("unit_sum", 24)
        f_out, x_mix = sig("f_out", 4), sig("x_mix", 8)
        g_done, s_done, h_done = sig("g_done"), sig("s_done"), sig("h_done")
        y_done = sig("y_done")
        rt_p, rt_v = sig("route_tensor", 3), sig("route_vector", 5)
        rt_lg, rt_pos, rt_ct = Part(rt_p, 0), Part(rt_p, 1), Part(rt_p, 2)
        rt_e, rt_sel, rt_cb, rt_cr, plan_ok = (Part(rt_v, k) for k in range(5))
        rt_ex, rt_bc, rt_cbe, rt_pbe = sig("rt_ex"), sig("rt_bc"), sig("rt_cbe"), sig("rt_pbe")
        xt_p, xt_a, xt_d = sig("xt_p"), sig("xt_a"), sig("xt_d")
        in_ok, out_ok = sig("pick_in_ok"), sig("pick_out_ok")
        ga_p, ga_a, ga_d = sig("gather_p"), sig("gather_a"), sig("gather_d")
        do_p, yg_a, yg_d = sig("down_p"), sig("yg_a"), sig("yg_d")
        sc_p, sc_e = sig("scatter_p"), sig("scatter_e")
        ETURNS = FT + DSL
        assert ETURNS % RING == 0 and (FT + KT + 1) % RING == 0
        CREDIT_H, CREDIT_Y = 3, 2

        TOK = ((0, P), (P, P), (TP, TS))

        block = ctx.enter_context(nc.Block())

        @block.sync
        def _(sp):
            turns = Turns()

            def load(turns, src, width):
                s, n = turns.take()
                if not isinstance(n, int) or n > 0:
                    sp.wait_ge(slot_fr[s].sem, n)
                sp.dma_start(ring[:, s, 0:width], src).then_inc(slot_ld[s].sem, 16)

            sp.dma_start(X[:, :, :], a["x"]).then_inc(ld_x.sem, 16)
            sp.dma_start(con[:, 0:CON_HEAD], a["con"][:, 0:CON_HEAD]).then_inc(ld_head.sem, 16)
            sp.dma_start(vec[:, :, :], a["vec"]).then_inc(ld_head.sem, 16)
            sp.dma_start(gate_bias[:, :], a["bias"]).then_inc(ld_con.sem, 16)
            sp.dma_start(m0[:, :, :], a["m0"]).then_inc(ld_con.sem, 16)
            for l in range(DEPTH):
                if l > 0:
                    sp.wait_ge(*x_mix(l - 1, 8))
                    sp.wait_ge(*nm_xn(2 * l - 1, KT))
                for k in range(len(EARLY)):
                    load(turns, a["mix"][l, k], SLOT)
                    if k == 1:
                        sp.dma_start(lw[:, :], a["lw"][l]).then_inc(ld_lw.sem, 16)
                    if l == 0 and k == RING - 1:
                        sp.dma_start(con[:, CON_HEAD:], a["con"][:, CON_HEAD:]).then_inc(ld_con.sem, 16)
                with sp.Fori(0, len(UNITS) // 4) as j:
                    inner = turns.loop(j, 4)
                    for k in range(4):
                        slab = a["mix"][l, bass.ds(j * 4 + (len(EARLY) + k), 1), :, 0:12 * P]
                        load(inner, slab.rearrange("a p n -> p (a n)"), 12 * P)
                turns.after(len(UNITS) // 4, 4)
                for k in range(4):
                    load(turns, a["mix"][l, len(EARLY) + len(UNITS) + k], SLOT)
                if l == 0:
                    with sp.Fori(0, NDENSE) as e:
                        inner = turns.loop(e, FT + KT)
                        for f in range(FT):
                            load(inner, a["gu"][bass.ds(e * FT + f, 1)].rearrange("a p n -> p (a n)"), SLOT)
                        for d in range(KT):
                            load(inner, a["down"][bass.ds(e * KT + d, 1)].rearrange("a p n -> p (a n)"), FT * P)
                    turns.after(NDENSE, FT + KT, 1)
                    continue

                def expert(i, e):
                    inner = turns.loop(i, ETURNS)
                    for f in range(FT):
                        load(inner, a["egu"][bass.ds(e * FT + f, 1)].rearrange("a p n -> p (a n)"), SLOT)
                    for k in range(DSL):
                        width = D * len(DOWN[k])
                        load(inner, a["edown"][bass.ds(e * DSL + k, 1), :, 0:width].rearrange("a p n -> p (a n)"), width)

                sp.wait_ge(*rw_y(l))
                sp.dma_start(pcon, a["pcon"]).then_inc(ld_con.sem, 16)
                expert(0, 0)
                sp.wait_ge(*plan_ok(0))
                npass = sp.value_load(plan[0:1, PLAN_N - 1:PLAN_N], min_val=NE, max_val=NE + MAXEXTRA)
                with sp.Fori(1, npass) as i:
                    expert(i, sp.value_load(plan[0:1, bass.ds(i, 1)], min_val=0, max_val=NE - 1))
            sp.wait_ge(*nm_xn(2 * DEPTH, KT))
            sp.dma_start(o["y"], xn[:, :, :]).then_inc(st_y.sem, 16)
            sp.wait_ge(st_y.sem, 16)

        @block.tensor
        def _(pe):
            turns = Turns()
            mm = pe.matmul

            def slab(turns):
                s, n = turns.take()
                pe.wait_ge(slot_ld[s].sem, (n + 1) * 16)
                return s

            def norm(n):
                for k in range(KT):
                    pe.wait_ge(*nm_sq(n, k + 1))
                    last = mm(ps[:, 0, 0:T], C("ones", P), norm_sq[:, k, :], start=(k == 0), stop=(k == KT - 1))
                last.then_inc(nm_ms.sem, 1)

            current = [None, None]

            def groups(l, first, end):
                for n in range(first, end):
                    kind, j = GROUPS[n]
                    if n >= 4:
                        pe.wait_ge(*evac(l, n - 3))
                    bank = ps[:, n % 4, :]
                    if kind == "mif":
                        pe.wait_ge(ld_lw.sem, 16 * (l + 1))
                        for k in range(KT):
                            w0 = LW["if"] + IF * k
                            last = mm(bank[0:IF, 0:T], lw[:, w0:w0 + IF], xn[:, k, :], start=(k == 0), stop=(k == KT - 1))
                        last.then_inc(proj.sem, 1)
                        continue
                    tokens = kind in ("mv", "rv")
                    piece, part, is_last = piece_of(kind, j)
                    if current[0] != (l, kind, piece):
                        current[0], current[1] = (l, kind, piece), slab(turns)
                    s = current[1]
                    for k in range(KT):
                        if tokens:
                            c0, m = TOK[part]
                            last = mm(bank[0:m, 0:256], xn[:, k, c0:c0 + m], ring[:, s, 256 * k:256 * k + 256],
                                      start=(k == 0), stop=(k == KT - 1))
                        else:
                            if n == 0:
                                pe.wait_ge(*nm_xn(2 * l, k + 1))
                            w0 = 256 * k + P * part
                            last = mm(bank[:, 0:T], ring[:, s, w0:w0 + P], xn[:, k, :],
                                      start=(k == 0), stop=(k == KT - 1))
                    if is_last:
                        last.then_inc(slot_fr[s].sem, 1)
                    else:
                        last.then_inc(proj.sem, 1)

            def head_norm(q, src, sq, centre, ones):
                for j in range(4):
                    last = mm(ps[:, 4 + j, 0:T], centre, src[:, j, :], start=True, stop=True)
                    last.then_inc(hn_c.sem, 1)
                for j in range(4):
                    pe.wait_ge(hn_s.sem, 4 * q + j + 1)
                    pe.wait_ge(hn_x.sem, 4 * q + j + 1)
                    mm(ps[:, 4 + j, 0:T], ones, sq[:, j, :], start=True, stop=True).then_inc(hn_v.sem, 1)

            def mlstm_columns(l):
                pe.wait_ge(ld_con.sem, 48)
                pe.wait_ge(*gr_ok(l))
                for i, (c0, m) in enumerate(TOK):
                    for r in range(2):
                        last = pe.transpose(ps[0:m, 4, 8 * i + 4 * r:8 * i + 4 * r + 4],
                                            (rows[0:NH, 0, c0:c0 + m], rows[0:NH, 3, c0:c0 + m])[r],
                                            C("ident", NH, NH))
                last.then_inc(ml_col.sem, 1)

            def mlstm_qk(l):
                pe.wait_ge(*xc_ok(l))
                for n in range(8):
                    h, which = n // 2, ("wq", "wk")[n % 2]
                    if n >= 2:
                        pe.wait_ge(*mqk_e(l, n - 1))
                    mm(ps[:, 5 + n % 2, 0:T], lw[:, LW[which] + P * h:LW[which] + P * h + P], xc[:, h, :],
                       start=True, stop=True).then_inc(mqk_p.sem, 1)
                for i, (c0, m) in enumerate(TOK):
                    pe.wait_ge(*mqk_e(l, 8 + i - 1))
                    for h in range(NH):
                        last = mm(ps[0:m, 5 + i % 2, P * h:P * h + P], xc[:, h, c0:c0 + m],
                                  lw[:, LW["wk"] + P * h:LW["wk"] + P * h + P], start=True, stop=True)
                    last.then_inc(mqk_p.sem, 1)

            def mlstm_head(l, h):
                if h == 0:
                    pe.wait_ge(*ml_colv(l))
                    pe.wait_ge(*mqk_e(l, 11))
                    pe.wait_ge(*er_ok(l))
                    pe.wait_ge(*evac(l, through("mv")))
                    pe.wait_ge(ld_c0.sem, 16 * (l + 1))
                else:
                    pe.wait_ge(*ml_h(l, h))
                pick = con[0:NH, CON["sel"] + P * h:CON["sel"] + P * h + P]
                mm(ps[:, 4, 0:T], pick, rows[0:NH, 1, :], start=True, stop=True)
                mm(ps[:, 4, T:T + TS], pick, arow[0:NH, :], start=True, stop=True)
                mm(ps[:, 5, 0:T], pick, rows[0:NH, 2, :], start=True, stop=True).then_inc(ml_bc.sem, 1)
                mm(ps[:, 6, 0:TP], mk[:, h, 0:P], mq[:, h, 0:TP], start=True, stop=True)
                mm(ps[:, 6, TP:TP + P], mk[:, h, P:TP], mq[:, h, P:TP], start=True, stop=True)
                mm(ps[0:TS, 6, TP + P:PW], mk[:, h, TP:T], mq[:, h, TP:T], start=True, stop=True).then_inc(ml_s.sem, 1)
                groups(l, AT_HEADS + 3 * h, AT_HEADS + 3 * h + 2)
                pe.wait_ge(*ml_pw(l, h + 1))
                for bank, part in ((7, "num"), (4, "den")):
                    def left(i):
                        rows_ = TOK[i][1]
                        return mvt[0:rows_, i, P * h:P * h + P] if part == "num" else C("ones", P, rows_)
                    mm(ps[:, bank, 0:TP], left(0), ml_PW[:, 0:TP], start=True, stop=False, skip_group_check=True)
                    mm(ps[:, bank, P:TP], left(1), ml_PW[:, TP:TP + P], start=False, stop=False,
                       skip_group_check=True)
                    last = mm(ps[:, bank, TP:T], left(2), ml_PW[0:TS, TP + P:PW], start=False, stop=False,
                              skip_group_check=True)
                    if part == "num":
                        for b in range(SB):
                            cs = slice(ST * b, ST * b + ST)
                            mm(ps[:, bank, TP + ST * b:TP + ST * b + ST], C0[:, b, h, :], qa[:, cs],
                               start=False, stop=(b == SB - 1), skip_group_check=True)
                    else:
                        mm(ps[:, bank, TP:T], C("ones", P), nq, start=False, stop=True,
                           skip_group_check=True).then_inc(ml_nd.sem, 1)

            def mlstm_state(l):
                pe.wait_ge(*kdec_ok(l))
                pe.wait_ge(*ml_h(l, 4))
                for h in range(NH):
                    for i in range(2):
                        mm(ps[:, 4, P * h:P * h + P], mkt[:, i, P * h:P * h + P], mvt[:, i, P * h:P * h + P],
                           start=(i == 0), stop=(i == 1))
                for h in range(NH):
                    for i in range(2):
                        mm(ps[:, 5, h:h + 1], mkt[:, i, P * h:P * h + P], C("ones", 1), start=(i == 0), stop=(i == 1))
                    last = mm(ps[:, 5, 8 + h:8 + SB * NH:NH], mkt[0:TS, 2, P * h:P * h + P], C("bmask", SB, TS),
                              start=True, stop=True)
                last.then_inc(ml_cp.sem, 1)
                for b in range(SB):
                    pe.wait_ge(*ml_kb(l, b + 1))
                    if b >= 2:
                        pe.wait_ge(*ml_sca(l, b - 1))
                    for h in range(NH):
                        last = mm(ps[:, 6 + b % 2, P * h:P * h + P], kb[0:TS, b % 2, P * h:P * h + P],
                                  mvt[0:TS, 2, P * h:P * h + P], start=True, stop=True)
                    last.then_inc(ml_sc.sem, 1)
                    if b % 2 == 1:
                        groups(l, AT_STATE + b // 2, AT_STATE + b // 2 + 1)

            def retention_rotate(l):
                pe.wait_ge(*evac(l, through("rk")))
                for j in range(4):
                    mm(ps[:, 4 + j, 0:T], C("swap", P), rqk[:, j, :], start=True, stop=True).then_inc(r_sw.sem, 1)

            def retention_keys(l):
                pe.wait_ge(*r_qr(l))
                for i, (c0, m) in enumerate(TOK):
                    for j in range(2):
                        last = pe.transpose(ps[0:m, 4 + i, P * j:P * j + P], qr[:, 2 + j, c0:c0 + m], C("ident", P))
                    last.then_inc(r_kt.sem, 1)

            def retention_scores(l, h):
                i, p0 = h // 2, DK * (h % 2)
                if h == 0:
                    pe.wait_ge(*r_ktd(l, 3))
                if h >= 2:
                    pe.wait_ge(*r_pw(l, h - 1))
                bank, r = 4 + h % 2, slice(p0, p0 + DK)
                mm(ps[:, bank, 0:TP], qr[r, 2 + i, 0:P], qr[r, i, 0:TP], start=True, stop=True)
                mm(ps[:, bank, TP:TP + P], qr[r, 2 + i, P:TP], qr[r, i, P:TP], start=True, stop=True)
                mm(ps[0:TS, bank, TP + P:PW], qr[r, 2 + i, TP:T], qr[r, i, TP:T], start=True,
                   stop=True).then_inc(r_sc.sem, 1)

            def retention_values(l, h):
                i, p0 = h // 2, DK * (h % 2)
                r = slice(p0, p0 + DK)
                if h == 0:
                    pe.wait_ge(*evac(l, through("rv")))
                    pe.wait_ge(ld_ret.sem, 32 * (l + 1))
                if h >= 2:
                    pe.wait_ge(*r_oe(l, h - 1))
                pe.wait_ge(*r_pw(l, h + 1))
                bank, w = 6 + h % 2, rpw[:, h % 2, :]
                mm(ps[:, bank, 0:TP], rvt[:, 0, P * h:P * h + P], w[:, 0:TP], start=True, stop=False,
                   skip_group_check=True)
                mm(ps[:, bank, P:TP], rvt[:, 1, P * h:P * h + P], w[:, TP:TP + P], start=False, stop=False,
                   skip_group_check=True)
                mm(ps[:, bank, TP:T], rvt[0:TS, 2, P * h:P * h + P], w[0:TS, TP + P:PW], start=False, stop=False,
                   skip_group_check=True)
                for b in range(SB):
                    last = mm(ps[:, bank, TP + ST * b:TP + ST * b + ST], S0_ret[r, b, i, :],
                              qd[r, i, ST * b:ST * b + ST], start=False, stop=(b == SB - 1), skip_group_check=True)
                last.then_inc(r_o.sem, 1)

            def retention_state(l):
                pe.wait_ge(*r_pw(l, 4))
                pe.wait_ge(*r_oe(l, 4))
                for h in range(NH):
                    i, p0 = h // 2, DK * (h % 2)
                    for t in range(2):
                        last = mm(ps[p0:p0 + DK, 4, P * i:P * i + P], ktd[:, t, DK * h:DK * h + DK],
                                  rvt[:, t, P * h:P * h + P], start=(t == 0), stop=(t == 1))
                last.then_inc(r_sp.sem, 1)
                for b in range(SB):
                    pe.wait_ge(*r_kb(l, b + 1))
                    if b >= 2:
                        pe.wait_ge(*r_ssa(l, b - 1))
                    for h in range(NH):
                        i, p0 = h // 2, DK * (h % 2)
                        last = mm(ps[p0:p0 + DK, 5 + b % 2, P * i:P * i + P], rkb[0:TS, b % 2, DK * h:DK * h + DK],
                                  rvt[0:TS, 2, P * h:P * h + P], start=True, stop=True)
                    last.then_inc(r_ss.sem, 1)
                    if b in (2, 5):
                        groups(l, AT_RSTATE + b // 3, AT_RSTATE + b // 3 + 1)

            def rwkv_prepare(l):
                pe.wait_ge(*w_thl(l))
                pe.wait_ge(*hn_y(l, 2))
                for n in range(12):
                    which, j = n // 4, n % 4
                    if n >= 2:
                        pe.wait_ge(*w_lorae(l, n - 1))
                    r = (slice(0, DK), slice(DK, P), slice(0, P))[which]
                    off = LW["g2" if which == 2 else "lora"] + P * j
                    mm(ps[:, 4 + n % 2, 0:T], lw[r, off:off + P], (lora_g if which == 2 else lora_in)[r, :],
                       start=True, stop=True).then_inc(w_lora.sem, 1)
                    if n >= 2:
                        fill(l, 1)
                pe.wait_ge(*w_lorae(l, 12))
                pe.wait_ge(*w_sq(l))
                for j in range(4):
                    mm(ps[:, 4 + j, 0:T], C("ones64", P), rw_e1[:, j, :], start=True, stop=True)\
                        .then_inc(w_ss.sem, 1)
                fill(l, 24)
                pe.wait_ge(*w_rk(l))
                pe.wait_ge(*w_ssq(l, 4))
                for j in range(4):
                    mm(ps[:, 4 + j, 0:T], C("ones64", P), rw_e2[:, j, :], start=True, stop=True)\
                        .then_inc(w_bo.sem, 1)
                fill(l, 24)
                for c in range(NC):
                    w = CH if c < NC - 1 else TS
                    for j in range(4):
                        last = pe.transpose(ps[0:w, 2 + c % 2, P * j:P * j + P], zs[:, 8 + j, CH * c:CH * c + w],
                                            C("ident", P))
                    last.then_inc(w_vt.sem, 1)
                    if 1 <= c < NC - 1:
                        pe.wait_ge(*w_vte(l, c))
                fill(l, 12)
                pe.wait_ge(*w_vte(l, 5))

            def rwkv_gram(l):
                pe.wait_ge(*w_pre(l))
                for c in range(NC):
                    for p in range(2):
                        n, r = 2 * c + p, slice(CH * p, CH * p + CH)
                        if n >= 4:
                            pe.wait_ge(*w_g1e(l, n - 3))
                        for j in range(NP4):
                            last = mm(ps[:, 2 + n % 4, P * j:P * j + P], BK[r, j, c, :], KR[r, j, c, :],
                                      start=True, stop=True)
                        last.then_inc(w_g1.sem, 1)
                        if n >= 4:
                            fill(l, 1)
                for n in range(6):
                    p, c0 = n % 2, 2 * (n // 2)
                    r = slice(CH * p, CH * p + CH)
                    if n >= 2:
                        pe.wait_ge(*w_g2e(l, n - 1))
                    for c in range(c0, min(c0 + 2, NC)):
                        for j in range(NP4):
                            at_ = 256 * (c - c0) + CH * j
                            last = mm(ps[r, 6 + n % 2, at_:at_ + CH], KR[r, j, c, 0:CH], BK[r, j, c, 0:CH],
                                      start=True, stop=True)
                    last.then_inc(w_g2.sem, 1)
                fill(l, 24)

            def rwkv_invert(l):
                pe.wait_ge(*w_x0(l))
                pe.wait_ge(*w_g2e(l, 6))
                pe.wait_ge(*w_g1e(l, 10))
                for m in range(len(LEVELS)):
                    for g in range(LEVEL_GROUPS[m]):
                        us = range(8 * g, min(8 * g + 8, NU))
                        if m > 0:
                            pe.wait_ge(*(w_te(l, 2 * m - 1), w_to(l, 2 * m - 1))[g])
                        for u in us:
                            last = mm(ps[:, 2 + g, CH * (u - 8 * g):CH * (u - 8 * g) + CH], Abd[:, u, :], Xc[:, u, :],
                                      start=True, stop=True)
                        last.then_inc(w_y.sem, 1)
                    for g in range(LEVEL_GROUPS[m]):
                        us = range(8 * g, min(8 * g + 8, NU))
                        pe.wait_ge(*w_ye(l, join(m, g)))
                        if m > 0:
                            pe.wait_ge(*w_to(l, 2 * m))
                            pe.wait_ge(*w_te(l, 2 * m))
                        for u in us:
                            last = mm(ps[:, 5 + g, CH * (u - 8 * g):CH * (u - 8 * g) + CH], Xbd[:, u, :],
                                      Yc[:, u, :], start=True, stop=True)
                        last.then_inc(w_p.sem, 1)
                    if m < len(LEVELS) - 1:
                        for q in range(4):
                            pe.wait_ge(*w_pe(l, join(m, q // 2)))
                            for k in range(4):
                                u = 4 * q + k
                                last = pe.transpose(ps[0:CH, 2 + q, P * k:P * k + P], Xc[:, u, :],
                                                    C("ident", P))
                            last.then_inc(w_t.sem, 1)

            def rwkv_tokens(l):
                fill(l, 2)
                pe.wait_ge(*w_pe(l, NJOIN))
                for c in range(NC):
                    for j in range(NP4):
                        last = pe.transpose(ps[:, 2 + c, P * j:P * j + P], BK[:, j, c, :], C("ident", P))
                    last.then_inc(w_bt.sem, 1)

            def head_cols(h):
                return slice(CH * h, CH * h + CH)

            def sample_old_state(l, j0):
                if j0 == 0:
                    pe.wait_ge(ld_rw.sem, 16 * (l + 1))
                for j in (j0, j0 + 1):
                    for b in range(SB):
                        dst = ps[:, 7, :].rearrange("p (j q n) -> p j q n", j=8, q=2)[:, j, :, ST * b:ST * b + ST]
                        src = KR[:, j, NC - 1, :].rearrange("p (q n) -> p q n", q=2)[:, :, ST * b:ST * b + ST]
                        last = mm(dst, S0bd[:, b, j, :], src, start=True, stop=True)
                    if j == 3:
                        last.then_inc(w_cx.sem, 1)
                    fill(l, 1)

            def rwkv_chunk(l, c):
                sample = c == NC - 1
                if c == 0:
                    pe.wait_ge(*w_xt(l, 2))
                    pe.wait_ge(*w_bte(l, 5))
                    pe.wait_ge(*w_sz(l))
                for h in range(2 * NP4):
                    j, p = h // 2, h % 2
                    last = mm(ps[0:CH, 2, head_cols(h)], G[:, c, p, P * j:P * j + CH], UV[:, c, head_cols(h)],
                              start=(h == 0), stop=False, skip_group_check=True)
                if not sample:
                    if c > 0:
                        pe.wait_ge(*w_su(l, c))
                    for j in range(NP4):
                        last = mm(ps[0:CH, 2, P * j:P * j + P], KR[:, j, c, 0:CH], Sbd[:, j, :], start=False,
                                  stop=(j == NP4 - 1), skip_group_check=True)
                last.then_inc(w_r.sem, 1)
                obank = 5 + c % 2
                if c >= 2:
                    pe.wait_ge(*w_oe(l, c - 1))
                if sample:
                    pe.wait_ge(*w_cxe(l))
                    for j in range(NP4):
                        last = pe.transpose(ps[0:TS, 7, P * j:P * j + P], CX[:, j, 0, :], C("ident", P))
                    last.then_inc(w_ct.sem, 1)
                else:
                    for j in range(NP4):
                        last = mm(ps[:, obank, CH * j:CH * j + CH], Sbd[:, j, :], KR[:, j, c, CH:2 * CH],
                                  start=(j == 0), stop=False, skip_group_check=True)
                    last.then_inc(w_oc.sem, 1)
                pe.wait_ge(*w_rn(l, c + 1))
                for h in range(2 * NP4):
                    j, p = h // 2, h % 2
                    last = mm(ps[0:CH, 3, head_cols(h)], XT[0:CH, NP4 * c + j, CH * p:CH * p + CH],
                              Rn[0:CH, head_cols(h)], start=True, stop=True)
                last.then_inc(w_u.sem, 1)
                if c < NC - 2:
                    fill(l, 2)
                if c == NC - 2:
                    sample_old_state(l, 0)
                pe.wait_ge(*w_ue(l, c + 1))
                if not sample:
                    for j in range(NP4):
                        last = mm(ps[:, 4, P * j:P * j + P], BKt[:, c, P * j:P * j + P], UV[:, c, P * j:P * j + P],
                                  start=True, stop=True)
                    last.then_inc(w_s.sem, 1)
                for h in range(2 * NP4):
                    j, p = h // 2, h % 2
                    last = mm(ps[CH * p:CH * p + CH, obank, CH * j:CH * j + CH], UV[:, c, head_cols(h)],
                              G[:, c, p, P * j + CH:P * j + P], start=(sample and h < 2), stop=True,
                              skip_group_check=True)
                last.then_inc(w_ob.sem, 1)
                if c < NC - 2:
                    fill(l, 3)
                if c == NC - 2:
                    sample_old_state(l, 2)

            def rwkv_sample_state(l):
                for b in range(SB):
                    pe.wait_ge(*w_kb(l, b + 1))
                    if b >= 2:
                        pe.wait_ge(*w_sta(l, b - 1))
                    for j in range(NP4):
                        last = mm(ps[:, 3 + b % 2, P * j:P * j + P], KBm[b % 2][:, P * j:P * j + P],
                                  UV[:, NC - 1, P * j:P * j + P], start=True, stop=True)
                    last.then_inc(w_st.sem, 1)
                    fill(l, 2 if b < 3 else 1)

            def unit_gate(l, s, bank, k0, k1):
                for k in range(k0, k1):
                    last = mm(ps[:, bank, 0:T], ring[:, s, P * k:P * k + P], xn[:, k, :], start=(k == 0),
                              stop=(k == KT - 1))
                if k1 == KT:
                    last.then_inc(u_gate.sem, 1)

            def unit_branch(s, bank, y, k0=0, k1=4):
                for k in range(k0, k1):
                    last = mm(ps[:, bank, 0:T], ring[:, s, P * (KT + k):P * (KT + k) + P], y[:, k, :],
                              start=(k == 0), stop=(k == 3))
                if k1 == 4:
                    last.then_inc(slot_fr[s].sem, 1)

            filled = [0, 0]

            def fill(l, products):
                for _ in range(products):
                    u, k = filled[0] // PRODUCTS, filled[0] % PRODUCTS
                    if k == 0:
                        filled[1] = slab(turns)
                        if u == 0:
                            pe.wait_ge(*evac(l, NG))
                        else:
                            pe.wait_ge(*u_sig(l, u))
                    if k == KT:
                        if u % KT == 0:
                            pe.wait_ge(*hn_y(l, 1 + u // KT))
                        if u > 0:
                            pe.wait_ge(*u_add(l, u))
                    if k < KT:
                        unit_gate(l, filled[1], 0, k, k + 1)
                    else:
                        unit_branch(filled[1], 1, (y_ml, y_ret)[u // KT], k - KT, k - KT + 1)
                    filled[0] = (filled[0] + 1) % (PRODUCTS * NEARLY_DONE)

            def closing(l):
                pe.wait_ge(*u_sig(l, NEARLY_DONE))
                pe.wait_ge(*u_add(l, NEARLY_DONE))
                base = 24 * l + NEARLY_DONE
                with pe.Fori(0, 2) as i:
                    inner = turns.loop(i, 4)
                    s = [0] * 4
                    for k in range(4):
                        s[k] = slab(inner)
                        pe.wait_ge(u_sig.sem, i * 4 + (base + k - 3))
                        unit_gate(l, s[k], k, 0, KT)
                    pe.wait_ge(*rw_y(l))
                    for k in range(4):
                        pe.wait_ge(u_mul.sem, i * 4 + (base + k - 1))
                        unit_branch(s[k], 4 + k % 2, y_rw)
                turns.after(2, 4)
                pe.wait_ge(*u_add(l, 24))
                for d in range(KT):
                    if d % 2 == 0:
                        s = slab(turns)
                    if d >= 2:
                        pe.wait_ge(*x_mix(l, d - 1))
                    for k in range(KT):
                        w0 = 256 * k + P * (d % 2)
                        last = mm(ps[:, 6 + d % 2, 0:T], ring[:, s, w0:w0 + P], mixed[:, k, :],
                                  start=(k == 0), stop=(k == KT - 1))
                    last.then_inc((slot_fr[s] if d % 2 else f_out).sem, 1)

            def route():
                for i, (c0, m) in enumerate(TOK):
                    for k in range(KT):
                        pe.wait_ge(*nm_xn(3, k + 1))
                        last = mm(ps[0:m, 6, NE * i:NE * i + NE], xn[:, k, c0:c0 + m],
                                  lw[:, LW["router"] + NE * k:LW["router"] + NE * k + NE],
                                  start=(k == 0), stop=(k == KT - 1))
                last.then_inc(rt_lg.sem, 1)
                for n in range(6):
                    c0, m = TOK[n // 2]
                    for k in range(4):
                        last = pe.transpose(ps[0:m, n, P * k:P * k + P], xn[:, 4 * (n % 2) + k, c0:c0 + m], C("ident", P))
                    last.then_inc(xt_p.sem, 1)
                pe.wait_ge(ld_con.sem, 64)
                pe.wait_ge(*rt_sel(0))
                for i, (c0, m) in enumerate(TOK):
                    for k in range(i + 1):
                        mask = PCON("tri", m, TOK[k][1]) if k == i else C("ones", m, TOK[k][1])
                        mm(ps[0:m, 7, NE * i:NE * i + NE], mask, gt[0:TOK[k][1], k, :], start=(k == 0), stop=(k == i))
                for k, (c0, m) in enumerate(TOK):
                    last = mm(ps[0:1, 7, 32:32 + NE], C("ones", 1, m), gt[0:m, k, :], start=(k == 0), stop=(k == 2))
                last.then_inc(rt_pos.sem, 1)
                pe.wait_ge(*rt_cb(0))
                for bank, src in ((6, ex), (7, posn)):
                    for i, (c0, m) in enumerate(TOK):
                        last = pe.transpose(ps[0:NE, bank, c0:c0 + m], src[0:m, i, :], C("ident", m, m))
                last.then_inc(rt_ct.sem, 1)

            def broadcast_rows():
                pe.wait_ge(*rt_cr(0))
                for n in range(2 * NE):
                    e, which = n // 2, n % 2
                    if e >= 2:
                        pe.wait_ge((rt_cbe, rt_pbe)[which].sem, e - 1)
                    mm(ps[:, 2 * which + e % 2, 0:T], con[0:NE, CON["sel"] + P * e:CON["sel"] + P * e + P],
                       (crow, prow)[which][0:NE, :], start=True, stop=True).then_inc(rt_bc.sem, 1)
                pe.wait_ge(rt_cbe.sem, NE)
                pe.wait_ge(rt_pbe.sem, NE)

            def gather(n):
                pe.wait_ge(in_ok.sem, n + 1)
                for k in range(KT):
                    for i, (c0, m) in enumerate(TOK):
                        last = mm(ps[:, 4 + k // 4, P * (k % 4):P * (k % 4) + MB], xt[0:m, i, P * k:P * k + P],
                                  pick_in[0:m, i, :], start=(i == 0), stop=(i == 2))
                    if k % 4 == 3:
                        last.then_inc(ga_p.sem, 1)

            def scatter(n):
                pe.wait_ge(yg_a.sem, n + 1)
                pe.wait_ge(yg_d.sem, n + 1)
                pe.wait_ge(out_ok.sem, n + 1)
                for d in range(KT):
                    if d >= 2:
                        pe.wait_ge(sc_e.sem, n * KT + (d - 1))
                    mm(ps[:, 4 + d % 2, 0:T], yg[:, P * d:P * d + P], pick_out, start=True, stop=True)\
                        .then_inc(sc_p.sem, 1)

            def experts():
                base = FT * NDENSE + CREDIT_H
                pe.wait_ge(xt_a.sem, 3)
                pe.wait_ge(xt_d.sem, 3)
                gather(0)
                broadcast_rows()
                pe.wait_ge(*plan_ok(0))
                npass = pe.value_load(plan[0:1, PLAN_N - 1:PLAN_N], min_val=NE, max_val=NE + MAXEXTRA)
                with pe.Fori(0, npass) as i:
                    inner = turns.loop(i, ETURNS)
                    pe.wait_ge(ga_a.sem, i + 1)
                    pe.wait_ge(ga_d.sem, i + 1)
                    for f in range(FT):
                        if f == 3:
                            scatter(i)
                        s = slab(inner)
                        pe.wait_ge(h_done.sem, i * FT + (base + max(f - 1, 0)))
                        for w in range(2):
                            for k in range(KT):
                                w0 = P * (KT * w + k)
                                last = mm(ps[:, 2 * (f % 2) + w, 0:MB], ring[:, s, w0:w0 + P], xg[:, k, :],
                                          start=(k == 0), stop=(k == KT - 1))
                            last.then_inc((slot_fr[s] if w else g_done).sem, 1)
                    pe.wait_ge(sc_e.sem, i * KT + KT)
                    gather(i + 1)
                    for tiles in DOWN:
                        s = slab(inner)
                        for n, f in enumerate(tiles):
                            pe.wait_ge(h_done.sem, i * FT + (base + f + 1))
                            for w in range(2):
                                w0 = D * n + 512 * w
                                last = mm(ps[:, 6 + w, :], ehid[:, f, :], ring[:, s, w0:w0 + 512],
                                          start=(f == 0), stop=(f == FT - 1))
                                if f == FT - 1 and w == 0:
                                    last.then_inc(do_p.sem, 1)
                        last.then_inc(slot_fr[s].sem, 1)
                pe.wait_ge(ga_a.sem, npass + 1)
                pe.wait_ge(ga_d.sem, npass + 1)
                scatter(npass)

            def feed_forward():
                with pe.Fori(0, NDENSE) as e:
                    inner = turns.loop(e, FT + KT)
                    for f in range(FT):
                        s = slab(inner)
                        pe.wait_ge(h_done.sem, e * FT + (f + (2 if f < 2 else 1)))
                        for w in range(2):
                            for k in range(KT):
                                if f == 0 and w == 0:
                                    pe.wait_ge(*nm_xn(1, k + 1))
                                w0 = P * (KT * w + k)
                                last = mm(ps[:, 2 * (f % 3) + w, 0:T], ring[:, s, w0:w0 + P], xn[:, k, :],
                                          start=(k == 0), stop=(k == KT - 1))
                            last.then_inc((slot_fr[s] if w else g_done).sem, 1)
                    for d in range(KT):
                        s = slab(inner)
                        pe.wait_ge(y_done.sem, e * KT + (d + 1))
                        for f in range(FT):
                            if d == 0:
                                pe.wait_ge(h_done.sem, e * FT + (CREDIT_H + f + 1))
                            last = mm(ps[:, 6 + d % 2, 0:T], ring[:, s, P * f:P * f + P], hid[:, f, :],
                                      start=(f == 0), stop=(f == FT - 1))
                        last.then_inc(slot_fr[s].sem, 1)
                turns.after(NDENSE, FT + KT, 1)

            pe.wait_ge(ld_head.sem, 32)
            for l in range(DEPTH):
                norm(2 * l)
                groups(l, 0, AT_HEADS)
                mlstm_columns(l)
                mlstm_qk(l)
                for h in range(NH):
                    mlstm_head(l, h)
                    groups(l, AT_HEADS + 3 * h + 2, AT_HEADS + 3 * h + 3)
                mlstm_state(l)
                pe.wait_ge(*ml_sca(l, 8))
                pe.wait_ge(*ml_cpe(l))
                pe.wait_ge(*ml_out(l))
                head_norm(3 * l, ml_o, ml_sq, C("cent128", P), C("ones", P))
                groups(l, AT_MLNORM, AT_ROTATE)
                pe.wait_ge(*hn_q(l, 4))
                retention_rotate(l)
                groups(l, AT_ROTATE, AT_RET)
                retention_keys(l)
                retention_scores(l, 0)
                for h in range(NH):
                    if h < NH - 1:
                        retention_scores(l, h + 1)
                    retention_values(l, h)
                    groups(l, AT_RET + h, AT_RET + h + 1)
                retention_state(l)
                pe.wait_ge(*r_ssa(l, 8))
                pe.wait_ge(*r_spe(l))
                head_norm(3 * l + 1, ret_o, ret_sq, C("cent128", P), C("ones", P))
                fill(l, 60)
                rwkv_prepare(l)
                rwkv_gram(l)
                rwkv_invert(l)
                rwkv_tokens(l)
                for c in range(NC):
                    rwkv_chunk(l, c)
                rwkv_sample_state(l)
                pe.wait_ge(*w_oe(l, 5))
                pe.wait_ge(*w_sta(l, 8))
                head_norm(3 * l + 2, rw_o, rw_sq, C("cent64", P), C("ones64", P))
                closing(l)
                norm(2 * l + 1)
                if l == 0:
                    feed_forward()
                else:
                    route()
                    experts()
            norm(2 * DEPTH)

        @block.scalar
        def _(act):
            turns = Turns()
            A = act.activation
            links = [0]

            def link(ins):
                links[0] += 1
                ins.then_inc(ach.sem, 1)
                act.wait_ge(ach.sem, links[0])

            def norm(n, npass=None):
                if n % 2 == 1:
                    act.wait_ge(st_rw.sem, 32 * (n // 2 + 1))
                if n == 0:
                    act.wait_ge(ld_x.sem, 16)
                for k in range(KT):
                    if n % 2 == 1:
                        act.wait_ge(*x_mix(n // 2, k + 1))
                    elif n == 2:
                        act.wait_ge(y_done.sem, CREDIT_Y + KT * (NDENSE - 1) + k + 1)
                    elif n > 2:
                        act.wait_ge(sc_e.sem, npass * KT + (k + 1))
                    A(norm_sq[:, k, :], X[:, k, :], ACT.Square).then_inc(nm_sq.sem, 1)
                act.wait_ge(*nm_ms(n))
                A(rstd[:, :], ps[:, 0, 0:T], ACT.Sqrt, scale=1.0 / D, bias=C("eps", 1)).then_inc(nm_root.sem, 1)

            current = [None, 0, 0]

            def projections(l, first, end):
                for n in range(first, end):
                    kind, j = GROUPS[n]
                    piece, part, is_last = piece_of(kind, j)
                    if piece is not None and current[0] != (l, kind, piece):
                        current[0] = (l, kind, piece)
                        current[1:] = turns.take()
                    if is_last:
                        act.wait_ge(slot_fr[current[1]].sem, current[2] + 1)
                    else:
                        act.wait_ge(*proj(l, sum(not piece_of(*g)[2] for g in GROUPS[:n + 1])))
                    src = ps[:, n % 4, 0:T]
                    if kind == "mx":
                        A(mxp[:, j, XPAD:XPAD + TP], src[:, 0:TP], ACT.Copy)
                        dst = mxp[:, j, XPAD + TP:].rearrange("p (b t) -> p b t", b=SB)[:, :, XPAD:]
                        last = A(dst, seq4(src[:, TP:T]), ACT.Copy)
                    elif kind == "zrw":
                        A(z[:, j, 1:1 + TP], src[:, 0:TP], ACT.Copy)
                        dst = z[:, j, 1 + TP:].rearrange("p (b t) -> p b t", b=SB)[:, :, 1:]
                        last = A(dst, seq4(src[:, TP:T]), ACT.Copy)
                    elif kind == "mif":
                        act.wait_ge(ld_con.sem, 48)
                        A(rows[0:NH, 0, :], src[0:NH, :], ACT.Identity, bias=gate_bias[0:NH, l:l + 1])
                        last = A(rows[0:NH, 1, :], src[32:IF, :], ACT.Identity, bias=gate_bias[32:IF, l:l + 1])
                    elif kind in ("mv", "rv"):
                        m = TOK[part][1]
                        dst = (mvt if kind == "mv" else rvt)[0:m, part, 256 * piece:256 * piece + 256]
                        last = A(dst, ps[0:m, n % 4, 0:256], ACT.Copy)
                    elif kind in ("rq", "rk"):
                        last = A(rqk[:, j + (2 if kind == "rk" else 0), :], src, ACT.Copy,
                                 scale=1.0 if kind == "rq" else DK ** -0.5)
                    elif kind == "mo":
                        last = A(y_ml[:, j, :], src, ACT.Sigmoid)
                    else:
                        last = A(y_ret[:, j, :], src, ACT.Silu)
                    last.then_inc(evac.sem, 1)

            def head_norm(q, src, sq, n, eps):
                for j in range(4):
                    act.wait_ge(hn_x.sem, 4 * q + j + 1)
                    A(sq[:, j, :], src[:, j, :], ACT.Square).then_inc(hn_s.sem, 1)
                for j in range(4):
                    act.wait_ge(hn_v.sem, 4 * q + j + 1)
                    A(sq[:, j, :], ps[:, 4 + j, 0:T], ACT.Sqrt, scale=1.0 / n, bias=C("eps", 1, P, eps))\
                        .then_inc(hn_q.sem, 1)
                if q % 3 == 1:
                    unit_gates(q // 3, "norm")
                    unit_gates(q // 3, "shift")

            def mlstm_gates(l):
                act.wait_ge(*u_abs(l))
                link(A(rows[0:NH, 2, :], rows[0:NH, 2, :], ACT.Exp, scale=-1.0))
                A(rows[0:NH, 2, :], rows[0:NH, 2, :], ACT.Ln, bias=1.0).then_inc(u_exp.sem, 1)
                projections(l, AT_GATES, AT_KEYS)
                act.wait_ge(*lf_ok(l))
                A(rows[0:NH, 3, :], rows[0:NH, 3, :], ACT.Exp)
                A(arow[0:NH, :], arow[0:NH, :], ACT.Exp).then_inc(gr_ok.sem, 1)
                A(rows[0:NH, 2, :], rows[0:NH, 2, :], ACT.Exp, scale=-1.0).then_inc(er_ok.sem, 1)

            def mlstm_qk(l):
                for n in range(11):
                    act.wait_ge(*mqk_p(l, n + 1))
                    if n < 8:
                        h = n // 2
                        last = A((mq, mk)[n % 2][:, h, :], ps[:, 5 + n % 2, 0:T], ACT.Copy,
                                 scale=(1.0, P ** -0.5)[n % 2])
                    else:
                        m = TOK[n - 8][1]
                        last = A(mkt[0:m, n - 8, :], ps[0:m, 5 + n % 2, :], ACT.Copy, scale=P ** -0.5)
                    last.then_inc(mqk_e.sem, 1)

            def mlstm_head(l, h):
                act.wait_ge(*ml_wl(l, h + 1))
                A(ml_W[:, 0:TP + P], ml_W[:, 0:TP + P], ACT.Exp)
                A(ml_W[0:TS, TP + P:PW], ml_W[0:TS, TP + P:PW], ACT.Exp).then_inc(ml_ex.sem, 1)
                projections(l, AT_HEADS + 3 * h, AT_HEADS + 3 * h + 2)
                act.wait_ge(*ml_nd(l, h + 1))
                A(ml_den, ps[:, 4, 0:T], ACT.Abs).then_inc(ml_ad.sem, 1)

            def mlstm_state(l):
                act.wait_ge(*ml_cp(l))
                if l > 0:
                    act.wait_ge(st_ml.sem, 64 * l)
                A(Cp, ps[:, 4, :], ACT.Copy)
                A(n_out[:, 0:NH], ps[:, 5, 0:NH], ACT.Copy).then_inc(ml_cpe.sem, 1)

            def retention(l):
                for h in range(NH):
                    act.wait_ge(*r_o(l, h + 1))
                    A(ret_o[:, h, :], ps[:, 6 + h % 2, 0:T], ACT.Copy).then_inc(r_oe.sem, 1)
                    projections(l, AT_RET + h, AT_RET + h + 1)
                act.wait_ge(*r_sp(l))
                A(Sp_ret, ps[:, 4, 0:256], ACT.Copy).then_inc(r_spe.sem, 1)

            def rwkv_prepare(l):
                act.wait_ge(*w_zs(l))
                A(lora_in[0:DK, :], zs[0:DK, 12, :], ACT.Tanh)
                A(lora_in[DK:P, :], zs[DK:P, 12, :], ACT.Copy)
                A(lora_g, zs[:, 13, :], ACT.Sigmoid).then_inc(w_thl.sem, 1)
                act.wait_ge(st_ret.sem, 32 * (l + 1))
                for n in range(12):
                    which, j = n // 4, n % 4
                    act.wait_ge(*w_lora(l, n + 1))
                    src = ps[:, 4 + n % 2, 0:T]
                    if which == 2:
                        last = A(rw_g[:, j, :], src, ACT.Copy)
                    else:
                        last = A((rw_lw, rw_a)[which][:, j, :], src, ACT.Sigmoid,
                                 bias=V(l, ("w0", "a0")[which], j))
                    last.then_inc(w_lorae.sem, 1)
                unit_gates(l, "lora")
                for j in range(4):
                    act.wait_ge(*w_ss(l, j + 1))
                    A(rw_e1[:, j, :], ps[:, 4 + j, 0:T], ACT.Sqrt).then_inc(w_ssq.sem, 1)
                unit_gates(l, "square")
                unit_gates(l, "bonus", 0, 1)
                act.wait_ge(*w_F(l))
                A(rw_e2, rw_e2, ACT.Exp)
                A(rw_lw, rw_e1, ACT.Exp, scale=-1.0)
                A(rw_e1, rw_e1, ACT.Exp).then_inc(w_E.sem, 1)
                unit_gates(l, "bonus", 1)
                for c in range(NC):
                    act.wait_ge(*w_vt(l, c + 1))
                    if c == 0:
                        act.wait_ge(*w_zuv(l, 4))
                    w = CH if c < NC - 1 else TS
                    A(UV[CH:CH + w, c, :], ps[0:w, 2 + c % 2, :], ACT.Copy).then_inc(w_vte.sem, 1)
                unit_gates(l, "pre")

            def rwkv_invert(l):
                for m in range(len(LEVELS)):
                    for g in range(LEVEL_GROUPS[m]):
                        n = min(8, NU - 8 * g)
                        act.wait_ge(*w_y(l, join(m, g)))
                        A(Yc[:, 8 * g:8 * g + n, :], ps[:, 2 + g, 0:CH * n].rearrange("p (a b) -> p a b", a=n),
                          ACT.Copy).then_inc(w_ye.sem, 1)
                    if m < len(LEVELS) - 1:
                        for q in (0, 2):
                            act.wait_ge(*w_t(l, 4 * m + q + 1))
                            src = ps[0:CH, 2 + q, :].rearrange("p (a b) -> p a b", a=4)
                            A(Xbd[0:CH, 4 * q:4 * q + 4, 0:CH], src[:, :, 0:CH], ACT.Copy)
                            A(Xbd[CH:P, 4 * q:4 * q + 4, CH:P], src[:, :, CH:P], ACT.Copy).then_inc(w_te.sem, 1)
                unit_gates(l, "tokens")
                act.wait_ge(*w_pe(l, NJOIN))
                A(XT[0:CH, :, 0:CH], Xc[0:CH, :, :], ACT.Copy).then_inc(w_xt.sem, 1)
                for c in range(NC):
                    act.wait_ge(*w_bt(l, c + 1))
                    A(BKt[:, c, :], ps[:, 2 + c, :], ACT.Copy).then_inc(w_bte.sem, 1)
                    if c == 0:
                        act.wait_ge(*w_xt(l, 2))
                        act.dma_start(S0bd, a["rw"][l]).then_inc(ld_rw.sem, 16)

            def rwkv_chunks(l):
                for c in range(NC):
                    if c == NC - 1:
                        act.wait_ge(*w_cx(l))
                        A(CX, ps[:, 7, 0:256].rearrange("p (j q n) -> p j q n", j=4, q=2), ACT.Copy)\
                            .then_inc(w_cxe.sem, 1)
                    act.wait_ge(*w_u(l, c + 1))
                    A(UV[0:CH, c, :], ps[0:CH, 3, :], ACT.Copy).then_inc(w_ue.sem, 1)
                    if c < NC - 1:
                        act.wait_ge(*w_ob(l, c + 1))
                        A(rw_o[:, :, CH * c:CH * c + CH],
                          ps[:, 5 + c % 2, 0:256].rearrange("p (a b) -> p a b", a=4), ACT.Copy).then_inc(w_oe.sem, 1)
                        unit_gates(l, f"chunk{c}")
                unit_gates(l, "samples")

            def unit_gates(l, place, first=0, end=None):
                for u in units_at(place, KT)[first:end]:
                    act.wait_ge(*u_gate(l, u + 1))
                    if u >= 2:
                        act.wait_ge(*u_add(l, u - 1))
                    A(gate[:, u % 2, :], ps[:, 0, 0:T], ACT.Sigmoid).then_inc(u_sig.sem, 1)

            def closing(l):
                base = 24 * l + NEARLY_DONE
                with act.Fori(0, 2) as i:
                    for k in range(4):
                        act.wait_ge(u_gate.sem, i * 4 + (base + k + 1))
                        act.wait_ge(u_add.sem, i * 4 + (base + k - 3))
                        A(gates[:, k, :], ps[:, k, 0:T], ACT.Sigmoid).then_inc(u_sig.sem, 1)
                turns.pass_over(len(UNITS) + len(OUTS))

            def feed_forward():
                with act.Fori(0, NDENSE) as e:
                    for f in range(FT):
                        act.wait_ge(g_done.sem, e * FT + (f + 1))
                        A(sil[:, f % 3, :], ps[:, 2 * (f % 3), 0:T], ACT.Silu).then_inc(s_done.sem, 1)
                turns.after(NDENSE, FT + KT, 1)

            def gathered(n):
                act.wait_ge(ga_p.sem, n * 2 + 1)
                A(xg[:, 0:4, :], ps[:, 4, :].rearrange("p (k n) -> p k n", k=4), ACT.Copy).then_inc(ga_a.sem, 1)

            def experts():
                act.wait_ge(*rt_e(0))
                A(ex, ex, ACT.Exp).then_inc(rt_ex.sem, 1)
                for n in (0, 2, 4):
                    act.wait_ge(xt_p.sem, n + 1)
                    m = TOK[n // 2][1]
                    A(xt[0:m, n // 2, 0:512], ps[0:m, n, :], ACT.Copy).then_inc(xt_a.sem, 1)
                gathered(0)
                for e in range(NE):
                    act.wait_ge(rt_bc.sem, 2 * e + 1)
                    A(comb[:, e, :], ps[:, e % 2, 0:T], ACT.Copy).then_inc(rt_cbe.sem, 1)
                act.wait_ge(*plan_ok(0))
                npass = act.value_load(plan[0:1, PLAN_N - 1:PLAN_N], min_val=NE, max_val=NE + MAXEXTRA)
                with act.Fori(0, npass) as i:
                    for f in range(FT):
                        act.wait_ge(g_done.sem, i * FT + (FT * NDENSE + f + 1))
                        A(esil[:, f % 3, :], ps[:, 2 * (f % 2), 0:MB], ACT.Silu).then_inc(s_done.sem, 1)
                    gathered(i + 1)
                    act.wait_ge(do_p.sem, i + 1)
                    A(yg[:, 0:512], ps[:, 6, :], ACT.Copy).then_inc(yg_a.sem, 1)
                return npass

            act.wait_ge(ld_head.sem, 32)
            for l in range(DEPTH):
                norm(2 * l)
                projections(l, 0, AT_CONV)
                act.wait_ge(*conv_acc(l))
                A(xc, xc, ACT.Silu).then_inc(xc_ok.sem, 1)
                projections(l, AT_CONV, AT_GATES)
                mlstm_gates(l)
                projections(l, AT_KEYS, AT_HEADS)
                mlstm_qk(l)
                for h in range(NH):
                    mlstm_head(l, h)
                    projections(l, AT_HEADS + 3 * h + 2, AT_HEADS + 3 * h + 3)
                mlstm_state(l)
                projections(l, AT_STATE, AT_MLNORM)
                head_norm(3 * l, ml_o, ml_sq, P, 1)
                projections(l, AT_MLNORM, AT_RET)
                retention(l)
                projections(l, AT_RSTATE, NG)
                head_norm(3 * l + 1, ret_o, ret_sq, P, 1)
                rwkv_prepare(l)
                unit_gates(l, "gram")
                unit_gates(l, "first")
                rwkv_invert(l)
                rwkv_chunks(l)
                head_norm(3 * l + 2, rw_o, rw_sq, CH, 2)
                closing(l)
                norm(2 * l + 1)
                if l == 0:
                    feed_forward()
                else:
                    npass = experts()
            norm(2 * DEPTH, npass)

        @block.vector
        def _(dve):
            turns = Turns()
            links = [0]
            TT, TSC, STT = dve.tensor_tensor, dve.tensor_scalar, dve.scalar_tensor_tensor
            MUL, ADD, SUB, MAX, MIN = ALU.mult, ALU.add, ALU.subtract, ALU.max, ALU.min

            def link(ins):
                links[0] += 1
                ins.then_inc(dch.sem, 1)
                dve.wait_ge(dch.sem, links[0])

            def mid(ap, n):
                return ap.unsqueeze(1).broadcast_to([ap.shape[0], n, ap.shape[1]])

            def end(ap, n):
                return ap.unsqueeze(len(ap.shape)).broadcast_to(list(ap.shape) + [n])

            def norm(n):
                l = min(n // 2, DEPTH - 1)
                gain = "final" if n == 2 * DEPTH else ("norm_mix", "norm_ffn")[n % 2]
                dve.wait_ge(*nm_root(n))
                link(dve.reciprocal(rstd[:, :], rstd[:, :]))
                for k in range(KT):
                    STT(xn[:, k, :], X[:, k, :], V(l, gain, k), rstd[:, :], MUL, MUL).then_inc(nm_xn.sem, 1)

            def head_norm(q, src, sq, finish):
                for j in range(4):
                    dve.wait_ge(hn_c.sem, 4 * q + j + 1)
                    dve.tensor_copy(src[:, j, :], ps[:, 4 + j, 0:T]).then_inc(hn_x.sem, 1)
                for j in range(4):
                    dve.wait_ge(hn_q.sem, 4 * q + j + 1)
                    last = dve.reciprocal(sq[:, j, :], sq[:, j, :])
                if q % 3 == 1:
                    unit_sums(q // 3, "norm", 0, 1)
                link(last)
                finish()

            def histories(l):
                dve.wait_ge(ld_hist.sem, 32 * (l + 1))
                dve.memset(mxp[:, :, 0:XPAD], 0.0)
                dve.memset(z[:, :, 0:1], 0.0)
                for j in range(4):
                    dst = mxp[:, j, XPAD + TP:].rearrange("p (b t) -> p b t", b=SB)[:, :, 0:XPAD]
                    src = hist[:, j * SB * XPAD:(j + 1) * SB * XPAD].rearrange("p (b t) -> p b t", b=SB)
                    dve.tensor_copy(dst, src)
                zc = z[:, :, 1 + TP:].rearrange("p j (b t) -> p j b t", b=SB)[:, :, :, 0]
                link(dve.tensor_copy(zc, prev[:, :].rearrange("p (j b) -> p j b", b=SB)))

            def conv(l):
                for j in range(4):
                    dve.wait_ge(*evac(l, j + 1))
                    smp = mxp[:, j, XPAD + TP:].rearrange("p (b t) -> p b t", b=SB)
                    for k in range(CONV):
                        w = V(l, "conv_w", 4 * k + j)
                        accp, accs = xc[:, j, 0:TP], seq4(xc[:, j, TP:T])
                        inp, ins = mxp[:, j, k:k + TP], smp[:, :, k:k + ST]
                        if k == 0:
                            TSC(accp, inp, w, V(l, "conv_b", j), MUL, ADD)
                            last = TSC(accs, ins, w, V(l, "conv_b", j), MUL, ADD)
                        else:
                            STT(accp, inp, w, accp, MUL, ADD)
                            last = STT(accs, ins, w, accs, MUL, ADD)
                        if k < CONV - 1:
                            link(last)
                last.then_inc(conv_acc.sem, 1)
                if l > 0:
                    dve.wait_ge(st_small.sem, 32 * l)
                dve.tensor_copy(conv_out[:, :, 0:XPAD], mxp[:, :, TP:TP + XPAD])
                src = mxp[:, :, XPAD + TP:].rearrange("p j (b t) -> p j b t", b=SB)[:, :, :, ST:]
                link(dve.tensor_copy(conv_out[:, :, XPAD:].rearrange("p j (b t) -> p j b t", b=SB), src))
                conv_out_ok(l)

            def conv_out_ok(l):
                dve.sem_inc(co_ok.sem, 1)

            def mlstm_gates(l):
                R = [rows[0:NH, k, :] for k in range(4)]
                cum = gate_rows[0:NH, 0, :]
                dve.wait_ge(*evac(l, through("mif")))
                dve.wait_ge(ld_con.sem, 48)
                link(TSC(R[2], R[1], -1.0, None, MUL))
                link(TT(R[2], R[2], R[1], MAX))
                TSC(R[1], R[1], 0.0, None, MIN).then_inc(u_abs.sem, 1)
                dve.wait_ge(*u_exp(l))
                link(TT(R[1], R[1], R[2], SUB))
                link(dve.tensor_tensor_scan(R[3], C("reset_mul", T, NH), R[1], 0.0, MUL, ADD))
                link(TT(R[0], R[0], R[3], SUB))
                link(dve.tensor_tensor_scan(cum, C("reset_add", T, NH), R[0], 0.0, ADD, MAX))
                TSC(cum[:, 0:TP], cum[:, 0:TP], 0.0, None, MAX)
                m0b = end(m0[:, l, :], ST)
                link(TT(seq4(cum[:, TP:T]), seq4(cum[:, TP:T]), m0b, MAX))
                TSC(R[1], cum, -1.0, None, MUL)
                TT(R[2], R[3], cum, ADD)
                link(TT(seq4(arow[0:NH, :]), m0b, seq4(cum[:, TP:T]), SUB))
                if l > 0:
                    dve.wait_ge(st_ml.sem, 64 * l)
                dve.tensor_copy(m_out[:, 0:1], R[2][:, TP - 1:TP])
                dve.tensor_copy(m_out[:, 1:1 + SB], seq4(R[2][:, TP:T])[:, :, ST - 1])
                TSC(R[3][:, 0:TP], R[0][:, 0:TP], cum[:, TP - 1:TP], None, SUB)
                lastM = seq4(cum[:, TP:T])[:, :, ST - 1:ST].broadcast_to([NH, SB, ST])
                TT(seq4(R[3][:, TP:T]), seq4(R[0][:, TP:T]), lastM, SUB).then_inc(lf_ok.sem, 1)
                dve.wait_ge(*ml_col(l))
                dve.tensor_copy(gwc[:, 0:16], ps[:, 4, 0:16])
                link(dve.tensor_copy(gwc[0:TS, 16:24], ps[0:TS, 4, 16:24]))
                dve.sem_inc(ml_colv.sem, 1)

            def mlstm_keys(l):
                dve.wait_ge(*mqk_e(l, 11))
                for i, (_, m) in enumerate(TOK):
                    v = mkt[0:m, i, :].rearrange("p (h e) -> p h e", h=NH)
                    last = TT(v, v, end(gwc[0:m, 8 * i + 4:8 * i + 8], P), MUL)
                last.then_inc(kdec_ok.sem, 1)

            def mlstm_head(l, h):
                dve.wait_ge(*ml_bc(l, h + 1))
                dve.tensor_copy(aL[:, :, h], seq4(ps[:, 4, T:T + TS])[:, :, ST - 1])
                link(TT(qa, mq[:, h, TP:T], ps[:, 4, T:T + TS], MUL))
                if h == 0:
                    dve.wait_ge(ld_n0.sem, 16 * (l + 1))
                n0v = end(n0.rearrange("p (b h) -> p b h", b=SB)[:, :, h], ST)
                TT(seq4(nq), seq4(qa), n0v, MUL)
                g = [gwc[:, 8 * i + h:8 * i + h + 1] for i in range(3)]
                STT(ml_W[:, 0:P], ps[:, 4, 0:P], g[0], C("causal_neg", P), ADD, ADD)
                TSC(ml_W[:, P:TP], ps[:, 4, P:TP], g[0], None, ADD)
                STT(ml_W[:, TP:TP + P], ps[:, 4, P:TP], g[1], C("causal_neg", P), ADD, ADD)
                STT(ml_W[0:TS, TP + P:PW], ps[0:TS, 4, TP:T], g[2][0:TS, :], C("sample_neg", TS, TS), ADD, ADD)\
                    .then_inc(ml_wl.sem, 1)
                dve.wait_ge(*ml_ex(l, h + 1))
                dve.wait_ge(*ml_s(l, h + 1))
                TT(ml_PW[:, 0:TP + P], ps[:, 6, 0:TP + P], ml_W[:, 0:TP + P], MUL)
                TT(ml_PW[0:TS, TP + P:PW], ps[0:TS, 6, TP + P:PW], ml_W[0:TS, TP + P:PW], MUL)\
                    .then_inc(ml_pw.sem, 1)
                dve.wait_ge(*ml_ad(l, h + 1))
                link(TT(ml_den, ml_den, ps[:, 5, 0:T], MAX))
                link(dve.reciprocal(ml_den, ml_den))
                TT(ml_o[:, h, :], ps[:, 7, 0:T], ml_den, MUL).then_inc(ml_h.sem, 1)

            def mlstm_state(l):
                dve.wait_ge(*ml_cpe(l))
                for b in range(SB):
                    if b >= 2:
                        dve.wait_ge(*ml_sc(l, b - 1))
                    TSC(kb[0:TS, b % 2, :], mkt[0:TS, 2, :], C("bmask", 1, TS, b), None, MUL).then_inc(ml_kb.sem, 1)
                    if b > 0:
                        update(l, b - 1)
                update(l, SB - 1)
                link(TT(n_out[:, NH:], n0, aL.rearrange("p b h -> p (b h)"), MUL))
                TT(n_out[:, NH:], n_out[:, NH:], ps[:, 5, 8:8 + SB * NH], ADD).then_inc(ml_out.sem, 1)

            def update(l, b):
                link(TT(C0[:, b, :, :], C0[:, b, :, :], end(aL[:, b, :], P), MUL))
                dve.wait_ge(*ml_sc(l, b + 1))
                v = ps[:, 6 + b % 2, :].rearrange("p (h e) -> p h e", h=NH)
                TT(C0[:, b, :, :], C0[:, b, :, :], v, ADD).then_inc(ml_sca.sem, 1)

            def mlstm_finish(l):
                for j in range(4):
                    last = STT(ml_o[:, j, :], ml_o[:, j, :], V(l, "ml_gn", j), ml_sq[:, j, :], MUL, MUL)
                link(last)
                for j in range(4):
                    last = STT(ml_o[:, j, :], xc[:, j, :], V(l, "ml_skip", j), ml_o[:, j, :], MUL, ADD)
                link(last)
                dve.wait_ge(*evac(l, through("mo")))
                TT(y_ml[:, :, :], ml_o, y_ml[:, :, :], MUL).then_inc(hn_y.sem, 1)

            def retention(l):
                TT(qr, rqk, mid(C("cos", T), 4), MUL)
                for j in range(4):
                    dve.wait_ge(*r_sw(l, j + 1))
                    last = TT(rt[:, j, :], ps[:, 4 + j, 0:T], C("sin", T), MUL)
                link(last)
                link(TT(qr, qr, rt, ADD))
                for i in range(2):
                    last = TT(qd[:, i, :], qr[:, i, TP:T], C("qdec", TS, P, TS * i), MUL)
                last.then_inc(r_qr.sem, 1)
                for i, (_, m) in enumerate(TOK):
                    dve.wait_ge(*r_kt(l, i + 1))
                    src = ps[0:m, 4 + i, 0:256].rearrange("p (h e) -> p h e", h=NH)
                    dst = ktd[0:m, i, :].rearrange("p (h e) -> p h e", h=NH)
                    TT(dst, src, end(C("kdec", NH, m, NH * i), DK), MUL).then_inc(r_ktd.sem, 1)
                dve.wait_ge(ld_ret.sem, 32 * (l + 1))
                for h in range(NH):
                    if h >= 2:
                        dve.wait_ge(*r_o(l, h - 1))
                    dve.wait_ge(*r_sc(l, h + 1))
                    TT(rpw[:, h % 2, 0:TP + P], ps[:, 4 + h % 2, 0:TP + P], dec[:, h, 0:TP + P], MUL)
                    TT(rpw[0:TS, h % 2, TP + P:PW], ps[0:TS, 4 + h % 2, TP + P:PW], dec[0:TS, h, TP + P:PW], MUL)\
                        .then_inc(r_pw.sem, 1)
                for b in range(SB):
                    if b >= 2:
                        dve.wait_ge(*r_ss(l, b - 1))
                    TSC(rkb[0:TS, b % 2, :], ktd[0:TS, 2, :], C("bmask", 1, TS, b), None, MUL).then_inc(r_kb.sem, 1)
                    if b > 0:
                        retention_update(l, b - 1)
                retention_update(l, SB - 1)

            def retention_update(l, b):
                dve.wait_ge(*r_ss(l, b + 1))
                for i in range(2):
                    last = STT(S0_ret[:, b, i, :], S0_ret[:, b, i, :], C("g4", 1, P, i),
                               ps[:, 5 + b % 2, P * i:P * i + P], MUL, ADD)
                last.then_inc(r_ssa.sem, 1)

            def retention_finish(l):
                for j in range(4):
                    last = STT(ret_o[:, j, :], ret_o[:, j, :], V(l, "ret_gn", j), ret_sq[:, j, :], MUL, MUL)
                link(last)
                dve.wait_ge(*evac(l, through("rg")))
                TT(y_ret[:, :, :], ret_o, y_ret[:, :, :], MUL).then_inc(hn_y.sem, 1)

            def rwkv_prepare(l):
                dve.wait_ge(st_ml.sem, 64 * (l + 1))
                dve.wait_ge(*evac(l, NG))
                dve.tensor_copy(shift_out[:, :, 0:1], z[:, :, TP:TP + 1])
                zq = z[:, :, 1 + TP:].rearrange("p j (b t) -> p j b t", b=SB)
                link(dve.tensor_copy(shift_out[:, :, 1:], zq[:, :, :, ST]))
                dve.sem_inc(so_ok.sem, 1)
                unit_sums(l, "norm", 1)
                link(TT(zs[:, :, 0:TP], z[:, :, 0:TP], z[:, :, 1:1 + TP], SUB))
                unit_sums(l, "shift", 0, 1)
                TT(zs[:, :, TP:T].rearrange("p j (b t) -> p j b t", b=SB), zq[:, :, :, 0:ST], zq[:, :, :, 1:], SUB)
                for j in range(ZT):
                    last = STT(zs[:, j, 0:TP], zs[:, j, 0:TP], V(l, "mu", j), z[:, j, 1:1 + TP], MUL, ADD)
                    if j == ZT // 2:
                        unit_sums(l, "shift", 1, 2)
                link(last)
                for j in range(ZT):
                    d = seq4(zs[:, j, TP:T])
                    last = STT(d, d, V(l, "mu", j), zq[:, j][:, :, 1:], MUL, ADD)
                last.then_inc(w_zs.sem, 1)
                dve.wait_ge(*w_zs(l))
                for j in range(4):
                    last = TSC(rw_kk[:, j, :], zs[:, 4 + j, :], V(l, "kk", j), None, MUL)
                link(last)
                TT(rw_e1, rw_kk, rw_kk, MUL).then_inc(w_sq.sem, 1)
                unit_sums(l, "shift", 2)
                unit_sums(l, "lora")
                dve.wait_ge(*w_lorae(l, 12))
                for j in range(4):
                    last = TSC(rw_e2[:, j, :], rw_a[:, j, :], -1.0, V(l, "ka", j), ADD, MUL)
                link(last)
                link(STT(rw_kp, rw_e2, 1.0, zs[:, 4:8, :], ADD, MUL))
                for j in range(4):
                    last = STT(rw_e2[:, j, :], zs[:, j, :], V(l, "rk", j), rw_kp[:, j, :], MUL, MUL)
                last.then_inc(w_rk.sem, 1)
                unit_sums(l, "square", 0, 1)
                dve.wait_ge(*w_ssq(l, 4))
                link(TSC(rw_e1, rw_e1, 1e-12, None, MAX))
                last = dve.reciprocal(rw_e1, rw_e1)
                unit_sums(l, "square", 1)
                link(last)
                link(TT(rw_kk, rw_kk, rw_e1, MUL))
                dve.wait_ge(st_ret.sem, 32 * (l + 1))
                for j in range(4):
                    dve.wait_ge(*w_bo(l, j + 1))
                    TT(rw_bv[:, j, :], ps[:, 4 + j, 0:T], zs[:, 8 + j, :], MUL)
                unit_sums(l, "bonus", 0, 1)
                link(TSC(rw_lw, rw_lw, -RW_DECAY, None, MUL))
                for j in range(4):
                    last = dve.tensor_tensor_scan(rw_e1[:, j, :], C("reset64", T), rw_lw[:, j, :], 0.0, MUL, ADD)
                link(last)
                TT(rw_e2, rw_e1, rw_lw, SUB).then_inc(w_F.sem, 1)
                dve.wait_ge(*w_F(l))
                dve.wait_ge(*w_zuv(l, 4))
                link(TT(rw_a, rw_a, rw_kk, MUL))
                unit_sums(l, "bonus", 1)
                dve.wait_ge(*w_E(l))

                def blocks(dst, q, x, y):
                    for j in range(NP4):
                        out = dst[:, j, 0:NC - 1, CH * q:CH * q + CH]
                        TT(out, x[:, j, 0:TP].rearrange("p (c s) -> p c s", c=NC - 1),
                           y[:, j, 0:TP].rearrange("p (c s) -> p c s", c=NC - 1), MUL)
                    return TT(dst[:, :, NC - 1, CH * q:CH * q + TS], x[:, :, TP:T], y[:, :, TP:T], MUL)

                blocks(KR, 0, rw_kk, rw_e2)
                blocks(KR, 1, zs[:, 0:4, :], rw_e1)
                blocks(BK, 0, rw_a, rw_lw)
                blocks(BK, 1, rw_kp, rw_lw)
                dve.tensor_copy(PL[:, :, 0:4], rw_e1[:, :, CH - 1:TP:CH])
                link(dve.tensor_copy(PL[:, :, 4:], rw_e1[:, :, TP + ST - 1:T:ST]))
                dve.sem_inc(w_pre.sem, 1)
                unit_sums(l, "pre")

            def rwkv_gram(l):
                for c in range(NC):
                    mask = C("gram_p" if c < NC - 1 else "gram_s", P)
                    for p in range(2):
                        n = 2 * c + p
                        dve.wait_ge(*w_g1(l, n + 1))
                        TT(G[:, c, p, :].rearrange("p (j e) -> p j e", j=4),
                           ps[:, 2 + n % 4, :].rearrange("p (j e) -> p j e", j=4), mid(mask, 4), MUL)\
                            .then_inc(w_g1e.sem, 1)
                unit_sums(l, "gram")
                dve.wait_ge(*w_zab(l, 2))
                for n in range(6):
                    p, c0 = n % 2, 2 * (n // 2)
                    r = slice(CH * p, CH * p + CH)
                    dve.wait_ge(*w_g2(l, n + 1))
                    for c in range(c0, min(c0 + 2, NC)):
                        src = ps[r, 6 + n % 2, 256 * (c - c0):256 * (c - c0) + 256].rearrange("p (j e) -> p j e", j=4)
                        mask = con[r, CON["a_p" if c < NC - 1 else "a_s"]:][:, 0:CH]
                        last = TT(Abd[r, 4 * c:4 * c + 4, CH * p:CH * p + CH], src, mid(mask, 4), MUL)
                    last.then_inc(w_g2e.sem, 1)
                dve.wait_ge(*w_g2e(l, 6))
                for p in range(2):
                    r = slice(CH * p, CH * p + CH)
                    m0_, m0t = con[0:CH, CON["join0"]:][:, 0:CH], con[r, CON["join0t"]:][:, 0:CH]
                    for c in range(NC):
                        TT(Xc[r, 4 * c:4 * c + 4, :],
                           G[0:CH, c, p, :].rearrange("p (j e) -> p j e", j=4)[:, :, 0:CH], mid(m0_, 4), MUL)
                    dg = slice(CH * p, CH * p + CH)
                    link(TT(Xbd[r, :, dg], Abd[r, :, dg], mid(m0t, NU), MUL))
                    if p == 1:
                        unit_sums(l, "first", 0, 1)
                    eye = con[r, CON["ident64"]:][:, 0:CH]
                    TT(Xc[r, :, :], Xc[r, :, :], mid(eye, NU), ADD)
                    last = TT(Xbd[r, :, dg], Xbd[r, :, dg], mid(eye, NU), ADD)
                last.then_inc(w_x0.sem, 1)
                dve.wait_ge(*w_x0(l))
                unit_sums(l, "first", 1)

            def rwkv_invert(l):
                for m in range(len(LEVELS)):
                    for g in range(LEVEL_GROUPS[m]):
                        n = min(8, NU - 8 * g)
                        us = slice(8 * g, 8 * g + n)
                        dve.wait_ge(*w_p(l, join(m, g)))
                        src = ps[:, 5 + g, 0:CH * n].rearrange("p (a b) -> p a b", a=n)
                        link(TT(Yc[:, us, :], src, mid(C("joins", CH, P, CH * m), n), MUL))
                        TT(Xc[:, us, :], Xc[:, us, :], Yc[:, us, :], ADD).then_inc(w_pe.sem, 1)
                    if m < len(LEVELS) - 1:
                        for q in (1, 3):
                            dve.wait_ge(*w_t(l, 4 * m + q + 1))
                            src = ps[0:CH, 2 + q, :].rearrange("p (a b) -> p a b", a=4)
                            dve.tensor_copy(Xbd[0:CH, 4 * q:4 * q + 4, 0:CH], src[:, :, 0:CH])
                            dve.tensor_copy(Xbd[CH:P, 4 * q:4 * q + 4, CH:P], src[:, :, CH:P]).then_inc(w_to.sem, 1)
                unit_sums(l, "tokens")
                dve.wait_ge(*w_pe(l, NJOIN))
                dve.tensor_copy(XT[0:CH, :, CH:P], Xc[CH:P, :, :]).then_inc(w_xt.sem, 1)
                dve.memset(Sbd, 0.0).then_inc(w_sz.sem, 1)
                dve.wait_ge(*w_sz(l))

            def rwkv_chunks(l):
                for c in range(NC):
                    dve.wait_ge(*w_r(l, c + 1))
                    if c == NC - 1:
                        link(TSC(Rn[0:CH, :], ps[0:CH, 2, :], -1.0, None, MUL))
                        dve.wait_ge(*w_ct(l))
                        TT(Rn[0:TS, :], Rn[0:TS, :], ps[0:TS, 7, :], SUB).then_inc(w_rn.sem, 1)
                        dve.wait_ge(*w_ob(l, c + 1))
                        dve.wait_ge(*w_cxe(l))
                        src = ps[:, 5 + c % 2, 0:256].rearrange("p (a b) -> p a b", a=4)[:, :, 0:TS]
                        TT(rw_o[:, :, TP:T], src, CX[:, :, 1, :], ADD).then_inc(w_oe.sem, 1)
                        continue
                    TSC(Rn[0:CH, :], ps[0:CH, 2, :], -1.0, None, MUL).then_inc(w_rn.sem, 1)
                    dve.wait_ge(*w_s(l, c + 1))
                    for p in range(2):
                        r, dg = slice(CH * p, CH * p + CH), slice(CH * p, CH * p + CH)
                        src = ps[r, 4, :].rearrange("p (j e) -> p j e", j=4)[:, :, dg]
                        last = TT(Sbd[r, :, dg], Sbd[r, :, dg], src, ADD)
                    link(last)
                    for p in range(2):
                        r, dg = slice(CH * p, CH * p + CH), slice(CH * p, CH * p + CH)
                        last = TT(Sbd[r, :, dg], Sbd[r, :, dg], end(PL[r, :, c], CH), MUL)
                    last.then_inc(w_su.sem, 1)
                    unit_sums(l, f"chunk{c}")
                for b in range(SB):
                    if b >= 2:
                        dve.wait_ge(*w_st(l, b - 1))
                    TSC(KBm[b % 2], BKt[:, NC - 1, :], C("bmask2", 1, P, b), None, MUL).then_inc(w_kb.sem, 1)
                    if b > 0:
                        rwkv_update(l, b - 1)
                rwkv_update(l, SB - 1)
                unit_sums(l, "samples")

            def rwkv_update(l, b):
                dve.wait_ge(*w_st(l, b + 1))
                src = ps[:, 3 + b % 2, :].rearrange("p (j e) -> p j e", j=4)
                link(TT(S0bd[:, b, :, :], S0bd[:, b, :, :], src, ADD))
                TT(S0bd[:, b, :, :], S0bd[:, b, :, :], end(PL[:, :, 4 + b], P), MUL).then_inc(w_sta.sem, 1)

            def rwkv_finish(l):
                for j in range(4):
                    last = STT(rw_o[:, j, :], rw_o[:, j, :], V(l, "gn_w", j), rw_sq[:, j, :], MUL, MUL)
                link(last)
                for j in range(4):
                    last = STT(rw_o[:, j, :], rw_o[:, j, :], V(l, "gn_b", j), rw_bv[:, j, :], ADD, ADD)
                last.then_inc(hn_y.sem, 1)
                dve.wait_ge(*hn_y(l, 3))
                TT(y_rw[:, :, :], rw_o, rw_g, MUL).then_inc(rw_y.sem, 1)

            def unit_sums(l, place, first=0, end=None):
                for u in units_at(place, PRODUCTS)[first:end]:
                    s, used = turns.take()
                    dve.wait_ge(*u_sig(l, u + 1))
                    dve.wait_ge(slot_fr[s].sem, used + 1)
                    g, m = gate[:, u % 2, :], mixed[:, u % KT, :]
                    TT(m if u < KT else g, ps[:, 1, 0:T], g, MUL).then_inc(u_mul.sem, 1)
                    dve.wait_ge(*u_mul(l, u + 1))
                    if u < KT:
                        dve.sem_inc(u_add.sem, 1)
                    else:
                        TT(m, m, g, ADD).then_inc(u_add.sem, 1)

            def closing(l):
                base = 24 * l + NEARLY_DONE
                with dve.Fori(0, 2) as i:
                    inner = turns.loop(i, 4)
                    for k in range(4):
                        s, used = inner.take()
                        dve.wait_ge(u_sig.sem, i * 4 + (base + k + 1))
                        dve.wait_ge(slot_fr[s].sem, used + 1)
                        TT(gates[:, k, :], ps[:, 4 + k % 2, 0:T], gates[:, k, :], MUL).then_inc(u_mul.sem, 1)
                        dve.wait_ge(u_mul.sem, i * 4 + (base + k + 1))
                        m = mixed[:, bass.ds(i * 4 + k, 1), :].rearrange("p a n -> p (a n)")
                        TT(m, m, gates[:, k, :], ADD).then_inc(u_add.sem, 1)
                turns.after(2, 4)
                for d in range(KT):
                    if d % 2 == 0:
                        s, used = turns.take()
                        dve.wait_ge(*f_out(l, d // 2 + 1))
                    else:
                        dve.wait_ge(slot_fr[s].sem, used + 1)
                    TT(X[:, d, :], X[:, d, :], ps[:, 6 + d % 2, 0:T], ADD).then_inc(x_mix.sem, 1)

            def route():
                dve.memset(posn, 0.0)
                dve.memset(pick_out, 0.0).then_inc(out_ok.sem, 1)
                dve.memset(yg[:, 0:512], 0.0).then_inc(yg_a.sem, 1)
                dve.memset(yg[:, 512:D], 0.0).then_inc(yg_d.sem, 1)
                link(dve.memset(lg, 0.0))
                dve.wait_ge(*rt_lg(0))
                dve.tensor_copy(lg[:, 0:2, :], ps[:, 6, 0:16].rearrange("p (i e) -> p i e", i=2))
                link(dve.tensor_copy(lg[0:TS, 2, :], ps[0:TS, 6, 16:24]))
                for i in range(3):
                    last = dve.max(top[:, i, :], lg[:, i, :])
                link(last)
                v1 = top[:, :, 1:2].broadcast_to([P, 3, NE])
                TT(gt, lg, v1, ALU.is_gt)
                TT(eq, lg, v1, ALU.is_equal)
                link(TT(ex, lg, top[:, :, 0:1].broadcast_to([P, 3, NE]), SUB))
                dve.sem_inc(rt_e.sem, 1)
                for i in range(3):
                    dve.tensor_tensor_scan(cum[:, i, :], eq[:, i, :], eq[:, i, :], 0.0, ADD, ALU.bypass)
                link(dve.reduce_sum(cnt, gt, AX_X))
                link(TSC(cnt, cnt, -1.0, 2.0, MUL, ADD))
                link(TT(cum, cum, end(cnt, NE), ALU.is_le))
                link(TT(eq, eq, cum, MUL))
                link(TT(gt, gt, eq, ADD))
                dve.sem_inc(rt_sel.sem, 1)
                for n in (1, 3, 5):
                    dve.wait_ge(xt_p.sem, n + 1)
                    m = TOK[n // 2][1]
                    dve.tensor_copy(xt[0:m, n // 2, 512:D], ps[0:m, n, :]).then_inc(xt_d.sem, 1)
                dve.wait_ge(rt_ex.sem, 1)
                link(TT(ex, ex, gt, MUL))
                link(dve.reduce_sum(cnt2, ex, AX_X))
                link(dve.reciprocal(cnt2, cnt2))
                TT(ex, ex, end(cnt2, NE), MUL)
                dve.wait_ge(*rt_pos(0))
                STT(posn[:, 0:2, :], ps[:, 7, 0:16].rearrange("p (i e) -> p i e", i=2), 1.0, gt[:, 0:2, :], ADD, MUL)
                STT(posn[0:TS, 2, :], ps[0:TS, 7, 16:24], 1.0, gt[0:TS, 2, :], ADD, MUL)
                counts = ps[0:1, 7, 32:32 + NE].unsqueeze(1).broadcast_to([1, MAXB - 1, NE])
                link(TT(need[0:1, :].rearrange("p (b e) -> p b e", e=NE), counts,
                        PCON("more", slots_n, 1).rearrange("p (b e) -> p b e", e=NE), ALU.is_gt))
                dve.sem_inc(rt_cb.sem, 1)
                pick_tokens(0, 0)
                dve.wait_ge(*rt_ct(0))
                dve.tensor_copy(crow[0:NE, :], ps[0:NE, 6, 0:T])
                dve.tensor_copy(prow[0:NE, :], ps[0:NE, 7, 0:T]).then_inc(rt_cr.sem, 1)
                dve.tensor_copy(draft[0:1, :], PCON("first", PLAN_N, 1))
                link(dve.tensor_tensor_scan(rank[0:1, :], need[0:1, :], need[0:1, :], 0.0, ADD, ALU.bypass))
                TT(draft[0:1, PLAN_N - 1:PLAN_N], draft[0:1, PLAN_N - 1:PLAN_N], rank[0:1, slots_n - 1:slots_n], ADD)
                link(TT(need[0:1, :], rank[0:1, :], need[0:1, :], MUL))

                def table(name):
                    return PCON(name, MAXEXTRA * slots_n, 1).rearrange("p (k s) -> p k s", k=MAXEXTRA)

                link(TT(hits[0:1], mid(need[0:1, :], MAXEXTRA), table("rank"), ALU.is_equal))
                TT(hits2[0:1], hits[0:1], table("block"), MUL)
                link(TT(hits[0:1], hits[0:1], table("expert"), MUL))
                dve.reduce_sum(draft[0:1, NE:NE + MAXEXTRA], hits[0:1], AX_X)
                at_ = NE + MAXEXTRA + 1 + NE
                link(dve.reduce_sum(draft[0:1, at_:at_ + MAXEXTRA], hits2[0:1], AX_X))
                link(dve.tensor_copy(plan[:, :], draft[0:1, :]))
                dve.sem_inc(plan_ok.sem, 1)

            def pick_tokens(e, b):
                for i, (c0, m) in enumerate(TOK):
                    if isinstance(b, int):
                        places = PCON("iota", MB, m, MB * b)
                        scalar = posn[0:m, i, e:e + 1]
                    else:
                        places = pcon[0:m, bass.ds(b * MB + PC["iota"], MB)]
                        scalar = posn[0:m, i, bass.ds(e, 1)]
                    last = TSC(pick_in[0:m, i, :], places, scalar, None, ALU.is_equal)
                last.then_inc(in_ok.sem, 1)

            def gathered(n):
                dve.wait_ge(ga_p.sem, n * 2 + 2)
                dve.tensor_copy(xg[:, 4:8, :], ps[:, 5, :].rearrange("p (k n) -> p k n", k=4)).then_inc(ga_d.sem, 1)

            def scattered(n):
                for d in range(KT):
                    dve.wait_ge(sc_p.sem, n * KT + (d + 1))
                    TT(X[:, d, :], X[:, d, :], ps[:, 4 + d % 2, 0:T], ADD).then_inc(sc_e.sem, 1)

            def experts():
                gathered(0)
                for e in range(NE):
                    dve.wait_ge(rt_bc.sem, 2 * e + 2)
                    dve.tensor_copy(posb[:, e, :], ps[:, 2 + e % 2, 0:T]).then_inc(rt_pbe.sem, 1)
                dve.wait_ge(rt_pbe.sem, NE)
                dve.wait_ge(rt_cbe.sem, NE)
                blocks = NE + MAXEXTRA + 1
                npass = dve.value_load(plan[0:1, PLAN_N - 1:PLAN_N], min_val=NE, max_val=NE + MAXEXTRA)
                with dve.Fori(0, npass) as i:
                    inner = turns.loop(i, ETURNS)
                    e = dve.value_load(plan[0:1, bass.ds(i, 1)], min_val=0, max_val=NE - 1)
                    b = dve.value_load(plan[0:1, bass.ds(i + blocks, 1)], min_val=0, max_val=MAXB - 1)
                    e1 = dve.value_load(plan[0:1, bass.ds(i + 1, 1)], min_val=0, max_val=NE - 1)
                    b1 = dve.value_load(plan[0:1, bass.ds(i + (blocks + 1), 1)], min_val=0, max_val=MAXB - 1)
                    for f in range(FT):
                        if f == 3:
                            scattered(i)
                            STT(pick_out, posb[:, bass.ds(e, 1), :].rearrange("p a n -> p (a n)"),
                                pcon[:, bass.ds(b + PC["iotac"], 1)],
                                comb[:, bass.ds(e, 1), :].rearrange("p a n -> p (a n)"), ALU.is_equal, MUL)\
                                .then_inc(out_ok.sem, 1)
                            pick_tokens(e1, b1)
                        s, used = inner.take()
                        dve.wait_ge(s_done.sem, i * FT + (FT * NDENSE + f + 1))
                        dve.wait_ge(slot_fr[s].sem, used + 1)
                        TT(ehid[:, f, :], ps[:, 2 * (f % 2) + 1, 0:MB], esil[:, f % 3, :], MUL).then_inc(h_done.sem, 1)
                    gathered(i + 1)
                    for k in range(DSL):
                        s, used = inner.take()
                    dve.wait_ge(slot_fr[s].sem, used + 1)
                    dve.tensor_copy(yg[:, 512:D], ps[:, 7, :]).then_inc(yg_d.sem, 1)
                scattered(npass)

            def feed_forward():
                with dve.Fori(0, NDENSE) as e:
                    inner = turns.loop(e, FT + KT)
                    for f in range(FT):
                        s, used = inner.take()
                        dve.wait_ge(s_done.sem, e * FT + (f + 1))
                        dve.wait_ge(slot_fr[s].sem, used + 1)
                        TT(hid[:, f, :], ps[:, 2 * (f % 3) + 1, 0:T], sil[:, f % 3, :], MUL).then_inc(h_done.sem, 1)
                    for d in range(KT):
                        s, used = inner.take()
                        dve.wait_ge(slot_fr[s].sem, used + 1)
                        TT(X[:, d, :], X[:, d, :], ps[:, 6 + d % 2, 0:T], ADD).then_inc(y_done.sem, 1)
                turns.after(NDENSE, FT + KT, 1)

            for k in range(3):
                dve.sem_inc(h_done.sem, 1)
            for k in range(2):
                dve.sem_inc(y_done.sem, 1)
            dve.wait_ge(ld_head.sem, 32)
            for l in range(DEPTH):
                turns.pass_over(len(EARLY))
                norm(2 * l)
                histories(l)
                conv(l)
                mlstm_gates(l)
                mlstm_keys(l)
                for h in range(NH):
                    mlstm_head(l, h)
                mlstm_state(l)
                head_norm(3 * l, ml_o, ml_sq, lambda: mlstm_finish(l))
                dve.wait_ge(*hn_y(l, 1))
                retention(l)
                head_norm(3 * l + 1, ret_o, ret_sq, lambda: retention_finish(l))
                dve.wait_ge(*hn_y(l, 2))
                rwkv_prepare(l)
                rwkv_gram(l)
                rwkv_invert(l)
                rwkv_chunks(l)
                head_norm(3 * l + 2, rw_o, rw_sq, lambda: rwkv_finish(l))
                closing(l)
                norm(2 * l + 1)
                if l == 0:
                    feed_forward()
                else:
                    route()
                    experts()
            norm(2 * DEPTH)

        @block.gpsimd
        def _(pool):
            for l in range(DEPTH):
                if l > 0:
                    pool.wait_ge(y_done.sem, CREDIT_Y + KT * NDENSE)
                    pool.wait_ge(*w_zs(l - 1))
                pool.dma_start(hist[:, :], a["hist"][l]).then_inc(ld_hist.sem, 16)
                pool.dma_start(prev[:, :], a["prev"][l]).then_inc(ld_hist.sem, 16)
                pool.dma_start(C0, a["C"][l]).then_inc(ld_c0.sem, 16)
                pool.dma_start(n0, a["n"][l]).then_inc(ld_n0.sem, 16)
                pool.wait_ge(*co_ok(l))
                pool.dma_start(o["conv"][l], conv_out[:, :, :]).then_inc(st_small.sem, 16)
                pool.wait_ge(*ml_out(l))
                pool.wait_ge(*ml_cpe(l))
                pool.dma_start(o["m"][l], m_out[:, :]).then_inc(st_ml.sem, 16)
                pool.dma_start(o["n"][l], n_out[:, :]).then_inc(st_ml.sem, 16)
                pool.dma_start(o["C_p"][l], Cp).then_inc(st_ml.sem, 16)
                pool.dma_start(o["C_s"][l], C0).then_inc(st_ml.sem, 16)
                pool.wait_ge(*hn_y(l, 1))
                pool.dma_start(dec, a["dec"].rearrange("p (h w) -> p h w", h=NH)).then_inc(ld_ret.sem, 16)
                pool.dma_start(S0_ret, a["ret"][l]).then_inc(ld_ret.sem, 16)
                pool.wait_ge(*r_spe(l))
                pool.dma_start(o["ret_p"][l], Sp_ret).then_inc(st_ret.sem, 16)
                pool.wait_ge(*r_ssa(l, 8))
                pool.dma_start(o["ret_s"][l], S0_ret).then_inc(st_ret.sem, 16)
                pool.wait_ge(*hn_y(l, 2))
                pool.wait_ge(st_ml.sem, 64 * (l + 1))
                pool.wait_ge(st_ret.sem, 32 * (l + 1))
                pool.memset(UV[0:CH, :, :], 0.0).then_inc(w_zuv.sem, 1)
                pool.wait_ge(*w_zuv(l, 1))
                pool.memset(UV[CH:P, NC - 1, :], 0.0).then_inc(w_zuv.sem, 1)
                for k, t in enumerate((BK, KR)):
                    pool.wait_ge(*w_zuv(l, 2 + k))
                    v = t[:, :, NC - 1, :].rearrange("p j (q s) -> p j q s", q=2)[:, :, :, TS:]
                    pool.memset(v, 0.0).then_inc(w_zuv.sem, 1)
                pool.wait_ge(*so_ok(l))
                pool.dma_start(o["shift"][l], shift_out[:, :, :]).then_inc(st_small.sem, 16)
                pool.wait_ge(*w_pre(l))
                pool.memset(Abd, 0.0).then_inc(w_zab.sem, 1)
                pool.memset(Xbd, 0.0).then_inc(w_zab.sem, 1)
                pool.wait_ge(*w_su(l, 4))
                pool.dma_start(o["rw_p"][l], Sbd).then_inc(st_rw.sem, 16)
                pool.wait_ge(*w_sta(l, 8))
                pool.dma_start(o["rw_s"][l], S0bd).then_inc(st_rw.sem, 16)
            for s, n in ((st_small, 32), (st_ml, 64), (st_ret, 32), (st_rw, 32)):
                pool.wait_ge(s.sem, n * DEPTH)


def kernel(**inputs):
    import numpy as _np
    import concourse.bacc as _bacc
    from concourse.bass_utils import run_bass_kernel_spmd as _run

    f = {k: _np.asarray(v) for k, v in inputs.items()}
    tiles = lambda v: v.reshape(v.shape[0], -1, P).transpose(0, 2, 1)

    x = _np.concatenate([f["x_prompt"].reshape(TP, D), f["x_sample"].reshape(TS, D)], 0)
    arrays = {"x": x.reshape(T, KT, P).transpose(2, 1, 0)}
    con, dec = shape_constants()
    arrays["con"], arrays["dec"] = con, dec
    vec = [f["norm_mix"], f["norm_ffn"], f["ret_gn"], f["ml_conv_w"].reshape(DEPTH, -1), f["ml_conv_b"], f["ml_gn"],
           f["ml_skip"], f["rw_mu"], f["rw_w0"], f["rw_a0"], f["rw_kk"], f["rw_ka"], f["rw_rk"], f["rw_gn_w"],
           f["rw_gn_b"], _np.stack([f["final_norm"]] * DEPTH)]
    arrays["vec"] = _np.concatenate([tiles(v) for v in vec], 2).transpose(1, 0, 2)
    apart = _np.zeros((DEPTH, IF - 2 * NH), _np.float32)
    arrays["bias"] = _np.concatenate([f["ml_bi"], apart, f["ml_bf"]], 1).T
    arrays["m0"] = f["state_mlstm_m"].transpose(2, 0, 1)
    rows_of = lambda w: w.reshape(w.shape[0], -1, P, w.shape[-1]).transpose(0, 2, 1, 3)
    router = _np.concatenate([_np.zeros((DEPTH - 1, D, NE), _np.float32), f["moe_router"]], 0)
    w_in = rows_of(f["w_in"])
    arrays["lw"] = _np.concatenate([
        _np.concatenate([w_in[..., 2560:2564], _np.zeros((DEPTH, P, KT, IF - 2 * NH), _np.float32), w_in[..., 2564:2568]],
                        3).reshape(DEPTH, P, -1),
        f["ml_wq"].transpose(0, 2, 1, 3).reshape(DEPTH, P, -1), f["ml_wk"].transpose(0, 2, 1, 3).reshape(DEPTH, P, -1),
        _np.concatenate([f["rw_w2"], f["rw_a2"]], 1), f["rw_g2"], rows_of(router).reshape(DEPTH, P, -1)], 2)
    first = {"rq": 0, "rk": 256, "rv": 512, "rg": 1024, "mx": 1536, "mv": 2048, "mo": 2568, "zrw": 3080}
    mix = _np.zeros((DEPTH, NSLAB, P, SLOT), _np.float32)
    w_br = f["w_branch"].reshape(DEPTH, 3, 4, P, D)
    w_out = rows_of(f["w_out"])
    for n, (kind, j) in enumerate(EARLY + UNITS + OUTS):
        if kind == "unit":
            c0 = 4872 + j[0] * D + j[1] * P
            mix[:, n, :, 0:KT * P] = w_in[..., c0:c0 + P].reshape(DEPTH, P, KT * P)
            mix[:, n, :, KT * P:12 * P] = w_br[:, j[0], :, :, P * j[1]:P * j[1] + P].transpose(0, 2, 1, 3)\
                .reshape(DEPTH, P, 4 * P)
        elif kind == "out":
            mix[:, n] = w_out[..., 256 * j:256 * j + 256].reshape(DEPTH, P, SLOT)
        else:
            c0 = first[kind] + 256 * j
            mix[:, n] = w_in[..., c0:c0 + 256].reshape(DEPTH, P, SLOT)
    arrays["mix"] = mix
    half = lambda w, ax: _np.stack(_np.split(w[0], 2, ax))
    cut = lambda w: w.reshape(-1, KT, P, FT, P).transpose(0, 3, 2, 1, 4).reshape(-1, P, KT * P)
    arrays["gu"] = _np.concatenate([cut(half(f["ffn_w_gate"], 1)), cut(half(f["ffn_w_up"], 1))], 2)
    arrays["down"] = half(f["ffn_w_down"], 0).reshape(NDENSE, FT, P, KT, P).transpose(0, 3, 2, 1, 4)\
        .reshape(NDENSE * KT, P, FT * P)
    arrays["egu"] = _np.concatenate([cut(f["moe_w_gate"][0]), cut(f["moe_w_up"][0])], 2)
    down = f["moe_w_down"][0].reshape(NE, FT, P, D)
    ed = _np.zeros((NE, DSL, P, 2, D), _np.float32)
    for k, tiles in enumerate(DOWN):
        ed[:, k, :, 0:len(tiles)] = down[:, tiles].transpose(0, 2, 1, 3)
    arrays["edown"] = ed.reshape(NE * DSL, P, 2 * D)
    arrays["pcon"] = plan_constants()
    arrays["hist"] = f["state_mlstm_conv"].reshape(DEPTH, SB, XPAD, 4, P).transpose(0, 4, 3, 1, 2)\
        .reshape(DEPTH, P, -1)
    arrays["prev"] = f["state_rwkv_shift"].reshape(DEPTH, SB, ZT, P).transpose(0, 3, 2, 1).reshape(DEPTH, P, -1)
    arrays["C"] = f["state_mlstm_C"].transpose(0, 3, 1, 2, 4)
    arrays["n"] = f["state_mlstm_n"].transpose(0, 3, 1, 2).reshape(DEPTH, P, -1)
    arrays["ret"] = f["state_ret"].reshape(DEPTH, SB, 2, 2, DK, P).transpose(0, 3, 4, 1, 2, 5)\
        .reshape(DEPTH, P, SB, 2, P)
    s0 = f["state_rwkv"].reshape(DEPTH, SB, NP4, 2, DK, DK)
    rw = _np.zeros((DEPTH, 2, DK, SB, NP4, 2, DK), _np.float32)
    for p in range(2):
        rw[:, p, :, :, :, p, :] = s0[:, :, :, p].transpose(0, 4, 1, 2, 3)
    arrays["rw"] = rw.reshape(DEPTH, P, SB, NP4, P)
    arrays = {"in_" + k: _np.ascontiguousarray(v) for k, v in arrays.items()}

    nc = _bacc.Bacc("TRN2", target_bir_lowering=False, num_devices=1)
    a = {k[3:]: nc.dram_tensor(k, v.shape, F32, kind="ExternalInput").ap() for k, v in arrays.items()}
    shapes = {"y": (P, KT, T), "conv": (DEPTH, P, 4, 27), "shift": (DEPTH, P, ZT, 9), "m": (DEPTH, NH, 9),
              "n": (DEPTH, P, NH + SB * NH), "C_p": (DEPTH, P, 512), "C_s": (DEPTH, P, SB, NH, P),
              "ret_p": (DEPTH, P, 256), "ret_s": (DEPTH, P, SB, 2, P), "rw_p": (DEPTH, P, NP4, P),
              "rw_s": (DEPTH, P, SB, NP4, P)}
    o = {k: nc.dram_tensor("out_" + k, s, F32, kind="ExternalOutput").ap() for k, s in shapes.items()}
    build(nc, a, o)
    res = _run(nc, [arrays], core_ids=[0]).results[0]
    r = {k: _np.asarray(res["out_" + k]) for k in shapes}

    y = r["y"].transpose(2, 1, 0).reshape(T, D)
    ret_p = r["ret_p"].reshape(DEPTH, 2, DK, 2, P).transpose(0, 3, 1, 2, 4).reshape(DEPTH, 1, NH, DK, P)
    ret_s = r["ret_s"].reshape(DEPTH, 2, DK, SB, 2, P).transpose(0, 3, 4, 1, 2, 5).reshape(DEPTH, SB, NH, DK, P)
    C_p = r["C_p"].reshape(DEPTH, P, NH, P).transpose(0, 2, 1, 3)[:, None]
    C_s = r["C_s"].transpose(0, 2, 3, 1, 4)
    n_p = r["n"][:, :, 0:NH].transpose(0, 2, 1)[:, None]
    n_s = r["n"][:, :, NH:].reshape(DEPTH, P, SB, NH).transpose(0, 2, 3, 1)
    m_p, m_s = r["m"][:, :, 0][:, None], r["m"][:, :, 1:].transpose(0, 2, 1)
    conv_p = r["conv"][..., 0:3].transpose(0, 3, 2, 1).reshape(DEPTH, 1, 3, 512)
    conv_s = r["conv"][..., 3:].reshape(DEPTH, P, 4, SB, 3).transpose(0, 3, 4, 2, 1).reshape(DEPTH, SB, 3, 512)
    shift = r["shift"].transpose(0, 3, 2, 1).reshape(DEPTH, 9, -1)

    def heads(v, n):
        v = v.reshape(DEPTH, 2, DK, n, NP4, 2, DK)
        v = _np.stack([v[:, p, :, :, :, p, :] for p in range(2)], 1)
        return v.transpose(0, 3, 4, 1, 5, 2).reshape(DEPTH, n, 2 * NP4, DK, DK)

    rw_p, rw_s = heads(r["rw_p"], 1), heads(r["rw_s"], SB)
    out = (y[:TP].reshape(1, TP, D), y[TP:].reshape(SB, ST, D), ret_p, C_p, n_p, m_p, conv_p, rw_p, shift[:, 0:1],
           ret_s, C_s, n_s, m_s, conv_s, rw_s, shift[:, 1:])
    return tuple(_np.ascontiguousarray(v) for v in out)
```
